# Optimizing a Trainium2 kernel written in Bass

```python
import math
import jax
import jax.numpy as jnp
from jax import lax
import numpy as np

D_MODEL = 1024
BATCH = 1
SEQ = 256
DEPTH = 1
DEC_BATCH = 8
DEC_SEQ = 8
PAST_LEN = 2048
PAGE_SIZE = 128

SSD_D_INNER = D_MODEL
SSD_HEADDIM = 64
SSD_HEADS = SSD_D_INNER // SSD_HEADDIM
SSD_GROUPS = 2
SSD_STATE = 128
SSD_CONV = 4
SSD_CHUNK = 128
SSD_CONV_DIM = SSD_D_INNER + 2 * SSD_GROUPS * SSD_STATE
S5_WIDTH = D_MODEL
S5_GROUP = 16
S5_GROUPS = S5_WIDTH // S5_GROUP
S5_STATE = 64
IN_PROJ_SPLITS = (
    SSD_D_INNER,
    SSD_D_INNER + SSD_CONV_DIM,
    SSD_D_INNER + SSD_CONV_DIM + SSD_HEADS,
    SSD_D_INNER + SSD_CONV_DIM + SSD_HEADS + S5_WIDTH,
    SSD_D_INNER + SSD_CONV_DIM + SSD_HEADS + S5_WIDTH + D_MODEL,
)
IN_PROJ_DIM = SSD_D_INNER + SSD_CONV_DIM + SSD_HEADS + S5_WIDTH + 2 * D_MODEL
MEM_LEN = 256
MEM_HEADS = 4
MEM_HEAD_DIM = D_MODEL // MEM_HEADS
MOE_GROUPS = 4
MOE_EXPERTS_PER_GROUP = 8
MOE_TOP_K = 2
MOE_D_FF = D_MODEL // 2
NORM_EPS = 1e-6

kernel_name = 'hybrid_ssd_s5_memxattn_hmoe_step'

def rms_norm(x, g):
    xf = x.astype(jnp.float32)
    y = xf * lax.rsqrt(jnp.mean(xf * xf, axis=-1, keepdims=True) + NORM_EPS)
    return (y * g.astype(jnp.float32)).astype(x.dtype)

def causal_depthwise_conv(u, buf, w, b):
    L = u.shape[1]
    up = jnp.concatenate([buf.astype(u.dtype), u], axis=1)
    out = b
    for k in range(SSD_CONV):
        out = out + up[:, k:k + L] * w[k]
    return jax.nn.silu(out), up[:, L:]

def ssd_chunked_scan(xh, dt, a, bm, cm, h0):
    bt, L = xh.shape[0], xh.shape[1]
    q = math.gcd(L, SSD_CHUNK)
    nc = L // q
    r = SSD_HEADS // SSD_GROUPS
    x = xh.astype(jnp.float32).reshape(bt, nc, q, SSD_GROUPS, r, SSD_HEADDIM)
    dt = dt.reshape(bt, nc, q, SSD_GROUPS, r)
    b = bm.astype(jnp.float32).reshape(bt, nc, q, SSD_GROUPS, SSD_STATE)
    c = cm.astype(jnp.float32).reshape(bt, nc, q, SSD_GROUPS, SSD_STATE)
    da_cs = jnp.cumsum(dt * a.reshape(SSD_GROUPS, r), axis=2)
    cs_t = jnp.moveaxis(da_cs, 2, -1)
    causal = jnp.tril(jnp.ones((q, q), dtype=bool))
    decay = jnp.exp(jnp.where(causal, cs_t[..., :, None] - cs_t[..., None, :], -jnp.inf))
    cb = jnp.einsum('bclgn,bcsgn->bcgls', c, b)
    dt_t = jnp.moveaxis(dt, 2, -1)
    m = cb[:, :, :, None] * decay * dt_t[..., None, :]
    y = jnp.einsum('bcgrls,bcsgrp->bclgrp', m, x)
    w_end = jnp.exp(da_cs[:, :, -1:] - da_cs) * dt
    s_chunk = jnp.einsum('bcsgn,bcsgr,bcsgrp->bcgrpn', b, w_end, x)
    chunk_decay = jnp.exp(da_cs[:, :, -1])

    def carry_fn(h, inp):
        s_c, d_c = inp
        return d_c[..., None, None] * h + s_c, h

    h_init = h0.astype(jnp.float32).reshape(bt, SSD_GROUPS, r, SSD_HEADDIM, SSD_STATE)
    h_last, h_in = lax.scan(carry_fn, h_init, (jnp.moveaxis(s_chunk, 1, 0), jnp.moveaxis(chunk_decay, 1, 0)))
    h_in = jnp.moveaxis(h_in, 0, 1)
    y = y + jnp.einsum('bclgn,bcgrpn,bclgr->bclgrp', c, h_in, jnp.exp(da_cs))
    return (y.reshape(bt, L, SSD_HEADS, SSD_HEADDIM),
            h_last.reshape(bt, SSD_HEADS, SSD_HEADDIM, SSD_STATE))

def s5_scan(u, h0_re, h0_im, lam_re, lam_im, log_step, b_re, b_im, c_re, c_im, d):
    bt, L = u.shape[0], u.shape[1]
    lam = lax.complex(lam_re.astype(jnp.float32), lam_im.astype(jnp.float32))
    step = jnp.exp(log_step.astype(jnp.float32))[:, None]
    lam_bar = jnp.exp(lam * step)
    b_bar = ((lam_bar - 1.0) / lam)[..., None] * lax.complex(b_re.astype(jnp.float32), b_im.astype(jnp.float32))
    ug = u.astype(jnp.float32).reshape(bt, L, S5_GROUPS, S5_GROUP)
    bu = jnp.einsum('gnk,blgk->blgn', b_bar, ug.astype(jnp.complex64))
    h0 = lax.complex(h0_re.astype(jnp.float32), h0_im.astype(jnp.float32))
    bu = bu.at[:, 0].add(lam_bar * h0)
    a = jnp.broadcast_to(lam_bar, (1, L) + lam_bar.shape)

    def combine(e1, e2):
        a1, b1 = e1
        a2, b2 = e2
        return a1 * a2, a2 * b1 + b2

    _, states = lax.associative_scan(combine, (a, bu), axis=1)
    c = lax.complex(c_re.astype(jnp.float32), c_im.astype(jnp.float32))
    y = jnp.real(jnp.einsum('gkn,blgn->blgk', c, states)) + d.astype(jnp.float32).reshape(S5_GROUPS, S5_GROUP) * ug
    h_last = states[:, -1]
    return y.reshape(bt, L, S5_WIDTH), jnp.real(h_last), jnp.imag(h_last)

def token_mixer(hn, conv_buf, ssd_h0, s5_re0, s5_im0, w_in, conv_w, conv_b, ssd_dt_bias, ssd_a_log, ssd_d,
                ssd_norm_g, w_ssd_branch, s5_lambda_re, s5_lambda_im, s5_log_step, s5_b_re, s5_b_im,
                s5_c_re, s5_c_im, s5_d, w_glu, b_glu, w_mix_out):
    bt, L = hn.shape[0], hn.shape[1]
    dtype = hn.dtype
    proj = hn @ w_in
    z, xbc, dt_raw, u5, gate_a, gate_b = jnp.split(proj, IN_PROJ_SPLITS, axis=-1)
    xbc_c, new_conv = causal_depthwise_conv(xbc, conv_buf, conv_w, conv_b)
    xs, bm, cm = jnp.split(xbc_c, [SSD_D_INNER, SSD_D_INNER + SSD_GROUPS * SSD_STATE], axis=-1)
    xh = xs.reshape(bt, L, SSD_HEADS, SSD_HEADDIM)
    dt = jax.nn.softplus(dt_raw.astype(jnp.float32) + ssd_dt_bias.astype(jnp.float32))
    a = -jnp.exp(ssd_a_log.astype(jnp.float32))
    y_ssd, new_ssd = ssd_chunked_scan(xh, dt, a, bm.reshape(bt, L, SSD_GROUPS, SSD_STATE),
                                      cm.reshape(bt, L, SSD_GROUPS, SSD_STATE), ssd_h0)
    y_ssd = y_ssd + ssd_d.astype(jnp.float32)[:, None] * xh.astype(jnp.float32)
    y_ssd = rms_norm(y_ssd.reshape(bt, L, SSD_D_INNER) * jax.nn.silu(z.astype(jnp.float32)), ssd_norm_g).astype(dtype)
    branch_a = y_ssd @ w_ssd_branch
    y_s5, new_re, new_im = s5_scan(u5, s5_re0, s5_im0, s5_lambda_re, s5_lambda_im, s5_log_step,
                                   s5_b_re, s5_b_im, s5_c_re, s5_c_im, s5_d)
    glu = y_s5.astype(dtype) @ w_glu + b_glu
    branch_b = glu[..., :D_MODEL] * jax.nn.sigmoid(glu[..., D_MODEL:])
    merged = jax.nn.sigmoid(gate_a) * branch_a + jax.nn.sigmoid(gate_b) * branch_b
    return merged @ w_mix_out, new_conv, new_ssd, new_re, new_im

def memory_kv(mem, g, w_k, w_v):
    bt, m = mem.shape[0], mem.shape[1]
    mn = rms_norm(mem, g)
    k = (mn @ w_k).reshape(bt, m, MEM_HEADS, MEM_HEAD_DIM)
    v = (mn @ w_v).reshape(bt, m, MEM_HEADS, MEM_HEAD_DIM)
    return k, v

def memory_attention(hn, k, v, w_q, w_o):
    bt, L = hn.shape[0], hn.shape[1]
    q = (hn @ w_q).reshape(bt, L, MEM_HEADS, MEM_HEAD_DIM)
    s = jnp.einsum('blhd,bmhd->bhlm', q, k.astype(q.dtype)).astype(jnp.float32) * (MEM_HEAD_DIM ** -0.5)
    p = jax.nn.softmax(s, axis=-1).astype(hn.dtype)
    o = jnp.einsum('bhlm,bmhd->blhd', p, v.astype(hn.dtype))
    return o.reshape(bt, L, D_MODEL) @ w_o

def hier_moe(x, w_rg, b_rg, w_re, b_re, w_gate, w_up, w_down):
    shp = x.shape
    t = x.reshape(-1, D_MODEL)
    g_prob = jax.nn.softmax((t @ w_rg).astype(jnp.float32) + b_rg.astype(jnp.float32), axis=-1)
    g_idx = jnp.argmax(g_prob, axis=-1)
    g_w = jnp.take_along_axis(g_prob, g_idx[:, None], axis=-1)
    e_logits = ((t @ w_re).astype(jnp.float32) + b_re.astype(jnp.float32)).reshape(-1, MOE_GROUPS, MOE_EXPERTS_PER_GROUP)
    e_logits = jnp.take_along_axis(e_logits, g_idx[:, None, None], axis=1)[:, 0]
    e_prob = jax.nn.softmax(e_logits, axis=-1)
    top_v, top_i = lax.top_k(e_prob, MOE_TOP_K)
    top_v = top_v / jnp.sum(top_v, axis=-1, keepdims=True)
    e_w = jnp.sum(jax.nn.one_hot(top_i, MOE_EXPERTS_PER_GROUP, dtype=jnp.float32) * top_v[..., None], axis=1)
    comb = ((g_w * jax.nn.one_hot(g_idx, MOE_GROUPS, dtype=jnp.float32))[:, :, None] * e_w[:, None, :]).astype(t.dtype)
    out = jnp.zeros_like(t)
    for g in range(MOE_GROUPS):
        hg = jax.nn.silu(jnp.einsum('td,edf->tef', t, w_gate[g])) * jnp.einsum('td,edf->tef', t, w_up[g])
        out = out + jnp.einsum('tef,efd->td', hg * comb[:, g, :, None], w_down[g])
    return out.reshape(shp)

def decoder_layer(x, mem_k, mem_v, conv_buf, ssd_h0, s5_re0, s5_im0,
                  norm_mix_g, w_in, conv_w, conv_b, ssd_dt_bias, ssd_a_log, ssd_d, ssd_norm_g, w_ssd_branch,
                  s5_lambda_re, s5_lambda_im, s5_log_step, s5_b_re, s5_b_im, s5_c_re, s5_c_im, s5_d,
                  w_glu, b_glu, w_mix_out, norm_mem_q_g, w_mem_q, w_mem_o, norm_ffn_g,
                  w_router_group, b_router_group, w_router_expert, b_router_expert,
                  w_exp_gate, w_exp_up, w_exp_down):
    mix, new_conv, new_ssd, new_re, new_im = token_mixer(
        rms_norm(x, norm_mix_g), conv_buf, ssd_h0, s5_re0, s5_im0, w_in, conv_w, conv_b, ssd_dt_bias,
        ssd_a_log, ssd_d, ssd_norm_g, w_ssd_branch, s5_lambda_re, s5_lambda_im, s5_log_step,
        s5_b_re, s5_b_im, s5_c_re, s5_c_im, s5_d, w_glu, b_glu, w_mix_out)
    h = x + mix
    h = h + memory_attention(rms_norm(h, norm_mem_q_g), mem_k, mem_v, w_mem_q, w_mem_o)
    h = h + hier_moe(rms_norm(h, norm_ffn_g), w_router_group, b_router_group, w_router_expert,
                     b_router_expert, w_exp_gate, w_exp_up, w_exp_down)
    return h, new_conv, new_ssd, new_re, new_im

def setup_inputs(seed: int = 0) -> dict:
    key = jax.random.key(seed)
    ks = jax.random.split(key, 48)

    def nrm(i, shape, scale):
        return scale * jax.random.normal(ks[i], shape, jnp.float32)

    def gain(i, shape):
        return 1.0 + 0.05 * jax.random.normal(ks[i], shape, jnp.float32)

    L = DEPTH
    dt0 = jnp.exp(jax.random.uniform(ks[10], (L, SSD_HEADS), jnp.float32, math.log(1e-3), math.log(1e-1)))
    s5_n = jnp.arange(S5_STATE, dtype=jnp.float32)
    mem_shape = (L, DEC_BATCH, MEM_LEN, MEM_HEADS, MEM_HEAD_DIM)
    s5_state_shape = (L, DEC_BATCH, S5_GROUPS, S5_STATE)
    expert_in = (L, MOE_GROUPS, MOE_EXPERTS_PER_GROUP, D_MODEL, MOE_D_FF)
    return {
        'x_prompt': nrm(0, (BATCH, SEQ, D_MODEL), 1.0),
        'x_sample': nrm(1, (DEC_BATCH, DEC_SEQ, D_MODEL), 1.0),
        'state_conv': nrm(2, (L, DEC_BATCH, SSD_CONV - 1, SSD_CONV_DIM), 1.0),
        'state_ssd': nrm(3, (L, DEC_BATCH, SSD_HEADS, SSD_HEADDIM, SSD_STATE), 0.3),
        'state_s5_re': nrm(4, s5_state_shape, 0.5),
        'state_s5_im': nrm(5, s5_state_shape, 0.5),
        'cache_mem_k': nrm(6, mem_shape, 1.0),
        'cache_mem_v': nrm(7, mem_shape, 1.0),
        'mem_prompt': nrm(8, (BATCH, MEM_LEN, D_MODEL), 1.0),
        'norm_mix_g': gain(9, (L, D_MODEL)),
        'w_in': nrm(11, (L, D_MODEL, IN_PROJ_DIM), D_MODEL ** -0.5),
        'conv_w': nrm(12, (L, SSD_CONV, SSD_CONV_DIM), SSD_CONV ** -0.5),
        'conv_b': nrm(13, (L, SSD_CONV_DIM), 0.02),
        'ssd_dt_bias': dt0 + jnp.log(-jnp.expm1(-dt0)),
        'ssd_a_log': jnp.log(jax.random.uniform(ks[14], (L, SSD_HEADS), jnp.float32, 1.0, 16.0)),
        'ssd_d': gain(15, (L, SSD_HEADS)),
        'ssd_norm_g': gain(16, (L, SSD_D_INNER)),
        'w_ssd_branch': nrm(17, (L, SSD_D_INNER, D_MODEL), SSD_D_INNER ** -0.5),
        's5_lambda_re': -0.5 + nrm(18, (L, S5_GROUPS, S5_STATE), 0.01),
        's5_lambda_im': math.pi * s5_n + nrm(19, (L, S5_GROUPS, S5_STATE), 0.01),
        's5_log_step': jax.random.uniform(ks[20], (L, S5_GROUPS), jnp.float32, math.log(1e-3), math.log(1e-1)),
        's5_b_re': nrm(21, (L, S5_GROUPS, S5_STATE, S5_GROUP), (2 * S5_GROUP) ** -0.5),
        's5_b_im': nrm(22, (L, S5_GROUPS, S5_STATE, S5_GROUP), (2 * S5_GROUP) ** -0.5),
        's5_c_re': nrm(23, (L, S5_GROUPS, S5_GROUP, S5_STATE), (2 * S5_STATE) ** -0.5),
        's5_c_im': nrm(24, (L, S5_GROUPS, S5_GROUP, S5_STATE), (2 * S5_STATE) ** -0.5),
        's5_d': nrm(25, (L, S5_WIDTH), 0.5),
        'w_glu': nrm(26, (L, S5_WIDTH, 2 * D_MODEL), S5_WIDTH ** -0.5),
        'b_glu': nrm(27, (L, 2 * D_MODEL), 0.02),
        'w_mix_out': nrm(28, (L, D_MODEL, D_MODEL), D_MODEL ** -0.5),
        'norm_mem_q_g': gain(29, (L, D_MODEL)),
        'norm_mem_kv_g': gain(30, (L, D_MODEL)),
        'w_mem_q': nrm(31, (L, D_MODEL, D_MODEL), D_MODEL ** -0.5),
        'w_mem_k': nrm(32, (L, D_MODEL, D_MODEL), D_MODEL ** -0.5),
        'w_mem_v': nrm(33, (L, D_MODEL, D_MODEL), D_MODEL ** -0.5),
        'w_mem_o': nrm(34, (L, D_MODEL, D_MODEL), D_MODEL ** -0.5),
        'norm_ffn_g': gain(35, (L, D_MODEL)),
        'w_router_group': nrm(36, (L, D_MODEL, MOE_GROUPS), D_MODEL ** -0.5),
        'b_router_group': nrm(37, (L, MOE_GROUPS), 0.01),
        'w_router_expert': nrm(38, (L, D_MODEL, MOE_GROUPS * MOE_EXPERTS_PER_GROUP), D_MODEL ** -0.5),
        'b_router_expert': nrm(39, (L, MOE_GROUPS * MOE_EXPERTS_PER_GROUP), 0.01),
        'w_exp_gate': nrm(40, expert_in, D_MODEL ** -0.5),
        'w_exp_up': nrm(41, expert_in, D_MODEL ** -0.5),
        'w_exp_down': nrm(42, (L, MOE_GROUPS, MOE_EXPERTS_PER_GROUP, MOE_D_FF, D_MODEL), MOE_D_FF ** -0.5),
        'norm_final_g': gain(43, (D_MODEL,)),
    }

def reference(x_prompt, x_sample, state_conv, state_ssd, state_s5_re, state_s5_im, cache_mem_k, cache_mem_v,
              mem_prompt, norm_mix_g, w_in, conv_w, conv_b, ssd_dt_bias, ssd_a_log, ssd_d, ssd_norm_g,
              w_ssd_branch, s5_lambda_re, s5_lambda_im, s5_log_step, s5_b_re, s5_b_im, s5_c_re, s5_c_im,
              s5_d, w_glu, b_glu, w_mix_out, norm_mem_q_g, norm_mem_kv_g, w_mem_q, w_mem_k, w_mem_v,
              w_mem_o, norm_ffn_g, w_router_group, b_router_group, w_router_expert, b_router_expert,
              w_exp_gate, w_exp_up, w_exp_down, norm_final_g):
    bp = x_prompt.shape[0]
    dtype = x_prompt.dtype
    zero_conv = jnp.zeros((bp, SSD_CONV - 1, SSD_CONV_DIM), dtype)
    zero_ssd = jnp.zeros((bp, SSD_HEADS, SSD_HEADDIM, SSD_STATE), dtype)
    zero_s5 = jnp.zeros((bp, S5_GROUPS, S5_STATE), dtype)
    hp, hs = x_prompt, x_sample
    conv_p, ssd_p, re_p, im_p, mk_p_l, mv_p_l = [], [], [], [], [], []
    conv_s, ssd_s, re_s, im_s = [], [], [], []
    for l in range(DEPTH):
        lw = (norm_mix_g[l], w_in[l], conv_w[l], conv_b[l], ssd_dt_bias[l], ssd_a_log[l], ssd_d[l],
              ssd_norm_g[l], w_ssd_branch[l], s5_lambda_re[l], s5_lambda_im[l], s5_log_step[l],
              s5_b_re[l], s5_b_im[l], s5_c_re[l], s5_c_im[l], s5_d[l], w_glu[l], b_glu[l], w_mix_out[l],
              norm_mem_q_g[l], w_mem_q[l], w_mem_o[l], norm_ffn_g[l], w_router_group[l], b_router_group[l],
              w_router_expert[l], b_router_expert[l], w_exp_gate[l], w_exp_up[l], w_exp_down[l])
        mk_p, mv_p = memory_kv(mem_prompt, norm_mem_kv_g[l], w_mem_k[l], w_mem_v[l])
        hp, c1, s1, r1, i1 = decoder_layer(hp, mk_p, mv_p, zero_conv, zero_ssd, zero_s5, zero_s5, *lw)
        hs, c2, s2, r2, i2 = decoder_layer(hs, cache_mem_k[l], cache_mem_v[l], state_conv[l], state_ssd[l],
                                           state_s5_re[l], state_s5_im[l], *lw)
        conv_p.append(c1); ssd_p.append(s1); re_p.append(r1); im_p.append(i1)
        mk_p_l.append(mk_p); mv_p_l.append(mv_p)
        conv_s.append(c2); ssd_s.append(s2); re_s.append(r2); im_s.append(i2)
    y_prompt = rms_norm(hp, norm_final_g)
    y_sample = rms_norm(hs, norm_final_g)
    return (y_prompt, y_sample,
            jnp.stack(conv_p), jnp.stack(ssd_p), jnp.stack(re_p), jnp.stack(im_p),
            jnp.stack(mk_p_l), jnp.stack(mv_p_l),
            jnp.stack(conv_s), jnp.stack(ssd_s), jnp.stack(re_s), jnp.stack(im_s))


_drawn_inputs = setup_inputs


def setup_inputs(seed=0):
    import zlib

    import numpy as np

    out = dict(_drawn_inputs(seed))
    spreads = {}
    factors = {'ssd_d': 3.664,
     's5_lambda_re': 4.457,
     'b_glu': 5.208,
     'norm_mem_q_g': 4.808,
     'b_router_group': 3.852,
     'b_router_expert': 4.497}
    for name, (base, spread) in spreads.items():
        noise = np.random.default_rng([zlib.crc32(name.encode()), seed]).standard_normal(out[name].shape)
        drawn = base * np.exp(spread * noise) if base else spread * noise
        out[name] = jnp.asarray(drawn.astype(out[name].dtype))
    for name, factor in factors.items():
        out[name] = (out[name] * factor).astype(out[name].dtype)
    return out
```

```python
from contextlib import ExitStack

import concourse.bass as bass
from concourse import mybir

F32 = mybir.dt.float32
F32R = mybir.dt.float32r
I32 = mybir.dt.int32
ACT = mybir.ActivationFunctionType
ALU = mybir.AluOpType
AX = mybir.AxisListType

P = 128
D = 1024
KT = D // P
NP, NS = 256, 64
T = NP + NS
NB, LS = 8, 8
ROWS = (128, 128, 64)
NC = 3
CD = 1536
CT = CD // P
HEADS, HD = 16, 64
STATE = 128
S5G, S5K, S5N = 64, 16, 64
NST = S5G * S5N // P
MEM, MH, MD = 256, 4, 256
NG, NE, TOPF = 4, 8, 512
EPS = 1e-6
TWO_PI = 6.283185307179586
PI = 3.1415925
BLK = 512
CH = 2048
RAW = 6
PAIR = 4
CHUNKS = [(x, part, half) for x, part in ((0, 0), (0, 1), (1, 0), (1, 1), (0, 2), (1, 2)) for half in range(2)]
NCH = len(CHUNKS)
GCH = NCH * NE // 2
CD0, LO0 = 8, RAW
RING = 6
STAT_SLOTS = 3
COL = {"z": 0, "xbc": D, "dt": D + CD, "u5": D + CD + HEADS, "ga": D + CD + HEADS + D, "gb": D + CD + HEADS + 2 * D}

V_MIX, V_SSD, V_Q, V_KV, V_FFN, V_D5, V_GLU, V_CW, V_CB = 0, 8, 16, 24, 32, 40, 48, 64, 112

BLOCKS = (
    [(f"u5{i}", "w_in", COL["u5"] + BLK * i) for i in range(2)]
    + [(f"xbc{i}", "w_in", COL["xbc"] + BLK * i) for i in range(3)]
    + [(f"mk{i}", "w_mem_k", BLK * i) for i in range(2)]
    + [(f"mv{i}", "w_mem_v", BLK * i) for i in range(2)]
    + [(f"z{i}", "w_in", COL["z"] + BLK * i) for i in range(2)]
    + [(f"ga{i}", "w_in", COL["ga"] + BLK * i) for i in range(2)]
    + [(f"sb{i}", "w_ssd_branch", BLK * i) for i in range(2)]
    + [(f"gb{i}", "w_in", COL["gb"] + BLK * i) for i in range(2)]
    + [("gv0", "w_glu", 0), ("gg0", "w_glu", D), ("gv1", "w_glu", BLK), ("gg1", "w_glu", D + BLK)]
    + [(f"mx{i}", "w_mix_out", BLK * i) for i in range(2)]
    + [(f"q{i}", "w_mem_q", BLK * i) for i in range(2)]
    + [(f"o{i}", "w_mem_o", BLK * i) for i in range(2)]
)
BIDX = {b[0]: n for n, b in enumerate(BLOCKS)}

FILL = (
    [("xbc", m) for m in range(CT)]
    + [("mk", m) for m in range(KT)]
    + [("mv", 2 * n + c) for n in range(2) for c in range(2)]
)


def plan():
    j = ["par"]
    j += [f"x{c}{h}" for c in range(NC) for h in range(2)]
    j += [f"m{c}{h}" for c in range(2) for h in range(2)]
    j += ["s5h", "cvs"]
    j += [f"u5{m}" for m in range(KT)]
    j += [f"bt{q}" for q in range(4)] + [f"ct{q}" for q in range(4)]
    for st in range(NST):
        j += [f"bu{st}r", f"bu{st}i"]
        if st < len(FILL):
            j.append(f"{FILL[st][0]}{FILL[st][1]}")
    j += [f"ko{m}{h}" for m in range(2) for h in range(2)]
    j += ["s5o0", "s5o1"] + [f"nc{q}" for q in range(3)]
    j += ["dtT", "dt3", "cs", "ecs"] + [f"ecp{q}" for q in range(2)]
    for c in range(NC):
        j += [f"tr{c}0", f"tr{c}1", f"tb{c}", f"cb{c}"]
    j += ["s00", "s01"]
    for q in range(4):
        j += [f"csb{q}{c}" for c in range(NC)]
        for t in (2 * q, 2 * q + 1):
            j += [f"h0{t}a", f"h0{t}b", f"yi{t}", f"yx{t}", f"ns{t}a", f"ns{t}b"]
    j += ["s10", "s11", "hl0", "hl1"]
    j += [f"z{m}" for m in range(KT)] + ["ssy"]
    j += [f"ga{m}" for m in range(KT)] + [f"sb{m}" for m in range(KT)] + [f"gb{m}" for m in range(KT)]
    for h in range(2):
        j += [f"gv{m}" for m in range(4 * h, 4 * h + 4)] + [f"gg{m}" for m in range(4 * h, 4 * h + 4)]
    j += [f"mx{n}{c}" for n in range(2) for c in range(NC)]
    j += [f"hq{c}{h}" for c in range(NC) for h in range(2)]
    j += [f"q{m}" for m in range(KT)]
    for c in range(2):
        for h in range(MH):
            j += [f"sc{c}{h}", f"pt{c}{h}", f"ao{c}{h}"]
    for b in range(NB):
        j += [f"kt{b}{i}" for i in range(4)] + [f"sp{b}", f"ot{b}"]
    j += [f"o{n}{c}" for n in range(2) for c in range(NC)]
    j += [f"ft{c}{h}" for c in range(NC) for h in range(2)]
    j += ["lg", "rk"]
    return j


PLAN = plan()
RB = 6
BANK = {job: (n % RB, n // RB) for n, job in enumerate(PLAN)}
assert len(BANK) == len(PLAN)
LAST = {}
for _n, _k in (("u5", KT), ("xbc", CT), ("mk", KT), ("z", KT), ("ga", KT), ("sb", KT), ("gb", KT), ("q", KT)):
    for _i in range(_k // 4):
        LAST[f"{_n}{_i}"] = f"{_n}{4 * _i + 3}"
for _i in range(2):
    LAST[f"mv{_i}"] = f"mv{2 * _i + 1}"
    LAST[f"gv{_i}"], LAST[f"gg{_i}"] = f"gv{4 * _i + 3}", f"gg{4 * _i + 3}"
    LAST[f"mx{_i}"], LAST[f"o{_i}"] = f"mx{_i}{NC - 1}", f"o{_i}{NC - 1}"

SEMS = (
    "ld_par ld_x ld_mem ld_small ld_s5 ld_st ld_kv0 ld_kv1 ld_h ld_fin "
    "dve act pool consts rows ss var rs0 xn s5w s5c s5par bx cx inj "
    "tab_ready tab_used scan s5rot sl y5_full y5_free convout xc "
    "dtx sp_e dt_ready cs_in wdec etot bblk csd csm mt y_done ysq yr yn glu_used "
    "hn2 nmax pexp sb_full ob_full osb zeroed rt_a rt_e rt_oh npass "
    "fin_y pg gx_full gx_free xhi xlo chunk_done hi lo sil hh t_full hthi htlo y_free sc_full sc_free rgdec fin fy "
    "out_v out_k out_s5 out_cv out_st out_hl out_y0 out_y1 out_y2"
).split()


def layer(nc, a, o):
    ctx = ExitStack()
    with ctx:
        def sb(name, shape, dt=F32):
            return ctx.enter_context(nc.sbuf_tensor(name, shape, dt))

        def sem(name):
            return ctx.enter_context(nc.semaphore(name))

        ring_at = (nc.sbuf_base + 31) // 32 * 32
        ring = sb("ring", [P, RING * 4096])
        work_at = (nc.sbuf_base + 31) // 32 * 32
        work = sb("work", [P, 23400])

        def rounded(name, at, cols):
            return nc.alloc_sbuf_tensor_at(name, [P, cols], F32R, offset=at)

        wsplit = rounded("wsplit", ring_at, PAIR * 2 * CH)
        xsplit = rounded("xsplit", work_at + 4 * 9984, 2 * D)
        hsplit = rounded("hsplit", work_at + 4 * 14080, 4 * TOPF)
        slots = [ring[:, 4096 * i:4096 * (i + 1)] for i in range(RING)]

        def w(at, *dims):
            n = 1
            for d in dims:
                n *= d
            v = work[:, at:at + n]
            return view(v, dims)

        def r(at, *dims):
            n = 1
            for d in dims:
                n *= d
            at += STAT_SLOTS * 4096
            return view(ring[:, at:at + n], dims)

        def view(v, dims):
            names = "abcd"[:len(dims)]
            if len(dims) == 1:
                return v
            kw = {names[i]: dims[i] for i in range(len(dims) - 1)}
            return v.rearrange(f"p ({' '.join(names)}) -> p {' '.join(names)}", **kw)

        ident = sb("ident", [P, P])
        ones = sb("ones", [P, P])
        upto = sb("upto", [P, P])
        before = sb("before", [P, P])
        upto_s = sb("upto_s", [NS, NB, LS])
        same_s = sb("same_s", [NS, NB, LS])
        neg = sb("neg", [P, P])
        neg_s = sb("neg_s", [NS, NB, LS])
        iota = sb("iota", [P, P])
        half2 = sb("half2", [P, 2])
        sel16 = sb("sel16", [P, 4, 2])
        grp2 = sb("grp2", [P, 2])
        start = sb("start", [P, T])
        vec = sb("vec", [P, 124])
        lam = sb("lam", [P, 104])
        hglu = sb("hglu", [P, KT])
        e = sb("e", [P, 8, 2, NST])
        s5p = sb("s5p", [P, 16, NST])
        wdt = sb("wdt", [P, KT, HEADS])
        wr = sb("wr", [P, KT, NG + NG * NE])
        rbias = sb("rbias", [P, NG + NG * NE])
        dtb = sb("dtb", [P, HEADS])
        alog = sb("alog", [P, HEADS])
        cst = sb("cst", [P, CT, 3 * NB])
        last3 = sb("last3", [P, CT, 27])
        ss = sb("ss", [P, 5])
        var = sb("var", [P, 5])
        rs0 = sb("rs0", [P, 5])
        rs1 = sb("rs1", [P, 5])
        rs = sb("rs", [P, 5])
        rg = sb("rg", [P, NC, NG])
        comb = sb("comb", [P, NC, NE])
        np_i = sb("np_i", [P, 1], I32)
        cg = sb("cg", [P, NG * NE])

        psum = [ctx.enter_context(nc.psum_tensor(f"bank{i}", [P, 512], F32)) for i in range(8)]
        s = {n: sem(n) for n in SEMS}
        full = [sem(f"full{i}") for i in range(RB)]
        free = [sem(f"free{i}") for i in range(RB)]
        w_in_sem = [sem(f"w_slot{i}") for i in range(STAT_SLOTS)]
        raw_in = [sem(f"raw_in{i}") for i in range(RAW)]

        def bank(job):
            return psum[BANK[job][0]]

        def got(eng, job):
            b, turn = BANK[job]
            eng.wait_ge(full[b], turn + 1)

        def done(eng, job):
            b, turn = BANK[job]
            eng.wait_ge(free[b], turn + 1)

        def emptied(ins, job):
            ins.then_inc(free[BANK[job][0]], 1)

        block = ctx.enter_context(nc.Block())

        xt = r(0, NC, D)
        hnT = w(0, KT, T)
        u5T = w(2560, KT, T)
        kT = w(5120, KT, MEM)
        vm = w(7168, 2, D)
        xn = [w(5120, D), w(6144, D)]
        st_nat = w(7168, 2, 2, P)
        cv_nat = w(7680, CD)
        memraw = w(9216, 2, D)
        junk = w(11264, D)
        lamrow = w(12288, 3, P)
        vecrow = w(12672, P)
        ddrow = w(12800, P)
        lsrow = w(12928, 2)
        dd8 = w(12930, 2)
        xcT = w(9216, CT, T)
        mnT = w(13056, KT, MEM)
        bnat = w(15104, 2, NST, S5K)
        bx = w(16128, 2, NST, 2, S5K)
        cnat = w(18176, 2, KT, S5N)
        cx = w(19200, 2, KT, 2, S5N)
        tmp512 = w(21248, 512)
        inj = w(22784, 2, NB, NST)
        h0s = w(21760, 2, NB, NST)
        tab = [r(2560 * i, 2, 4, T) for i in range(2)]
        bT = r(5120, KT, 2, P)
        cT = r(7168, KT, 2, P)
        tabtmp = r(9216, 2, 4, P)
        cvin = [r(10240 + 347 * i, 347) for i in range(2)]
        cvout = [r(10934 + 344 * i, 344) for i in range(2)]
        sl = r(11622, 2, 9 * NST)
        ub = [w(15104 + 640 * i, 2, T) for i in range(2)]
        m1 = w(16384, 2, T)
        m2 = w(17024, 2, T)
        wb = [w(17664 + 640 * i, 2, T) for i in range(2)]
        n1 = w(18944, 2, T)
        n2 = w(19584, 2, T)
        sbuf = [w(20224 + 640 * i, 2, T) for i in range(3)]
        rm = [w(22144 + 320 * i, T) for i in range(2)]
        kout = w(13056, 2, D)
        s5out = w(15104, 6, P)
        ncout = w(16128, CD)
        xdt = r(0, NC, D)
        wx = r(3072, NC, D)
        bblk = r(6144, 2, NB, P)
        h0 = r(8192, NB, P)
        h0T = r(9216, NB, P)
        nst = r(10240, NB, P)
        s0T = r(11264, D)
        hl = r(10240, D)
        hlo = r(9216, KT, P)
        y = w(13056, KT, T)
        ecs = w(17664, KT, 192)
        btok = w(19200, NC, 2, P)
        cbT = w(19968, NC, 2, P)
        dm = [w(20736 + 512 * i, 4, P) for i in range(4)]
        ytmp = w(22784, 192)
        dsm = sb("dsm", [P, 12, NC, HEADS])
        dtx, dte, dtl, dtm, dt_, dtA, csk, tot, wend, etot = (dsm[:, i] for i in range(10))
        anegb = dsm[:, 10, 0]
        dtS = w(23000, T)
        zs = [w(20736 + 320 * i, T) for i in range(2)]
        ysq = w(9216, KT, T)
        yv, yr0, yr1, rb = (w(21376 + 320 * i, T) for i in range(4))
        mrg = w(15616, KT, T)
        thB = w(9216, KT, T)
        val = w(11776, 4, T)
        th = [w(18176 + 320 * i, T) for i in range(2)]
        h = w(20300, NC, D)
        hn = w(17920, D)
        hn2T = w(0, KT, T)
        qT = w(2560, KT, T)
        kv = [w(9216, 2, 2, D), view(slots[5], (2, 2, D))]
        kbT = w(13312, KT, MEM)
        aoT = w(15360, KT, T)
        pr = w(18944, MEM)
        pT = w(19200, 2, P)
        oS = w(19456, MEM)
        att = w(19712, 32)
        tn = w(0, NC, D)
        tT = w(11008, KT, T)
        pg = w(3072, NC, NG * P)
        xg = w(4608, NG, KT, P)
        yall = w(3584, NG + 1, D)
        pgT = w(8704, NG, T)
        tT = w(11008, KT, T)
        xhi, xlo = (view(xsplit[:, D * i:D * (i + 1)], (KT, P)) for i in range(2))
        sil = [w(12032 + 512 * i, TOPF) for i in range(2)]
        hh = [w(13056 + 512 * i, TOPF) for i in range(2)]
        hthi, htlo = ([view(hsplit[:, TOPF * (2 * j + i):TOPF * (2 * j + i + 1)], (4, P)) for i in range(2)]
                      for j in range(2))
        raw = [ring[:, PAIR * 2 * CH + CH * i:PAIR * 2 * CH + CH * (i + 1)] for i in range(4)]
        raw += [w(16128 + CH * i, CH) for i in range(2)]
        whi = [wsplit[:, 2 * CH * i:2 * CH * i + CH] for i in range(PAIR)]
        wlo = [wsplit[:, 2 * CH * i + CH:2 * CH * (i + 1)] for i in range(PAIR)]
        rt = w(18176, 24, NC, NE)
        rtl = w(18176 + 576, NC, NG + NG * NE)
        rte = w(18176 + 704, NC, NG * NE)
        gfin = w(0, D)
        fy = [w(1024 + 1024 * i, D) for i in range(2)]

        def wblock(name, c0):
            return a[name][0][:, c0:c0 + BLK].rearrange("(k p) n -> p k n", p=P)

        def blk(name):
            return slots[BIDX[name] % STAT_SLOTS].rearrange("p (k n) -> p k n", k=KT)

        def load_passes(eng):
            eng.wait_ge(s["npass"], 1)
            return eng.value_load(np_i[0:1, 0:1], min_val=1, max_val=NC)

        def squares(act, n0):
            for c in range(NC):
                R = ROWS[c]
                act.activation(hn[0:R], h[0:R, c], ACT.Square, accum_out=ss[0:R, c:c + 1]).then_inc(s["ss"], 1)
                act.wait_ge(s["ss"], n0 + c + 1)

        def keep_last(act, st):
            act.wait_ge(s["s5rot"], st + 1)
            v = sl.rearrange("p r (q s) -> p r q s", q=9)
            act.activation(v[:, :, 0:1, st], sbuf[st % 3][:, :, NP - 1:NP], ACT.Copy)
            act.activation(v[:, :, 1:9, st], sbuf[st % 3][:, :, NP:T].rearrange("p r (b l) -> p r b l", b=NB)[:, :, :, LS - 1],
                           ACT.Copy).then_inc(s["sl"], 1)

        @block.sync
        def _(sp):
            sp.dma_start(xt[:, 0:2, :], a["x_prompt"][0].rearrange("(c p) d -> p c d", p=P)).then_inc(s["ld_x"], 16)
            sp.dma_start(xt[0:NS, 2, :], a["x_sample"].rearrange("b l d -> (b l) d")).then_inc(s["ld_x"], 16)

            def load_block(n):
                name, weight, c0 = BLOCKS[n]
                if n >= STAT_SLOTS:
                    got(sp, LAST[BLOCKS[n - STAT_SLOTS][0]])
                sp.dma_start(slots[n % STAT_SLOTS].rearrange("p (k n) -> p k n", k=KT), wblock(weight, c0)).then_inc(
                    w_in_sem[n % STAT_SLOTS], 16)

            for n in range(2):
                load_block(n)
            sp.dma_start(memraw, a["mem_prompt"][0].rearrange("(c p) d -> p c d", p=P)).then_inc(s["ld_mem"], 16)
            for n in range(2, BIDX["ga0"] + 1):
                load_block(n)
            sp.wait_ge(s["y5_full"], NST)
            done(sp, "s5o1")
            for t in range(KT):
                if t:
                    got(sp, f"h0{t - 1}b")
                    done(sp, f"ns{t - 1}b")
                sp.dma_start(h0, a["state_ssd"][0].rearrange("b (t h) p n -> t (h p) b n", h=2)[t]).then_inc(s["ld_st"], 16)
            for n in range(BIDX["ga1"], len(BLOCKS)):
                load_block(n)
                if BLOCKS[n][0] == "gb1":
                    sp.wait_ge(s["yn"], KT)
                    sp.dma_start(h[:, 0:2, :], a["x_prompt"][0].rearrange("(c p) d -> p c d", p=P)).then_inc(s["ld_h"], 16)
                    sp.dma_start(h[0:NS, 2, :], a["x_sample"].rearrange("b l d -> (b l) d")).then_inc(s["ld_h"], 16)
            sp.wait_ge(s["glu_used"], KT)
            sp.wait_ge(s["out_hl"], 16)
            sp.wait_ge(s["out_st"], 16 * KT)
            for b in range(NB):
                if b >= 2:
                    sp.wait_ge(s["ob_full"], b - 1)
                for i, name in enumerate(("cache_mem_k", "cache_mem_v")):
                    sp.dma_start(kv[b % 2][:, i], a[name][0, b].rearrange("(c p) h d -> p c (h d)", p=P)).then_inc(
                        s[f"ld_kv{b % 2}"], 16)
            for n in range(len(BLOCKS) - STAT_SLOTS, len(BLOCKS)):
                got(sp, LAST[BLOCKS[n][0]])
            sp.wait_ge(s["ob_full"], NB)
            for name, v in (("chunk_done", CD0), ("lo", LO0), ("hh", 2), ("hthi", 1), ("htlo", 1), ("y_free", 1), ("xlo", 1),
                            ("sc_free", 1)):
                sp.sem_inc(s[name], v)
            npass = load_passes(sp)
            with sp.Fori(0, npass) as rr:
                with sp.Fori(0, NG) as g:
                    for two in range(NE // 2):
                        for pos, (x, part, half) in enumerate(CHUNKS):
                            n = (rr * NG + g) * GCH + two * NCH + pos
                            slot, ex = pos % RAW, 2 * two + x
                            sp.wait_ge(s["lo"], n + 1)
                            if part < 2:
                                src = a[("w_exp_gate", "w_exp_up")[part]][0, bass.ds(g, 1), ex, 512 * half:512 * (half + 1)]
                            else:
                                src = a["w_exp_down"][0, bass.ds(g, 1), ex, 256 * half:256 * (half + 1)]
                            sp.dma_start(raw[slot].rearrange("p (k n) -> p k n", k=4 if part < 2 else 2),
                                         src.rearrange("g (k p) f -> p (g k) f", p=P)).then_inc(raw_in[slot], 16)
            sp.wait_ge(s["fin"], 1)
            sp.dma_start(gfin, a["norm_final_g"].rearrange("(a d) -> a d", a=1).to_broadcast([P, D])).then_inc(s["ld_fin"], 16)

        @block.gpsimd
        def _(pool):
            n = [0]

            def q(ins):
                n[0] += 1
                ins.then_inc(s["pool"], 1)
                pool.wait_ge(s["pool"], n[0])

            def keep(v, pattern, base, cm, fill, op=ALU.is_ge):
                q(pool.affine_select(out=v, in_=v, compare_op=op, fill=fill, base=base, pattern=pattern,
                                     channel_multiplier=cm))

            for v, c in ((ident, 0.0), (ones, 1.0), (upto, 1.0), (before, 1.0), (neg, 0.0), (half2, 0.0), (start, 1.0)):
                pool.memset(v[:, :], c)
            for v, c in ((upto_s, 1.0), (same_s, 1.0), (neg_s, 0.0), (sel16, 1.0), (dsm, 0.0), (rg, 0.0)):
                pool.memset(v.rearrange("p a b -> p (a b)") if len(v.shape) == 3 else v[:, :, :, :], c)
            pool.memset(ss[:, :], 1.0)
            q(pool.iota(iota[:, :], pattern=[[1, P]], base=0, channel_multiplier=0, allow_small_or_imprecise_dtypes=True))
            keep(ident[:, :], [[-1, P]], 0, 1, 1.0, ALU.not_equal)
            keep(upto[:, :], [[1, P]], 0, -1, 0.0)
            keep(before[:, :], [[1, P]], -1, -1, 0.0)
            keep(neg[:, :], [[1, P]], 0, -1, -1e30)
            keep(upto_s[:, :, :], [[LS, NB], [1, LS]], 0, -1, 0.0)
            keep(upto_s[:, :, :], [[-LS, NB], [0, LS]], 0, 1, 0.0)
            keep(neg_s[:, :, :], [[LS, NB], [1, LS]], 0, -1, -1e30)
            keep(neg_s[:, :, :], [[-LS, NB], [0, LS]], 0, 1, -1e30)
            keep(same_s[:, :, :], [[-LS, NB], [0, LS]], 0, 1, 0.0)
            keep(same_s[:, :, :], [[LS, NB], [0, LS]], LS - 1, -1, 0.0)
            keep(sel16[:, :, :], [[-32, 4], [-16, 2]], 0, 1, 0.0)
            keep(sel16[:, :, :], [[32, 4], [16, 2]], 15, -1, 0.0)
            q(pool.memset(half2[0:64, 0:1], 1.0))
            q(pool.memset(half2[64:128, 1:2], 1.0))
            q(pool.memset(start[:, 0:1], 0.0))
            pool.memset(start[:, NP:T].rearrange("p (b l) -> p b l", b=NB)[:, :, 0], 0.0).then_inc(s["consts"], 1)

            pool.wait_ge(s["s5par"], 1)

            def tables(oc):
                tb = tab[oc % 2]
                if oc >= 2:
                    pool.wait_ge(s["s5rot"], 4 * (oc - 1))
                    pool.wait_ge(s["tab_used"], 4 * (oc - 1))
                js = slice(4 * oc, 4 * oc + 4)
                pool.memset(tb[:, 0, :, 0:1], 1.0)
                q(pool.memset(tb[:, 1, :, 0:1], 0.0))
                q(pool.tensor_copy(tb[:, :, :, 1], e[:, 0, :, js]))
                for k in range(1, 8):
                    m = 2 ** k
                    new, old = tb[:, :, :, m:2 * m], tb[:, :, :, 0:m]
                    er = e[:, k, 0, js].unsqueeze(1).unsqueeze(3).to_broadcast([P, 2, 4, m])
                    ei = e[:, k, 1, js].unsqueeze(1).unsqueeze(3).to_broadcast([P, 2, 4, m])
                    pool.tensor_tensor(new, old, er, ALU.mult)
                    q(pool.tensor_tensor(tabtmp[:, :, :, 0:m], old, ei, ALU.mult))
                    pool.tensor_tensor(new[:, 0], new[:, 0], tabtmp[:, 1, :, 0:m], ALU.subtract)
                    q(pool.tensor_tensor(new[:, 1], new[:, 1], tabtmp[:, 0, :, 0:m], ALU.add))
                for ri in range(2):
                    ins = pool.tensor_copy(tb[:, ri, :, NP:T].rearrange("p j (b l) -> p j b l", b=NB),
                                           tb[:, ri, :, 0:LS].unsqueeze(2).to_broadcast([P, 4, NB, LS]))
                ins.then_inc(s["tab_ready"], 1)

            tables(0)
            tables(1)
            for st in range(NST):
                tb, j = tab[st // 4 % 2], st % 4
                cs_ = tb[:, 0:1, j].to_broadcast([P, 2, T])
                sn_ = tb[:, 1:2, j].to_broadcast([P, 2, T])
                pool.wait_ge(s["scan"], 2 * st + 2)
                pool.wait_ge(s["tab_ready"], max(2, st // 4 + 1))
                if st:
                    pool.wait_ge(s["s5rot"], st)
                pool.tensor_tensor(n1, wb[st % 2], cs_, ALU.mult)
                q(pool.tensor_tensor(n2, wb[st % 2], sn_, ALU.mult))
                if st >= 3:
                    pool.wait_ge(s["y5_full"], st - 2)
                    pool.wait_ge(s["sl"], st - 2)
                pool.tensor_tensor(sbuf[st % 3][:, 0], n1[:, 0], n2[:, 1], ALU.subtract)
                pool.tensor_tensor(sbuf[st % 3][:, 1], n1[:, 1], n2[:, 0], ALU.add).then_inc(s["s5rot"], 1)
                if st % 4 == 3 and st // 4 + 2 < NST // 4:
                    tables(st // 4 + 2)

            done(pool, "mv3")
            pool.dma_start(o["mv"][0, 0].rearrange("(c p) a d -> p c (a d)", p=P), vm).then_inc(s["out_v"], 16)
            done(pool, "ko11")
            done(pool, "ko10")
            pool.dma_start(o["mk"][0, 0].rearrange("(c p) a d -> p c (a d)", p=P), kout).then_inc(s["out_k"], 16)
            done(pool, "s5o1")
            done(pool, "s5o0")
            for ri, part in enumerate(("re", "im")):
                pool.dma_start(o[part + "p"].rearrange("l b (s h) n -> (l b s) (h n)", h=2),
                               s5out[0:NST, ri]).then_inc(s["out_s5"], 16)
                for k in range(2):
                    pool.dma_start(o[part + "s"].rearrange("l b (s h) n -> (l b s) (h n)", h=2)[P * k:P * (k + 1)],
                                   s5out[:, 2 + 2 * ri + k]).then_inc(s["out_s5"], 16)
            done(pool, "nc2")
            done(pool, "nc1")
            pool.dma_start(o["cvp"].rearrange("l b t n -> (l b t) n"), ncout[0:3]).then_inc(s["out_cv"], 16)
            pool.dma_start(o["cvs"].rearrange("l b t n -> (l b t) n"), ncout[3:27]).then_inc(s["out_cv"], 16)
            for t in range(KT):
                done(pool, f"ns{t}b")
                pool.dma_start(o["ssds"][0].rearrange("b (t h) p n -> t (h p) b n", h=2)[t], nst).then_inc(s["out_st"], 16)
            done(pool, "hl1")
            pool.dma_start(o["ssdp"][0, 0].rearrange("(t h) p n -> (h p) t n", h=2), hlo).then_inc(s["out_hl"], 16)
            for c in range(NC):
                pool.wait_ge(s["fy"], c + 1)
                if c < 2:
                    pool.dma_start(o["yp"][0, P * c:P * (c + 1)], fy[c % 2]).then_inc(s[f"out_y{c}"], 16)
                else:
                    pool.dma_start(o["ys"].rearrange("b l d -> (b l) d"), fy[c % 2][0:NS]).then_inc(s["out_y2"], 16)
            for name, v in (("out_v", 16), ("out_k", 16), ("out_s5", 96), ("out_cv", 32), ("out_st", 16 * KT),
                            ("out_hl", 16), ("out_y0", 16), ("out_y1", 16), ("out_y2", 16)):
                pool.wait_ge(s[name], v)

        @block.scalar
        def _(act):
            n = [0]

            def q(ins):
                n[0] += 1
                ins.then_inc(s["act"], 1)
                act.wait_ge(s["act"], n[0])

            def rows(dst, src, sem_):
                act.dma_start(dst, src).then_inc(s[sem_], 16)

            for at, name in ((V_MIX, "norm_mix_g"), (V_SSD, "ssd_norm_g"), (V_Q, "norm_mem_q_g"), (V_KV, "norm_mem_kv_g"),
                             (V_FFN, "norm_ffn_g"), (V_D5, "s5_d"), (V_GLU, "b_glu")):
                k = a[name].shape[1] // P
                rows(vecrow[at:at + k], a[name][0].rearrange("(k p) -> k p", p=P), "ld_par")
            rows(vecrow[V_CW:V_CB], a["conv_w"][0].rearrange("t (k p) -> (t k) p", p=P), "ld_par")
            rows(vecrow[V_CB:124], a["conv_b"][0].rearrange("(k p) -> k p", p=P), "ld_par")
            rows(lamrow[0:NST, 0], a["s5_lambda_re"][0].rearrange("(s h) n -> s (h n)", h=2), "ld_par")
            rows(lamrow[0:NST, 1], a["s5_lambda_im"][0].rearrange("(s h) n -> s (h n)", h=2), "ld_par")
            rows(lsrow[0:NST], a["s5_log_step"][0].rearrange("(s h) -> s h", h=2), "ld_par")
            rows(dd8[0:KT], a["ssd_d"][0].rearrange("(s h) -> s h", h=2), "ld_par")
            for ri, name in enumerate(("s5_b_re", "s5_b_im")):
                rows(bnat[:, ri], a[name][0].rearrange("(s h) n k -> (h n) s k", h=2), "ld_s5")
            for ri, name in enumerate(("s5_c_re", "s5_c_im")):
                rows(cnat[:, ri], a[name][0].rearrange("(t i) k n -> (i k) t n", i=8), "ld_s5")
            for ri, name in enumerate(("state_s5_re", "state_s5_im")):
                rows(st_nat[:, ri], a[name][0].rearrange("(r b) (s h) n -> (b s) r (h n)", r=2, h=2), "ld_s5")
            rows(cv_nat[0:3 * NB], a["state_conv"][0].rearrange("b t n -> (b t) n"), "ld_s5")
            rows(wdt[:, :, :], a["w_in"][0][:, COL["dt"]:COL["dt"] + HEADS].rearrange("(k p) n -> p k n", p=P), "ld_small")
            rows(wr[:, :, 0:NG], a["w_router_group"][0].rearrange("(k p) n -> p k n", p=P), "ld_small")
            rows(wr[:, :, NG:], a["w_router_expert"][0].rearrange("(k p) n -> p k n", p=P), "ld_small")
            rows(dtb[:, :], a["ssd_dt_bias"].to_broadcast([P, HEADS]), "ld_small")
            rows(alog[:, :], a["ssd_a_log"].to_broadcast([P, HEADS]), "ld_small")
            rows(rbias[:, 0:NG], a["b_router_group"].to_broadcast([P, NG]), "ld_small")
            rows(rbias[:, NG:], a["b_router_expert"].to_broadcast([P, NG * NE]), "ld_small")

            def root(use, k=5):
                act.wait_ge(s["var"], use + 1)
                q(act.activation(rs0[:, 0:k], var[:, 0:k], ACT.Ln))
                act.activation(rs0[:, 0:k], rs0[:, 0:k], ACT.Exp, scale=-0.5).then_inc(s["rs0"], 1)

            act.wait_ge(s["consts"], 1)
            act.wait_ge(s["ld_x"], 32)
            for c in range(NC):
                R = ROWS[c]
                act.activation(junk[0:R], xt[0:R, c], ACT.Square, accum_out=ss[0:R, c:c + 1]).then_inc(s["ss"], 1)
                act.wait_ge(s["ss"], c + 1)
            act.wait_ge(s["ld_mem"], 16)
            for c in range(2):
                act.activation(junk, memraw[:, c], ACT.Square, accum_out=ss[:, 3 + c:4 + c]).then_inc(s["ss"], 1)
                act.wait_ge(s["ss"], 4 + c)
            root(0)
            act.wait_ge(s["s5w"], 1)
            act.activation(s5p[:, 0], lam[:, 2 * NST:3 * NST], ACT.Exp).then_inc(s["s5c"], 1)
            act.wait_ge(s["s5w"], 2)
            act.activation(s5p[:, 3], s5p[:, 1], ACT.Exp).then_inc(s["s5c"], 1)
            act.wait_ge(s["s5w"], 3)
            act.activation(e[:, 0, 1], s5p[:, 6], ACT.Sin)
            act.activation(e[:, 0, 0], s5p[:, 7], ACT.Sin).then_inc(s["s5c"], 1)
            got(act, "s5h")
            emptied(act.activation(h0s.rearrange("p r b s -> p (r b s)"), bank("s5h")[:, 0:512], ACT.Copy), "s5h")
            got(act, "cvs")
            emptied(act.activation(cst[:, :, :].rearrange("p k t -> p (k t)"), bank("cvs")[:, 0:CT * 24], ACT.Copy), "cvs")
            for m in range(KT):
                got(act, f"u5{m}")
                emptied(act.activation(u5T[:, m], bank(f"u5{m}")[:, 0:T], ACT.Copy), f"u5{m}")
            for t_, dst in (("bt", bT), ("ct", cT)):
                for i in range(4):
                    got(act, f"{t_}{i}")
                    emptied(act.activation(dst[:, 2 * i:2 * i + 2].rearrange("p t r n -> p (t r n)"),
                                           bank(f"{t_}{i}")[:, :], ACT.Copy), f"{t_}{i}")

            def fill_evac(kind, m):
                job = f"{kind}{m}"
                got(act, job)
                if kind == "xbc":
                    if m >= 2:
                        act.wait_ge(s["convout"], m - 1)
                    dst = cvin[m % 2]
                    act.activation(dst[:, 3:3 + NP], bank(job)[:, 0:NP], ACT.Copy)
                    emptied(act.activation(dst[:, 259:347].rearrange("p (b l) -> p b l", b=NB)[:, :, 3:11],
                                           bank(job)[:, NP:T].rearrange("p (b l) -> p b l", b=NB), ACT.Copy), job)
                elif kind == "mk":
                    emptied(act.activation(kT[:, m], bank(job)[:, 0:MEM], ACT.Copy), job)
                else:
                    emptied(act.activation(vm[:, m % 2, BLK * (m // 2):BLK * (m // 2 + 1)], bank(job)[:, :], ACT.Copy), job)

            def conv_silu(m):
                act.wait_ge(s["convout"], m + 1)
                v = cvout[m % 2]
                act.activation(xcT[:, m, 0:NP], v[:, 0:NP], ACT.Silu)
                src = v[:, 256:344].rearrange("p (b l) -> p b l", b=NB)[:, :, 3:11]
                act.activation(xcT[:, m, NP:T].rearrange("p (b l) -> p b l", b=NB), src, ACT.Silu).then_inc(s["xc"], 1)

            act.wait_ge(s["inj"], 1)
            for st in range(NST):
                got(act, f"bu{st}r")
                if st >= 2:
                    act.wait_ge(s["scan"], 2 * (st - 1))
                act.activation(rm[st % 2], start[:, :], ACT.Copy, scale=s5p[:, 3, st:st + 1])
                emptied(act.activation(ub[st % 2][:, 0], bank(f"bu{st}r")[:, 0:T], ACT.Copy), f"bu{st}r")
                got(act, f"bu{st}i")
                emptied(act.activation(ub[st % 2][:, 1], bank(f"bu{st}i")[:, 0:T], ACT.Copy), f"bu{st}i")
                if st < len(FILL):
                    fill_evac(*FILL[st])
                if 1 <= st <= CT:
                    conv_silu(st - 1)
                if st >= 2:
                    keep_last(act, st - 2)
            keep_last(act, NST - 2)
            keep_last(act, NST - 1)
            for m in range(2):
                for hf in range(2):
                    job = f"ko{m}{hf}"
                    got(act, job)
                    emptied(act.activation(kout[:, m, 512 * hf:512 * hf + 512], bank(job)[:, :], ACT.Copy), job)
            got(act, "s5o0")
            emptied(act.activation(s5out[0:NST, 0:2].rearrange("p a n -> p (a n)"), bank("s5o0")[0:NST, 0:256], ACT.Copy), "s5o0")
            got(act, "s5o1")
            emptied(act.activation(s5out[:, 2:6].rearrange("p a n -> p (a n)"), bank("s5o1")[:, :], ACT.Copy), "s5o1")
            for i in range(3):
                got(act, f"nc{i}")
                emptied(act.activation(ncout[0:27, 512 * i:512 * i + 512], bank(f"nc{i}")[0:27, :], ACT.Copy), f"nc{i}")

            got(act, "dtT")
            emptied(act.activation(dtS[0:HEADS], bank("dtT")[0:HEADS, 0:T], ACT.Copy), "dtT")
            act.wait_ge(s["ld_small"], 16 * 7)
            act.activation(anegb, alog[:, :], ACT.Exp).then_inc(s["sp_e"], 1)
            act.wait_ge(s["dtx"], 1)
            q(act.activation(dtl, dte, ACT.Exp))
            act.activation(dtl, dtl, ACT.Ln, bias=1.0).then_inc(s["sp_e"], 1)
            got(act, "ecs")
            act.wait_ge(s["cs_in"], 1)
            act.activation(wend, dtl, ACT.Exp).then_inc(s["wdec"], 1)
            act.activation(etot, tot, ACT.Exp).then_inc(s["etot"], 1)
            emptied(act.activation(ecs[:, :, P:192], bank("ecs")[:, :].rearrange("p (t l) -> p t l", t=KT), ACT.Exp), "ecs")
            for i in range(2):
                got(act, f"ecp{i}")
                emptied(act.activation(ecs[:, 4 * i:4 * i + 4, 0:P], bank(f"ecp{i}")[:, :].rearrange("p (t l) -> p t l", t=4),
                                       ACT.Exp), f"ecp{i}")
            for c in range(NC):
                R = ROWS[c]
                got(act, f"tb{c}")
                emptied(act.activation(btok[0:R, c].rearrange("p g n -> p (g n)"), bank(f"tb{c}")[0:R, 0:256], ACT.Copy), f"tb{c}")
                got(act, f"cb{c}")
                emptied(act.activation(cbT[0:R, c, :, 0:R], bank(f"cb{c}")[0:R, 0:2 * P].rearrange(
                    "p (g l) -> p g l", g=2)[:, :, 0:R], ACT.Copy), f"cb{c}")
            for g in range(2):
                got(act, f"s0{g}")
                emptied(act.activation(s0T[:, 512 * g:512 * g + 512], bank(f"s0{g}")[:, :], ACT.Copy), f"s0{g}")
            for i in range(4):
                for c in range(NC):
                    R, k = ROWS[c], (3 * i + c)
                    act.wait_ge(s["csd"], k + 1)
                    d_ = dm[k % 4][0:R, :, 0:R]
                    act.activation(d_, d_, ACT.Exp).then_inc(s["csm"], 1)
                for t in (2 * i, 2 * i + 1):
                    if t:
                        got(act, f"yx{t - 1}")
                    for hf, k in (("a", 0), ("b", 4)):
                        got(act, f"h0{t}{hf}")
                        emptied(act.activation(h0T[:, k:k + 4].rearrange("p b n -> p (b n)"), bank(f"h0{t}{hf}")[:, :],
                                               ACT.Copy), f"h0{t}{hf}")
            got(act, f"yx{KT - 1}")
            for i in range(2):
                got(act, f"hl{i}")
                emptied(act.activation(hlo[:, 4 * i:4 * i + 4].rearrange("p t n -> p (t n)"), bank(f"hl{i}")[:, :],
                                       ACT.Copy), f"hl{i}")
            for m in range(KT):
                got(act, f"z{m}")
                if m >= 2:
                    act.wait_ge(s["y_done"], m - 1)
                emptied(act.activation(zs[m % 2], bank(f"z{m}")[:, 0:T], ACT.Silu), f"z{m}")
            for m in range(KT):
                act.wait_ge(s["y_done"], m + 1)
                act.activation(ysq[:, m], y[:, m], ACT.Square).then_inc(s["ysq"], 1)
            done(act, "ssy")
            q(act.activation(yr0, yv, ACT.Ln))
            act.activation(yr0, yr0, ACT.Exp, scale=-0.5).then_inc(s["yr"], 1)
            act.wait_ge(s["out_cv"], 32)
            act.wait_ge(s["out_s5"], 96)
            for m in range(KT):
                got(act, f"ga{m}")
                emptied(act.activation(mrg[:, m], bank(f"ga{m}")[:, 0:T], ACT.Tanh, scale=0.5), f"ga{m}")
            for m in range(KT):
                got(act, f"gb{m}")
                emptied(act.activation(thB[:, m], bank(f"gb{m}")[:, 0:T], ACT.Tanh, scale=0.5), f"gb{m}")
            for m in range(KT):
                if m % 4 == 0:
                    if m:
                        act.wait_ge(s["glu_used"], m)
                    for k in range(m, m + 4):
                        got(act, f"gv{k}")
                        emptied(act.activation(val[:, k - m], bank(f"gv{k}")[:, 0:T], ACT.Identity,
                                               bias=vec[:, V_GLU + k:V_GLU + k + 1]), f"gv{k}")
                got(act, f"gg{m}")
                if m >= 2:
                    act.wait_ge(s["glu_used"], m - 1)
                emptied(act.activation(th[m % 2], bank(f"gg{m}")[:, 0:T], ACT.Tanh, scale=0.5, bias=hglu[:, m:m + 1]), f"gg{m}")

            done(act, f"mx1{NC - 1}")
            squares(act, 5)
            root(1, 3)
            for m in range(KT):
                got(act, f"q{m}")
                emptied(act.activation(qT[:, m], bank(f"q{m}")[:, 0:T], ACT.Copy, scale=1.0 / 16), f"q{m}")
            for c in range(2):
                for hd in range(MH):
                    k = 4 * c + hd
                    act.wait_ge(s["nmax"], k + 1)
                    if k:
                        got(act, f"pt{(k - 1) // 4}{(k - 1) % 4}")
                    act.activation(pr, bank(f"sc{c}{hd}")[:, 0:MEM], ACT.Exp, bias=att[:, 0:1],
                                   accum_out=att[:, 1:2]).then_inc(s["pexp"], 1)
                    got(act, f"pt{c}{hd}")
                    if k:
                        got(act, f"ao{(k - 1) // 4}{(k - 1) % 4}")
                    emptied(act.activation(pT.rearrange("p m l -> p (m l)"), bank(f"pt{c}{hd}")[:, 0:256], ACT.Copy),
                            f"pt{c}{hd}")
            for b in range(NB):
                for i in range(2):
                    got(act, f"kt{b}{2 * i}")
                    if b and i == 0:
                        act.wait_ge(s["sb_full"], b)
                    emptied(act.activation(kbT[:, 4 * i:4 * i + 2].rearrange("p k m -> p (k m)"), bank(f"kt{b}{2 * i}")[:, :],
                                           ACT.Copy), f"kt{b}{2 * i}")
                act.wait_ge(s["nmax"], 8 + b + 1)
                got(act, f"sp{b - 1}" if b else "pt13")
                act.activation(pr, psum[6][:, 0:MEM], ACT.Exp, bias=att[:, 0:1], accum_out=att[:, 1:2]).then_inc(s["pexp"], 1)
                got(act, f"sp{b}")
                if b:
                    act.wait_ge(s["ob_full"], b)
                else:
                    got(act, "ao13")
                emptied(act.activation(pT.rearrange("p m l -> p (m l)"), bank(f"sp{b}")[:, 0:256], ACT.Copy), f"sp{b}")
            done(act, f"o1{NC - 1}")
            squares(act, 8)
            root(2, 3)

            act.wait_ge(s["rt_a"], 1)
            act.activation(rt[:, 2, :, 0:NG], rt[:, 1, :, 0:NG], ACT.Exp).then_inc(s["rt_e"], 1)
            act.wait_ge(s["rt_a"], 2)
            act.activation(rt[:, 12, :, 0:1], rt[:, 11, :, 0:1], ACT.Exp).then_inc(s["rt_e"], 1)

            npass = load_passes(act)
            with act.Fori(0, npass) as rr:
                for k in range(KT):
                    act.wait_ge(s["gx_full"], rr * 13 + k + 1)
                    act.activation(xg[:, :, k], psum[k % 4][:, :].rearrange("p (g l) -> p g l", g=NG), ACT.Copy,
                                   scale=vec[:, V_FFN + k:V_FFN + k + 1]).then_inc(s["gx_free"], 1)
                for g in range(NG):
                    act.wait_ge(s["gx_full"], rr * 13 + KT + g + 1)
                    act.activation(pgT[:, g], psum[(KT + g) % 4][:, 0:T], ACT.Copy).then_inc(s["gx_free"], 1)
                act.wait_ge(s["gx_full"], rr * 13 + 13)
                act.activation(cg[:, :], psum[0][:, 0:NG * NE], ACT.Copy).then_inc(s["gx_free"], 1)
                with act.Fori(0, NG) as g:
                    base = (rr * NG + g) * GCH
                    act.wait_ge(s["chunk_done"], base - 4 + CD0)
                    act.wait_ge(s["xlo"], rr * NG + g + 1)
                    act.activation(xhi, xg[:, bass.ds(g, 1)].rearrange("p g k l -> p (g k) l"), ACT.Copy).then_inc(s["xhi"], 1)
                    for two in range(NE // 2):
                        b2 = base + two * NCH

                        def silu(x):
                            act.wait_ge(s["chunk_done"], b2 + (2, 6)[x] + CD0)
                            act.activation(sil[x], psum[x][:, :], ACT.Silu).then_inc(s["sil"], 1)

                        def ht(x):
                            act.wait_ge(s["t_full"], (rr * NG + g) * NE + 2 * two + x + 1)
                            act.activation(hthi[x].rearrange("p j n -> p (j n)"), psum[4][:, :], ACT.Copy).then_inc(s["hthi"], 1)

                        for pos in range(NCH):
                            act.wait_ge(raw_in[pos % RAW], ((rr * NG + g) * (GCH // RAW) + two * (NCH // RAW) + pos // RAW + 1) * 16)
                            act.wait_ge(s["chunk_done"], b2 + pos - PAIR + 1 + CD0)
                            act.activation(whi[pos % PAIR], raw[pos % RAW], ACT.Copy).then_inc(s["hi"], 1)
                            if pos == 5:
                                silu(0)
                            if pos == 9:
                                silu(1)
                                ht(0)
                            if pos == 11:
                                ht(1)
            act.wait_ge(s["fin"], 1)
            squares(act, 11)
            root(3, 3)

        @block.tensor
        def _(pe):
            at = [0]

            def take(job):
                assert PLAN[at[0]] == job, (PLAN[at[0]], job)
                at[0] += 1
                b, turn = BANK[job]
                if turn:
                    pe.wait_ge(free[b], turn)
                return psum[b]

            def end(ins, job):
                ins.then_inc(full[BANK[job][0]], 1)

            def tr(out, in_, rows=P):
                return nc.tensor.transpose(out, in_, ident[0:rows, 0:rows])

            def have(block_):
                k = BIDX[block_]
                pe.wait_ge(w_in_sem[k % STAT_SLOTS], 16 * (k // STAT_SLOTS + 1))

            def proj(kind, m, src, N):
                job = f"{kind}{m}"
                b = take(job)
                if m % 4 == 0:
                    have(f"{kind}{m // 4}")
                wv = blk(f"{kind}{m // 4}")
                for k in range(KT):
                    ins = nc.tensor.matmul(b[:, 0:N], wv[:, k, P * (m % 4):P * (m % 4 + 1)], src[:, k, 0:N],
                                           start=(k == 0), stop=(k == KT - 1))
                end(ins, job)

            def proj_tok(job, block_, src, c, R):
                b = take(job)
                wv = blk(block_)
                for k in range(KT):
                    ins = nc.tensor.matmul(b[0:R, :], src[:, k, P * c:P * c + R], wv[:, k, :],
                                           start=(k == 0), stop=(k == KT - 1))
                end(ins, job)

            pe.wait_ge(s["consts"], 1)
            b = take("par")
            pe.wait_ge(s["ld_par"], 16 * 13)
            pe.wait_ge(s["rows"], 1)
            nc.tensor.transpose(b[:, 0:124], vecrow[0:124], ident[0:124, 0:124])
            for i in range(3):
                tr(b[:, 128 + NST * i:128 + NST * (i + 1)], lamrow[0:NST, i], NST)
            end(tr(b[:, 224:232], ddrow[0:KT], KT), "par")
            for i, (kind, c) in enumerate([("x", c) for c in range(NC)] + [("m", c) for c in range(2)]):
                R = ROWS[c] if kind == "x" else P
                pe.wait_ge(s["xn"], i + 1)
                for hf in range(2):
                    b = take(f"{kind}{c}{hf}")
                    for j in range(4):
                        ins = tr(b[:, P * j:P * j + R], xn[i % 2][0:R, P * (4 * hf + j):P * (4 * hf + j + 1)], R)
                    end(ins, f"{kind}{c}{hf}")
            pe.wait_ge(s["ld_s5"], 16 * 7)
            b = take("s5h")
            for ri in range(2):
                for k in range(2):
                    ins = tr(b[:, 256 * ri + P * k:256 * ri + P * (k + 1)], st_nat[:, ri, k])
            end(ins, "s5h")
            b = take("cvs")
            for k in range(CT):
                ins = tr(b[:, 24 * k:24 * k + 24], cv_nat[0:24, P * k:P * (k + 1)], 24)
            end(ins, "cvs")
            done(pe, "x21")
            done(pe, "x20")
            for m in range(KT):
                proj("u5", m, hnT, T)
            for t_, src in (("bt", bx), ("ct", cx)):
                pe.wait_ge(s["bx"] if t_ == "bt" else s["cx"], 1)
                for i in range(4):
                    b = take(f"{t_}{i}")
                    for k in range(2):
                        for ri in range(2):
                            ft = 2 * i + k
                            v = src[:, ri].rearrange("p a b c -> p (a b c)")[:, P * ft:P * (ft + 1)]
                            ins = tr(b[:, P * (2 * k + ri):P * (2 * k + ri + 1)], v)
                    end(ins, f"{t_}{i}")
            for i in range(4):
                done(pe, f"bt{i}")
                done(pe, f"ct{i}")
            done(pe, "u57")
            done(pe, "m11")
            done(pe, "m10")

            def s5_out(st):
                ft, i = st // 4, st % 4
                yb = psum[6 + ft % 2]
                pe.wait_ge(s["s5rot"], st + 1)
                if i == 0 and ft >= 2:
                    pe.wait_ge(s["y5_free"], ft - 1)
                for ri in range(2):
                    ins = nc.tensor.matmul(yb[32 * i:32 * i + 32, 0:T], cT[:, ft, ri, 32 * i:32 * i + 32],
                                           sbuf[st % 3][:, ri], start=(ri == 0), stop=(ri == 1))
                ins.then_inc(s["y5_full"], 1)

            for st in range(NST):
                ft, i = st // 4, st % 4
                for ri, c in enumerate("ri"):
                    b = take(f"bu{st}{c}")
                    end(nc.tensor.matmul(b[:, 0:T], bT[32 * i:32 * i + 32, ft, ri], u5T[32 * i:32 * i + 32, ft],
                                         start=True, stop=True), f"bu{st}{c}")
                if st < len(FILL):
                    kind, m = FILL[st]
                    if kind == "xbc":
                        proj("xbc", m, hnT, T)
                    elif kind == "mk":
                        proj("mk", m, mnT, MEM)
                    else:
                        if m % 2 == 0:
                            have(f"mv{m // 2}")
                        proj_tok(f"mv{m}", f"mv{m // 2}", mnT, m % 2, P)
                if st >= 2:
                    s5_out(st - 2)
            s5_out(NST - 2)
            s5_out(NST - 1)
            done(pe, "mk7")
            for m in range(2):
                for hf in range(2):
                    b = take(f"ko{m}{hf}")
                    for j in range(4):
                        ins = tr(b[:, P * j:P * (j + 1)], kT[:, 4 * hf + j, P * m:P * (m + 1)])
                    end(ins, f"ko{m}{hf}")
            pe.wait_ge(s["sl"], NST)
            b = take("s5o0")
            for ri in range(2):
                ins = tr(b[0:NST, P * ri:P * (ri + 1)], sl[:, ri, 0:NST])
            end(ins, "s5o0")
            b = take("s5o1")
            for ri in range(2):
                for k in range(2):
                    ins = tr(b[:, P * (2 * ri + k):P * (2 * ri + k + 1)], sl[:, ri, NST + P * k:NST + P * (k + 1)])
            end(ins, "s5o1")
            pe.wait_ge(s["convout"], CT)
            for i in range(3):
                b = take(f"nc{i}")
                for j in range(4):
                    ins = tr(b[0:27, P * j:P * (j + 1)], last3[:, 4 * i + j])
                end(ins, f"nc{i}")

            b = take("dtT")
            pe.wait_ge(s["ld_small"], 16 * 7)
            for k in range(KT):
                ins = nc.tensor.matmul(b[0:HEADS, 0:T], wdt[:, k], hnT[:, k], start=(k == 0), stop=(k == KT - 1))
            end(ins, "dtT")
            b = take("dt3")
            done(pe, "dtT")
            for c in range(NC):
                R = ROWS[c]
                ins = tr(b[0:R, HEADS * c:HEADS * (c + 1)], dtS[0:HEADS, P * c:P * c + R], HEADS)
            end(ins, "dt3")
            up = [upto[:, :], upto[:, :], upto_s[:, :, :].rearrange("p b l -> p (b l)")]
            al = [ones[:, :], ones[:, :], same_s[:, :, :].rearrange("p b l -> p (b l)")]
            b = take("cs")
            pe.wait_ge(s["dt_ready"], 1)
            for c in range(NC):
                R = ROWS[c]
                nc.tensor.matmul(b[0:R, HEADS * c:HEADS * (c + 1)], up[c], dtA[0:R, c], start=True, stop=True)
                ins = nc.tensor.matmul(b[0:R, 48 + HEADS * c:48 + HEADS * (c + 1)], al[c], dtA[0:R, c], start=True, stop=True)
            end(ins, "cs")

            def cum_rows(out, c, head, M):
                R = ROWS[c]
                return nc.tensor.matmul(out, dtA[0:R, c, head:head + 1].to_broadcast([R, M]), up[c], start=True, stop=True)

            b = take("ecs")
            for hd in range(HEADS):
                t, q_ = hd // 2, 64 * (hd % 2)
                ins = cum_rows(b[q_:q_ + 64, NS * t:NS * (t + 1)], 2, hd, HD)
            end(ins, "ecs")
            for i in range(2):
                b = take(f"ecp{i}")
                for hd in range(8 * i, 8 * i + 8):
                    t, q_ = hd // 2 - 4 * i, 64 * (hd % 2)
                    ins = cum_rows(b[q_:q_ + 64, P * t:P * (t + 1)], 1, hd, HD)
                end(ins, f"ecp{i}")
            pe.wait_ge(s["xc"], CT)
            for c in range(NC):
                R, c0 = ROWS[c], P * c
                for i in range(2):
                    b = take(f"tr{c}{i}")
                    for j in range(4):
                        ins = tr(b[0:R, P * j:P * (j + 1)], xcT[:, 4 * i + j, c0:c0 + R])
                    end(ins, f"tr{c}{i}")
                b = take(f"tb{c}")
                for g in range(2):
                    ins = tr(b[0:R, P * g:P * (g + 1)], xcT[:, 8 + g, c0:c0 + R])
                end(ins, f"tb{c}")
                b = take(f"cb{c}")
                for g in range(2):
                    ins = nc.tensor.matmul(b[0:R, P * g:P * g + R], xcT[:, 8 + g, c0:c0 + R], xcT[:, 10 + g, c0:c0 + R],
                                           start=True, stop=True)
                end(ins, f"cb{c}")
            done(pe, "tr21")
            done(pe, "tb2")
            for g in range(2):
                b = take(f"s0{g}")
                end(nc.tensor.matmul(b[:, :], btok[:, 0, g], wx[:, 0, 512 * g:512 * g + 512], start=True, stop=True), f"s0{g}")
            for i in range(4):
                g = i // 2
                for c in range(NC):
                    R = ROWS[c]
                    b = take(f"csb{i}{c}")
                    for j in range(4):
                        ins = cum_rows(b[0:R, P * j:P * j + R], c, 4 * i + j, R)
                    end(ins, f"csb{i}{c}")
                for t in (2 * i, 2 * i + 1):
                    pe.wait_ge(s["ld_st"], 16 * (t + 1))
                    for hf, k in (("a", 0), ("b", 4)):
                        b = take(f"h0{t}{hf}")
                        for j in range(4):
                            ins = tr(b[:, P * j:P * (j + 1)], h0[:, k + j])
                        end(ins, f"h0{t}{hf}")
                    b = take(f"yi{t}")
                    pe.wait_ge(s["mt"], 3 * i + 3)
                    for c in range(NC):
                        R, mt = ROWS[c], dm[(3 * i + c) % 4]
                        for q_ in range(2):
                            hd = 2 * t + q_
                            ins = nc.tensor.matmul(b[64 * q_:64 * q_ + 64, P * c:P * c + R], xdt[0:R, c, HD * hd:HD * (hd + 1)],
                                                   mt[0:R, hd % 4, 0:R], start=True, stop=True)
                    end(ins, f"yi{t}")
                    b = take(f"yx{t}")
                    done(pe, "s01")
                    nc.tensor.matmul(b[:, 0:P], s0T[:, P * t:P * (t + 1)], xcT[:, 10 + g, P:2 * P], start=True, stop=True)
                    done(pe, f"h0{t}b")
                    for k in range(NB):
                        ins = nc.tensor.matmul(b[:, P + LS * k:P + LS * (k + 1)], h0T[:, k],
                                               xcT[:, 10 + g, NP + LS * k:NP + LS * (k + 1)], start=True, stop=True)
                    end(ins, f"yx{t}")
                    pe.wait_ge(s["bblk"], 1)
                    for hf, k in (("a", 0), ("b", 4)):
                        b = take(f"ns{t}{hf}")
                        end(nc.tensor.matmul(b[:, :], wx[0:NS, 2, P * t:P * (t + 1)], bblk[0:NS, g, k:k + 4],
                                             start=True, stop=True), f"ns{t}{hf}")
            for g in range(2):
                b = take(f"s1{g}")
                end(nc.tensor.matmul(b[:, :], btok[:, 1, g], wx[:, 1, 512 * g:512 * g + 512], start=True, stop=True), f"s1{g}")
            done(pe, "s11")
            for i in range(2):
                b = take(f"hl{i}")
                for j in range(4):
                    ins = tr(b[:, P * j:P * (j + 1)], hl[:, P * (4 * i + j):P * (4 * i + j + 1)])
                end(ins, f"hl{i}")
            for m in range(KT):
                proj("z", m, hnT, T)
            b = take("ssy")
            pe.wait_ge(s["ysq"], KT)
            for m in range(KT):
                ins = nc.tensor.matmul(b[:, 0:T], ones[:, :], ysq[:, m], start=(m == 0), stop=(m == KT - 1))
            end(ins, "ssy")
            for m in range(KT):
                proj("ga", m, hnT, T)
            pe.wait_ge(s["yn"], KT)
            for m in range(KT):
                proj("sb", m, y, T)
            for m in range(KT):
                proj("gb", m, hnT, T)
            pe.wait_ge(s["y5_free"], KT)
            for i in range(2):
                for kind in ("gv", "gg"):
                    for m in range(4 * i, 4 * i + 4):
                        proj(kind, m, u5T, T)

            pe.wait_ge(s["glu_used"], KT)
            for i in range(2):
                have(f"mx{i}")
                for c in range(NC):
                    proj_tok(f"mx{i}{c}", f"mx{i}", mrg, c, ROWS[c])
            def norm_tr(kind, use):
                for c in range(NC):
                    R = ROWS[c]
                    pe.wait_ge(s["hn2"], 3 * use + c + 1)
                    for hf in range(2):
                        b = take(f"{kind}{c}{hf}")
                        src = hn if kind == "hq" else tn[:, c]
                        for j in range(4):
                            ins = tr(b[:, P * j:P * j + R], src[0:R, P * (4 * hf + j):P * (4 * hf + j + 1)], R)
                        end(ins, f"{kind}{c}{hf}")
                done(pe, f"{kind}20")
                done(pe, f"{kind}21")

            norm_tr("hq", 0)
            for m in range(KT):
                proj("q", m, hn2T, T)
            done(pe, "q7")
            for c in range(2):
                for hd in range(MH):
                    b = take(f"sc{c}{hd}")
                    for k in range(2):
                        ins = nc.tensor.matmul(b[:, 0:MEM], qT[:, 2 * hd + k, P * c:P * (c + 1)], kT[:, 2 * hd + k],
                                               start=(k == 0), stop=(k == 1))
                    end(ins, f"sc{c}{hd}")
                    b = take(f"pt{c}{hd}")
                    done(pe, f"sc{c}{hd}")
                    for k in range(2):
                        ins = tr(b[:, P * k:P * (k + 1)], pr[:, P * k:P * (k + 1)])
                    end(ins, f"pt{c}{hd}")
                    b = take(f"ao{c}{hd}")
                    done(pe, f"pt{c}{hd}")
                    for dt_i in range(2):
                        for k in range(2):
                            ins = nc.tensor.matmul(b[:, P * dt_i:P * (dt_i + 1)],
                                                   vm[:, k, MD * hd + P * dt_i:MD * hd + P * (dt_i + 1)], pT[:, k],
                                                   start=(k == 0), stop=(k == 1))
                    end(ins, f"ao{c}{hd}")
            pe.wait_ge(s["zeroed"], 1)
            for bb in range(NB):
                K, V = kv[bb % 2][:, 0], kv[bb % 2][:, 1]
                pe.wait_ge(s[f"ld_kv{bb % 2}"], 32 * (bb // 2 + 1))
                for i in range(4):
                    b = take(f"kt{bb}{i}")
                    for k in range(2):
                        for m in range(2):
                            ft = 2 * i + k
                            ins = tr(b[:, 256 * k + P * m:256 * k + P * (m + 1)], K[:, m, P * ft:P * (ft + 1)])
                    end(ins, f"kt{bb}{i}")
                for i in range(4):
                    done(pe, f"kt{bb}{i}")
                if bb:
                    pe.wait_ge(s["pexp"], 8 + bb)
                cols = slice(NP + LS * bb, NP + LS * (bb + 1))
                for hd in range(MH):
                    for k in range(2):
                        ins = nc.tensor.matmul(psum[6][32 * hd:32 * hd + LS, 0:MEM], qT[:, 2 * hd + k, cols],
                                               kbT[:, 2 * hd + k], start=(k == 0), stop=(k == 1))
                ins.then_inc(s["sb_full"], 1)
                b = take(f"sp{bb}")
                pe.wait_ge(s["pexp"], 8 + bb + 1)
                for k in range(2):
                    ins = tr(b[:, P * k:P * (k + 1)], pr[:, P * k:P * (k + 1)])
                end(ins, f"sp{bb}")
                done(pe, f"sp{bb}")
                if bb:
                    pe.wait_ge(s["osb"], bb)
                for hd in range(MH):
                    for k in range(2):
                        ins = nc.tensor.matmul(psum[7][32 * hd:32 * hd + LS, 0:MD], pT[:, k, 32 * hd:32 * hd + LS],
                                               V[:, k, MD * hd:MD * (hd + 1)], start=(k == 0), stop=(k == 1))
                ins.then_inc(s["ob_full"], 1)
                b = take(f"ot{bb}")
                pe.wait_ge(s["osb"], bb + 1)
                for k in range(2):
                    ins = tr(b[:, P * k:P * (k + 1)], oS[:, P * k:P * (k + 1)])
                end(ins, f"ot{bb}")
            done(pe, "ot7")
            done(pe, "ao13")
            for i in range(2):
                have(f"o{i}")
                for c in range(NC):
                    proj_tok(f"o{i}{c}", f"o{i}", aoT, c, ROWS[c])
            norm_tr("ft", 1)
            b = take("lg")
            for c in range(NC):
                R = ROWS[c]
                for k in range(KT):
                    ins = nc.tensor.matmul(b[0:R, 36 * c:36 * (c + 1)], tT[:, k, P * c:P * c + R], wr[:, k],
                                           start=(k == 0), stop=(k == KT - 1))
            end(ins, "lg")
            b = take("rk")
            pe.wait_ge(s["rt_oh"], 1)
            oh = rt[:, 4, :, 0:NG]
            for c in range(NC):
                R = ROWS[c]
                for c2 in range(c):
                    nc.tensor.matmul(b[0:R, NG * c:NG * (c + 1)], ones[:, 0:R], oh[:, c2], start=(c2 == 0), stop=False)
                nc.tensor.matmul(b[0:R, NG * c:NG * (c + 1)], before[0:R, 0:R], oh[0:R, c], start=(c == 0), stop=True)
            for c in range(NC):
                ins = nc.tensor.matmul(b[:, 16:16 + NG], ones[0:ROWS[c], :], oh[0:ROWS[c], c], start=(c == 0), stop=(c == NC - 1))
            end(ins, "rk")
            assert at[0] == len(PLAN)

            for i in range(RB):
                last = max(j for j in range(len(PLAN)) if j % RB == i)
                pe.wait_ge(free[i], last // RB + 1)
            npass = load_passes(pe)
            with pe.Fori(0, npass) as rr:
                pe.wait_ge(s["pg"], rr + 1)
                for k in range(KT):
                    if k < 4:
                        pe.wait_ge(s["sc_free"], rr * 6 + 1)
                    else:
                        pe.wait_ge(s["gx_free"], rr * 13 + k - 3)
                    for c in range(NC):
                        R = ROWS[c]
                        ins = nc.tensor.matmul(psum[k % 4][:, :], tn[0:R, c, P * k:P * (k + 1)], pg[0:R, c],
                                               start=(c == 0), stop=(c == NC - 1))
                    ins.then_inc(s["gx_full"], 1)
                for g in range(NG):
                    pe.wait_ge(s["gx_free"], rr * 13 + KT + g - 3)
                    for c in range(NC):
                        R = ROWS[c]
                        ins = tr(psum[(KT + g) % 4][:, P * c:P * c + R], pg[0:R, c, P * g:P * (g + 1)], R)
                    ins.then_inc(s["gx_full"], 1)
                pe.wait_ge(s["gx_free"], rr * 13 + 9)
                for g in range(NG):
                    for c in range(NC):
                        R = ROWS[c]
                        ins = nc.tensor.matmul(psum[0][:, NE * g:NE * (g + 1)], pg[0:R, c, P * g:P * (g + 1)], comb[0:R, c],
                                               start=(c == 0), stop=(c == NC - 1))
                ins.then_inc(s["gx_full"], 1)
                with pe.Fori(0, NG) as g:
                    grp = rr * NG + g
                    base = grp * GCH
                    pe.wait_ge(s["gx_free"], rr * 13 + 13)
                    pe.wait_ge(s["xlo"], grp + 2)
                    for two in range(NE // 2):
                        b2, e2 = base + two * NCH, grp * NE + 2 * two

                        def split_product(bank_, hi_, lo_, wh, wl, start, stop):
                            nc.tensor.matmul(bank_, hi_, wh, start=start, stop=False)
                            nc.tensor.matmul(bank_, hi_, wl, start=False, stop=False)
                            return nc.tensor.matmul(bank_, lo_, wh, start=False, stop=stop)

                        def turn(x):
                            pe.wait_ge(s["hh"], e2 + x + 3)
                            pe.wait_ge(s["hthi"], e2 + x + 1)
                            pe.wait_ge(s["htlo"], e2 + x + 1)
                            for j in range(4):
                                ins = tr(psum[4][:, P * j:P * (j + 1)], hh[x][:, P * j:P * (j + 1)])
                            ins.then_inc(s["t_full"], 1)

                        for pos, (x, part, half) in enumerate(CHUNKS):
                            pe.wait_ge(s["lo"], b2 + pos + 1 + LO0)
                            k_ = 4 if part < 2 else 2
                            wh, wl = (v[pos % PAIR].rearrange("p (k n) -> p k n", k=k_) for v in (whi, wlo))
                            if part < 2:
                                if part == 0 and half == 0:
                                    pe.wait_ge(s["hh"], e2 + x + 1)
                                for k in range(4):
                                    kk = 4 * half + k
                                    ins = split_product(psum[2 * part + x][:, :], xhi[:, kk], xlo[:, kk], wh[:, k], wl[:, k],
                                                        kk == 0, kk == KT - 1)
                            else:
                                if half == 0:
                                    pe.wait_ge(s["htlo"], e2 + x + 2)
                                    if two == 0 and x == 0:
                                        pe.wait_ge(s["y_free"], grp + 2)
                                for j in range(2):
                                    jj = 2 * half + j
                                    for n_ in range(2):
                                        ins = split_product(psum[6 + n_][:, :], hthi[x][:, jj], htlo[x][:, jj],
                                                            wh[:, j, BLK * n_:BLK * (n_ + 1)], wl[:, j, BLK * n_:BLK * (n_ + 1)],
                                                            two == 0 and x == 0 and jj == 0,
                                                            two == NE // 2 - 1 and x == 1 and jj == 3)
                            ins.then_inc(s["chunk_done"], 1)
                            if pos == 5:
                                turn(0)
                            if pos == 8:
                                turn(1)
                pe.wait_ge(s["fin_y"], rr + 1)
                for i in range(2):
                    for c in range(NC):
                        R, k = ROWS[c], 3 * i + c
                        if k >= 2:
                            pe.wait_ge(s["sc_free"], rr * 6 + k)
                        for g in range(NG):
                            ins = nc.tensor.matmul(psum[k % 2][0:R, :], pgT[:, g, P * c:P * c + R],
                                                   yall[:, g + 1, BLK * i:BLK * (i + 1)], start=(g == 0), stop=(g == NG - 1))
                        ins.then_inc(s["sc_full"], 1)
                pe.wait_ge(s["sc_free"], rr * 6 + 7)

        @block.vector
        def _(dve):
            n = [0]

            def q(ins):
                n[0] += 1
                ins.then_inc(s["dve"], 1)
                dve.wait_ge(s["dve"], n[0])

            TT, TS, STT = dve.tensor_tensor, dve.tensor_scalar, dve.scalar_tensor_tensor

            def root(use, k=5):
                TS(var[:, 0:k], ss[:, 0:k], 1.0 / D, EPS, ALU.mult, ALU.add).then_inc(s["var"], 1)
                dve.wait_ge(s["var"], use + 1)
                dve.wait_ge(s["rs0"], use + 1)
                q(TT(rs1[:, 0:k], rs0[:, 0:k], rs0[:, 0:k], ALU.mult))
                q(TT(rs1[:, 0:k], rs1[:, 0:k], var[:, 0:k], ALU.mult))
                q(TS(rs1[:, 0:k], rs1[:, 0:k], -0.5, 1.5, ALU.mult, ALU.add))
                q(TT(rs[:, 0:k], rs0[:, 0:k], rs1[:, 0:k], ALU.mult))

            dve.wait_ge(s["consts"], 1)
            dve.wait_ge(s["ld_par"], 16 * 13)
            q(dve.tensor_reduce(grp2[:, :], sel16[:, :, :].rearrange("p i a -> p a i"), AX.X, ALU.add))
            dve.memset(cvin[0][:, 0:3], 0.0)
            dve.memset(cvin[1][:, 0:3], 0.0)
            dve.tensor_copy(lamrow[0:NST, 2].rearrange("p (h n) -> p h n", h=2), lsrow[0:NST].unsqueeze(2).to_broadcast([NST, 2, 64]))
            dve.tensor_copy(ddrow[0:KT].rearrange("p (h n) -> p h n", h=2),
                            dd8[0:KT].unsqueeze(2).to_broadcast([KT, 2, 64])).then_inc(s["rows"], 1)
            got(dve, "par")
            dve.tensor_copy(vec[:, :], bank("par")[:, 0:124])
            emptied(dve.tensor_copy(lam[:, :], bank("par")[:, 128:232]), "par")
            done(dve, "par")
            TS(hglu[:, :], vec[:, V_GLU + KT:V_GLU + 2 * KT], 0.5, None, ALU.mult).then_inc(s["s5w"], 1)
            dve.wait_ge(s["ss"], 5)
            root(0)
            for i, (kind, c) in enumerate([("x", c) for c in range(NC)] + [("m", c) for c in range(2)]):
                R = ROWS[c] if kind == "x" else P
                src = xt[0:R, c] if kind == "x" else memraw[:, c]
                if i >= 2:
                    j = i - 2
                    got(dve, f"x{j}1")
                TS(xn[i % 2][0:R], src, rs[0:R, i:i + 1], None, ALU.mult).then_inc(s["xn"], 1)
                dst, v0 = (hnT, V_MIX) if kind == "x" else (mnT, V_KV)
                for hf in range(2):
                    job = f"{kind}{c}{hf}"
                    got(dve, job)
                    emptied(TT(dst[:, 4 * hf:4 * hf + 4, P * c:P * c + R],
                               bank(job)[:, :].rearrange("p (k l) -> p k l", k=4)[:, :, 0:R],
                               vec[:, v0 + 4 * hf:v0 + 4 * hf + 4].unsqueeze(2).to_broadcast([P, 4, R]), ALU.mult), job)

            (step, xr, xi, mag, k_, t0, red, redc, lbr, lbi, cr, ci, den, t1, t2, t3) = (s5p[:, i] for i in range(16))
            lr, li = lam[:, 0:NST], lam[:, NST:2 * NST]
            dve.wait_ge(s["s5c"], 1)
            q(TT(xi, li, step, ALU.mult))
            TT(xr, lr, step, ALU.mult).then_inc(s["s5w"], 1)
            magic = 12582912.0
            q(TS(k_, xi, 1.0 / TWO_PI, magic, ALU.mult, ALU.add))
            q(TS(k_, k_, magic, None, ALU.subtract))
            q(STT(out=red, in0=k_, scalar=-6.28125, in1=xi, op0=ALU.mult, op1=ALU.add))
            q(STT(out=red, in0=k_, scalar=-(TWO_PI - 6.28125), in1=red, op0=ALU.mult, op1=ALU.add))
            q(TS(red, red, PI, -PI, ALU.min, ALU.max))
            q(TS(redc, red, TWO_PI / 4, None, ALU.add))
            q(TS(t0, redc, PI, -TWO_PI, ALU.is_gt, ALU.mult))
            q(TT(redc, redc, t0, ALU.add))
            TS(redc, redc, PI, -PI, ALU.min, ALU.max).then_inc(s["s5w"], 1)
            dve.wait_ge(s["s5c"], 3)
            er, ei = e[:, 0, 0], e[:, 0, 1]
            q(TT(lbr, mag, er, ALU.mult))
            q(TT(lbi, mag, ei, ALU.mult))
            for k in range(1, 8):
                q(TT(t1, e[:, k - 1, 0], e[:, k - 1, 0], ALU.mult))
                q(TT(t2, e[:, k - 1, 1], e[:, k - 1, 1], ALU.mult))
                q(TT(e[:, k, 0], t1, t2, ALU.subtract))
                if k < 7:
                    q(STT(out=e[:, k, 1], in0=e[:, k - 1, 0], scalar=2.0, in1=e[:, k - 1, 1], op0=ALU.mult, op1=ALU.mult))
                else:
                    STT(out=e[:, k, 1], in0=e[:, k - 1, 0], scalar=2.0, in1=e[:, k - 1, 1], op0=ALU.mult, op1=ALU.mult)\
                        .then_inc(s["s5par"], 1)
            dve.wait_ge(s["s5par"], 1)
            q(TT(t1, lr, lr, ALU.mult))
            q(TT(t2, li, li, ALU.mult))
            q(TT(den, t1, t2, ALU.add))
            q(dve.reciprocal(den, den))
            q(TS(t0, lbr, 1.0, None, ALU.subtract))
            q(TT(t1, t0, lr, ALU.mult))
            q(TT(t2, lbi, li, ALU.mult))
            q(TT(t1, t1, t2, ALU.add))
            q(TT(cr, t1, den, ALU.mult))
            q(TT(t1, lbi, lr, ALU.mult))
            q(TT(t2, t0, li, ALU.mult))
            q(TT(t1, t1, t2, ALU.subtract))
            q(TT(ci, t1, den, ALU.mult))
            dve.wait_ge(s["ld_s5"], 16 * 7)
            crb, cib = (v.unsqueeze(2).to_broadcast([P, NST, S5K]) for v in (cr, ci))
            tm = view(tmp512, (NST, S5K))
            tm2 = view(junk[:, 0:512], (NST, S5K))
            for ri in range(2):
                q(TT(tm, bnat[:, ri], crb, ALU.mult))
                q(TT(tm2, bnat[:, 1 - ri], cib, ALU.mult))
                q(TT(tm, tm, tm2, ALU.subtract if ri == 0 else ALU.add))
                for h_ in range(2):
                    ins = TS(bx[:, ri, :, h_], tm, half2[:, h_:h_ + 1], None, ALU.mult)
                    if ri == 1 and h_ == 1:
                        ins.then_inc(s["bx"], 1)
                    else:
                        q(ins)
            for ri in range(2):
                for h_ in range(2):
                    ins = TS(cx[:, ri, :, h_], cnat[:, ri], grp2[:, h_:h_ + 1], 1.0 if ri == 0 else -1.0, ALU.mult, ALU.mult)
            ins.then_inc(s["cx"], 1)
            done(dve, "s5h")
            lb = [v.unsqueeze(1).to_broadcast([P, NB, NST]) for v in (lbr, lbi)]
            tj = view(tmp512[:, 0:256], (NB, NST))
            for ri in range(2):
                q(TT(inj[:, ri], h0s[:, ri], lb[0], ALU.mult))
                q(TT(tj, h0s[:, 1 - ri], lb[1], ALU.mult))
                ins = TT(inj[:, ri], inj[:, ri], tj, ALU.subtract if ri == 0 else ALU.add)
                if ri == 0:
                    q(ins)
            ins.then_inc(s["inj"], 1)
            dve.wait_ge(s["inj"], 1)

            def conv(m):
                job = f"xbc{m}"
                done(dve, job)
                vi, vo = cvin[m % 2], cvout[m % 2]
                if m >= 2:
                    dve.wait_ge(s["xc"], m - 1)
                q(dve.tensor_copy(vi[:, 259:347].rearrange("p (b l) -> p b l", b=NB)[:, :, 0:3],
                                  cst[:, m].rearrange("p (b t) -> p b t", b=NB)))
                q(TS(vo, vi[:, 0:344], vec[:, V_CW + m:V_CW + m + 1], vec[:, V_CB + m:V_CB + m + 1], ALU.mult, ALU.add))
                for k in range(1, 4):
                    q(STT(out=vo, in0=vi[:, k:k + 344], scalar=vec[:, V_CW + CT * k + m:V_CW + CT * k + m + 1], in1=vo,
                          op0=ALU.mult, op1=ALU.add))
                dve.tensor_copy(last3[:, m, 0:3], vi[:, 256:259])
                dve.tensor_copy(last3[:, m, 3:27].rearrange("p (b t) -> p b t", b=NB),
                                vi[:, 259:347].rearrange("p (b l) -> p b l", b=NB)[:, :, 8:11]).then_inc(s["convout"], 1)

            def y5_read(ft):
                dve.wait_ge(s["y5_full"], 4 * ft + 4)
                STT(out=u5T[:, ft], in0=u5T[:, ft], scalar=vec[:, V_D5 + ft:V_D5 + ft + 1], in1=psum[6 + ft % 2][:, 0:T],
                    op0=ALU.mult, op1=ALU.add).then_inc(s["y5_free"], 1)

            for st in range(NST):
                tb, j = tab[st // 4 % 2], st % 4
                cs_ = tb[:, 0:1, j].to_broadcast([P, 2, T])
                sn_ = tb[:, 1:2, j].to_broadcast([P, 2, T])
                dve.wait_ge(s["tab_ready"], st // 4 + 1)
                done(dve, f"bu{st}i")
                done(dve, f"bu{st}r")
                if st:
                    dve.wait_ge(s["scan"], 2 * st)
                TT(m1, ub[st % 2], cs_, ALU.mult)
                q(TT(m2, ub[st % 2], sn_, ALU.mult))
                TT(m1[:, 0], m1[:, 0], m2[:, 1], ALU.add).then_inc(s["tab_used"], 1)
                q(TT(m1[:, 1], m1[:, 1], m2[:, 0], ALU.subtract))
                first = m1[:, :, NP:T].rearrange("p r (b l) -> p r b l", b=NB)[:, :, :, 0]
                q(TT(first, first, inj[:, :, :, st], ALU.add))
                if st >= 2:
                    dve.wait_ge(s["s5rot"], st - 1)
                for ri in range(2):
                    ins = dve.tensor_tensor_scan(wb[st % 2][:, ri], rm[st % 2], m1[:, ri], 0.0, ALU.mult, ALU.add)
                    ins.then_inc(s["scan"], 1)
                if 1 <= st <= CT:
                    conv(st - 1)
                if st % 4 == 2 and st > 4:
                    y5_read(st // 4 - 1)
            y5_read(KT - 1)

            got(dve, "dt3")
            dve.wait_ge(s["ld_small"], 16 * 7)
            TT(dtx[:, 0:2], bank("dt3")[:, 0:32].rearrange("p (c n) -> p c n", c=2),
               dtb[:, :].unsqueeze(1).to_broadcast([P, 2, HEADS]), ALU.add)
            emptied(TT(dtx[0:NS, 2], bank("dt3")[0:NS, 32:48], dtb[0:NS, :], ALU.add), "dt3")
            done(dve, "dt3")
            q(TS(dtm, dtx, -1.0, None, ALU.mult))
            TT(dte, dtx, dtm, ALU.min).then_inc(s["dtx"], 1)
            dve.wait_ge(s["dtx"], 1)
            q(TS(dtm, dtx, 0.0, None, ALU.max))
            dve.wait_ge(s["sp_e"], 2)
            q(TT(dt_, dtm, dtl, ALU.add))
            STT(out=dtA, in0=dt_, scalar=-1.0, in1=anegb.unsqueeze(1).to_broadcast([P, NC, HEADS]),
                op0=ALU.mult, op1=ALU.mult).then_inc(s["dt_ready"], 1)
            got(dve, "cs")
            for dst, c0 in ((csk, 0), (tot, 48)):
                dve.tensor_copy(dst[:, 0:2], bank("cs")[:, c0:c0 + 32].rearrange("p (c n) -> p c n", c=2))
                ins = dve.tensor_copy(dst[0:NS, 2], bank("cs")[0:NS, c0 + 32:c0 + 48])
            emptied(ins, "cs")
            done(dve, "cs")
            TT(dtl, tot, csk, ALU.subtract).then_inc(s["cs_in"], 1)
            dve.wait_ge(s["wdec"], 1)
            q(TT(wend, wend, dt_, ALU.mult))
            dve.wait_ge(s["s5rot"], NST)
            dve.wait_ge(s["sl"], NST)
            for c in range(NC):
                R = ROWS[c]
                for i in range(2):
                    job = f"tr{c}{i}"
                    got(dve, job)
                    src = bank(job)[0:R, :].rearrange("p (n d) -> p n d", n=8)
                    cols, hs = slice(512 * i, 512 * i + 512), slice(8 * i, 8 * i + 8)
                    TT(xdt[0:R, c, cols].rearrange("p (n d) -> p n d", n=8), src,
                       dt_[0:R, c, hs].unsqueeze(2).to_broadcast([R, 8, HD]), ALU.mult)
                    emptied(TT(wx[0:R, c, cols].rearrange("p (n d) -> p n d", n=8), src,
                               wend[0:R, c, hs].unsqueeze(2).to_broadcast([R, 8, HD]), ALU.mult), job)
            done(dve, "tb2")
            for g in range(2):
                ins = TT(bblk[0:NS, g], btok[0:NS, 2, g].unsqueeze(1).to_broadcast([NS, NB, P]),
                         same_s[:, :, 0:1].to_broadcast([NS, NB, P]), ALU.mult)
            ins.then_inc(s["bblk"], 1)
            done(dve, "cb2")
            done(dve, "ecp1")
            done(dve, "s01")
            dve.wait_ge(s["out_k"], 16)
            dve.wait_ge(s["out_s5"], 96)
            dve.wait_ge(s["etot"], 1)
            for i in range(4):
                g = i // 2
                for c in range(NC):
                    R, k = ROWS[c], 3 * i + c
                    job, d_ = f"csb{i}{c}", dm[(3 * i + c) % 4][0:R, :, 0:R]
                    got(dve, job)
                    emptied(TT(d_, bank(job)[0:R, :].rearrange("p (n l) -> p n l", n=4)[:, :, 0:R],
                               csk[0:R, c, 4 * i:4 * i + 4].unsqueeze(2).to_broadcast([R, 4, R]), ALU.subtract), job)
                    done(dve, job)
                    mask = neg[:, :] if c < 2 else neg_s[:, :, :].rearrange("p b l -> p (b l)")
                    TT(d_, d_, mask.unsqueeze(1).to_broadcast([R, 4, R]), ALU.add).then_inc(s["csd"], 1)
                for c in range(NC):
                    R, k = ROWS[c], 3 * i + c
                    d_ = dm[k % 4][0:R, :, 0:R]
                    dve.wait_ge(s["csm"], k + 1)
                    TT(d_, d_, cbT[0:R, c, g, 0:R].unsqueeze(1).to_broadcast([R, 4, R]), ALU.mult).then_inc(s["mt"], 1)
                for t in (2 * i, 2 * i + 1):
                    dve.wait_ge(s["ld_st"], 16 * (t + 1))
                    if t:
                        dve.wait_ge(s["out_st"], 16 * t)
                    q(TT(nst, h0, ecs[:, t, P:192].rearrange("p (b l) -> p b l", b=NB)[:, :, LS - 1:LS].to_broadcast([P, NB, P]),
                         ALU.mult))
                    got(dve, f"yi{t}")
                    emptied(STT(out=y[:, t], in0=xcT[:, t], scalar=lam[:, 96 + t:97 + t], in1=bank(f"yi{t}")[:, 0:T],
                                op0=ALU.mult, op1=ALU.add), f"yi{t}")
                    got(dve, f"yx{t}")
                    emptied(TT(ytmp, ecs[:, t], bank(f"yx{t}")[:, 0:192], ALU.mult), f"yx{t}")
                    done(dve, f"yx{t}")
                    q(TT(y[:, t, P:T], y[:, t, P:T], ytmp, ALU.add))
                    for hf, k in (("a", 0), ("b", 4)):
                        job = f"ns{t}{hf}"
                        got(dve, job)
                        emptied(TT(nst[:, k:k + 4], nst[:, k:k + 4], bank(job)[:, :].rearrange("p (b n) -> p b n", b=4),
                                   ALU.add), job)
            dve.wait_ge(s["out_st"], 16 * KT)
            for g in range(2):
                cols = slice(512 * g, 512 * g + 512)
                q(TT(hl[:, cols].rearrange("p (n d) -> p n d", n=8), s0T[:, cols].rearrange("p (n d) -> p n d", n=8),
                     etot[:, 1, 8 * g:8 * g + 8].unsqueeze(2).to_broadcast([P, 8, HD]), ALU.mult))
                got(dve, f"s1{g}")
                emptied(TT(hl[:, cols], hl[:, cols], bank(f"s1{g}")[:, :], ALU.add), f"s1{g}")
            for m in range(KT):
                done(dve, f"z{m}")
                TT(y[:, m], y[:, m], zs[m % 2], ALU.mult).then_inc(s["y_done"], 1)
            got(dve, "ssy")
            emptied(TS(yv, bank("ssy")[:, 0:T], 1.0 / D, EPS, ALU.mult, ALU.add), "ssy")
            dve.wait_ge(s["yr"], 1)
            q(TT(yr1, yr0, yr0, ALU.mult))
            q(TT(yr1, yr1, yv, ALU.mult))
            q(TS(yr1, yr1, -0.5, 1.5, ALU.mult, ALU.add))
            q(TT(rb, yr0, yr1, ALU.mult))
            for m in range(KT):
                STT(out=y[:, m], in0=y[:, m], scalar=vec[:, V_SSD + m:V_SSD + m + 1], in1=rb, op0=ALU.mult, op1=ALU.mult)\
                    .then_inc(s["yn"], 1)
            for m in range(KT):
                got(dve, f"sb{m}")
                done(dve, f"ga{m}")
                emptied(STT(out=mrg[:, m], in0=mrg[:, m], scalar=1.0, in1=bank(f"sb{m}")[:, 0:T], op0=ALU.add, op1=ALU.mult),
                        f"sb{m}")
            done(dve, "sb7")
            for m in range(KT):
                v = val[:, m % 4]
                done(dve, f"gg{m}")
                q(STT(out=v, in0=th[m % 2], scalar=1.0, in1=v, op0=ALU.add, op1=ALU.mult))
                q(STT(out=v, in0=thB[:, m], scalar=1.0, in1=v, op0=ALU.add, op1=ALU.mult))
                STT(out=mrg[:, m], in0=v, scalar=0.5, in1=mrg[:, m], op0=ALU.mult, op1=ALU.add).then_inc(s["glu_used"], 1)
            dve.wait_ge(s["ld_h"], 32)
            for i in range(2):
                for c in range(NC):
                    R, job = ROWS[c], f"mx{i}{c}"
                    got(dve, job)
                    v = h[0:R, c, BLK * i:BLK * (i + 1)]
                    emptied(STT(out=v, in0=bank(job)[0:R, :], scalar=0.5, in1=v, op0=ALU.mult, op1=ALU.add), job)

            def norm(kind, use, gain, dst):
                dve.wait_ge(s["ss"], 5 + 3 * use)
                root(use, 3)
                for c in range(NC):
                    R = ROWS[c]
                    if kind == "hq" and c:
                        got(dve, f"hq{c - 1}1")
                    TS((hn if kind == "hq" else tn[:, c])[0:R], h[0:R, c], rs[0:R, c:c + 1], None, ALU.mult).then_inc(s["hn2"], 1)
                    for hf in range(2):
                        job = f"{kind}{c}{hf}"
                        got(dve, job)
                        emptied(TT(dst[:, 4 * hf:4 * hf + 4, P * c:P * c + R],
                                   bank(job)[:, :].rearrange("p (k l) -> p k l", k=4)[:, :, 0:R],
                                   vec[:, gain + 4 * hf:gain + 4 * hf + 4].unsqueeze(2).to_broadcast([P, 4, R]), ALU.mult), job)

            norm("hq", 1, V_Q, hn2T)

            def minus_max(src):
                q(dve.reduce_max(att[:, 3:4], src, AX.X))
                TS(att[:, 0:1], att[:, 3:4], -1.0, None, ALU.mult).then_inc(s["nmax"], 1)

            for c in range(2):
                for hd in range(MH):
                    k = 4 * c + hd
                    got(dve, f"sc{c}{hd}")
                    minus_max(bank(f"sc{c}{hd}")[:, 0:MEM])
                    dve.wait_ge(s["pexp"], k + 1)
                    q(dve.reciprocal(att[:, 2:3], att[:, 1:2]))
                    emptied(TS(pr, pr, att[:, 2:3], None, ALU.mult), f"sc{c}{hd}")
                    got(dve, f"ao{c}{hd}")
                    emptied(dve.tensor_copy(aoT[:, 2 * hd:2 * hd + 2, P * c:P * (c + 1)],
                                            bank(f"ao{c}{hd}")[:, 0:256].rearrange("p (k l) -> p k l", k=2)), f"ao{c}{hd}")
            dve.memset(psum[6][:, :], 0.0)
            dve.memset(psum[7][:, :], 0.0).then_inc(s["zeroed"], 1)
            for b in range(NB):
                for i in range(2):
                    job = f"kt{b}{2 * i + 1}"
                    got(dve, job)
                    if b and i == 0:
                        dve.wait_ge(s["sb_full"], b)
                    emptied(dve.tensor_copy(kbT[:, 4 * i + 2:4 * i + 4].rearrange("p k m -> p (k m)"), bank(job)[:, :]), job)
                dve.wait_ge(s["sb_full"], b + 1)
                minus_max(psum[6][:, 0:MEM])
                dve.wait_ge(s["pexp"], 8 + b + 1)
                q(dve.reciprocal(att[:, 2:3], att[:, 1:2]))
                dve.wait_ge(s["ob_full"], b + 1)
                if b:
                    got(dve, f"ot{b - 1}")
                TS(oS, psum[7][:, 0:MD], att[:, 2:3], None, ALU.mult).then_inc(s["osb"], 1)
                got(dve, f"ot{b}")
                emptied(dve.tensor_copy(
                    aoT[:, :, NP + LS * b:NP + LS * (b + 1)].rearrange("p (h k) l -> p k h l", k=2),
                    bank(f"ot{b}")[:, 0:256].rearrange("p (k h l) -> p k h l", k=2, h=MH)[:, :, :, 0:LS]), f"ot{b}")
            for i in range(2):
                for c in range(NC):
                    R, job = ROWS[c], f"o{i}{c}"
                    got(dve, job)
                    v = h[0:R, c, BLK * i:BLK * (i + 1)]
                    emptied(TT(v, v, bank(job)[0:R, :], ALU.add), job)
            norm("ft", 2, V_FFN, tT)

            q(dve.memset(rtl, 0.0))
            got(dve, "lg")
            TT(rtl[:, 0:2], bank("lg")[:, 0:72].rearrange("p (c n) -> p c n", c=2),
               rbias[:, :].unsqueeze(1).to_broadcast([P, 2, 36]), ALU.add)
            emptied(TT(rtl[0:NS, 2], bank("lg")[0:NS, 72:108], rbias[0:NS, :], ALU.add), "lg")
            done(dve, "lg")

            def top(i):
                return rt[:, i, :, 0:1]

            def wide(v, k):
                return v.to_broadcast([P, NC, k])

            def first_max(src, k, mx, out):
                q(dve.tensor_reduce(top(mx), src, AX.X, ALU.max))
                q(TT(rt[:, 3, :, 0:k], src, wide(top(mx), k), ALU.is_equal))
                q(STT(out=rt[:, 5, :, 0:k], in0=rt[:, 3, :, 0:k], scalar=-99.0,
                      in1=iota[:, 0:k].unsqueeze(1).to_broadcast([P, NC, k]), op0=ALU.mult, op1=ALU.add))
                q(dve.tensor_reduce(top(6), rt[:, 5, :, 0:k], AX.X, ALU.min))
                return TT(rt[:, out, :, 0:k], rt[:, 5, :, 0:k], wide(top(6), k), ALU.is_equal)

            lgG, lgE = rtl[:, :, 0:NG], rtl[:, :, NG:]
            first_max(lgG, NG, 0, 4).then_inc(s["rt_oh"], 1)
            dve.wait_ge(s["rt_oh"], 1)
            oh = rt[:, 4, :, 0:NG]
            TT(rt[:, 1, :, 0:NG], lgG, wide(top(0), NG), ALU.subtract).then_inc(s["rt_a"], 1)
            q(TT(rte.rearrange("p c (g e) -> p c g e", g=NG), lgE.rearrange("p c (g e) -> p c g e", g=NG),
                 oh.unsqueeze(3).to_broadcast([P, NC, NG, NE]), ALU.mult))
            q(dve.tensor_reduce(rt[:, 8], rte.rearrange("p c (g e) -> p c e g", g=NG), AX.X, ALU.add))
            q(first_max(rt[:, 8], NE, 9, 10))
            q(STT(out=rt[:, 13], in0=rt[:, 10], scalar=-1e30, in1=rt[:, 8], op0=ALU.mult, op1=ALU.add))
            q(first_max(rt[:, 13], NE, 14, 15))
            TT(top(11), top(14), top(9), ALU.subtract).then_inc(s["rt_a"], 1)
            dve.wait_ge(s["rt_e"], 1)
            q(dve.tensor_reduce(top(7), rt[:, 2, :, 0:NG], AX.X, ALU.add))
            q(dve.reciprocal(top(7), top(7)))
            dve.wait_ge(s["rt_e"], 2)
            q(TS(top(16), top(12), 1.0, None, ALU.add))
            q(dve.reciprocal(top(16), top(16)))
            q(TT(top(16), top(16), top(7), ALU.mult))
            q(TT(top(17), top(16), top(12), ALU.mult))
            q(TT(comb[:, :, :], rt[:, 10], wide(top(16), NE), ALU.mult))
            q(TT(rt[:, 18], rt[:, 15], wide(top(17), NE), ALU.mult))
            q(TT(comb[:, :, :], comb[:, :, :], rt[:, 18], ALU.add))
            got(dve, "rk")
            STT(out=rg[:, 0:2, :], in0=bank("rk")[:, 0:8].rearrange("p (c g) -> p c g", c=2), scalar=1.0, in1=oh[:, 0:2],
                op0=ALU.add, op1=ALU.mult)
            STT(out=rg[0:NS, 2, :], in0=bank("rk")[0:NS, 8:12], scalar=1.0, in1=oh[0:NS, 2], op0=ALU.add, op1=ALU.mult)
            emptied(dve.reduce_max(rt[:, 19, 0, 0:1], bank("rk")[:, 16:16 + NG], AX.X), "rk")
            done(dve, "rk")
            q(TS(rg[:, :, :], rg[:, :, :], 1.0, None, ALU.subtract))
            q(TS(rt[:, 20, 0, 0:1], rt[:, 19, 0, 0:1], float(P), 1.0, ALU.is_gt, ALU.add))
            q(TS(rt[:, 21, 0, 0:1], rt[:, 19, 0, 0:1], float(2 * P), None, ALU.is_gt))
            TT(np_i[:, :], rt[:, 20, 0, 0:1], rt[:, 21, 0, 0:1], ALU.add).then_inc(s["npass"], 1)

            npass = load_passes(dve)
            with dve.Fori(0, npass) as rr:
                for c in range(NC):
                    for g in range(NG):
                        ins = TS(pg[:, c, P * g:P * (g + 1)], iota[:, :], rg[:, c, g:g + 1], None, ALU.is_equal)
                ins.then_inc(s["pg"], 1)
                with dve.Fori(0, NG) as g:
                    grp = rr * NG + g
                    base = grp * GCH
                    dve.wait_ge(s["gx_free"], rr * 13 + 13)
                    dve.wait_ge(s["xhi"], grp + 1)
                    TT(xlo, xg[:, bass.ds(g, 1)].rearrange("p g k l -> p (g k) l"), xhi.bitcast(F32), ALU.subtract).then_inc(
                        s["xlo"], 1)
                    for two in range(NE // 2):
                        b2, e2 = base + two * NCH, grp * NE + 2 * two

                        def hidden(x):
                            dve.wait_ge(s["chunk_done"], b2 + (4, 8)[x] + CD0)
                            dve.wait_ge(s["sil"], e2 + x + 1)
                            STT(out=hh[x], in0=sil[x], scalar=cg[:, bass.ds(g * NE + 2 * two + x, 1)], in1=psum[2 + x][:, :],
                                op0=ALU.mult, op1=ALU.mult).then_inc(s["hh"], 1)

                        def ht(x):
                            dve.wait_ge(s["hthi"], e2 + x + 2)
                            TT(htlo[x].rearrange("p j n -> p (j n)"), psum[4][:, :],
                               hthi[x].rearrange("p j n -> p (j n)").bitcast(F32), ALU.subtract).then_inc(s["htlo"], 1)

                        for pos in range(NCH):
                            if pos == 7:
                                hidden(0)
                            if pos == 11:
                                hidden(1)
                            dve.wait_ge(s["hi"], b2 + pos + 1)
                            TT(wlo[pos % PAIR], raw[pos % RAW], whi[pos % PAIR].bitcast(F32), ALU.subtract).then_inc(s["lo"], 1)
                            if two == 0 and pos == 3:
                                dve.wait_ge(s["chunk_done"], base + CD0)
                                for i in range(2):
                                    ins = dve.tensor_copy(yall[:, bass.ds(g, 1), BLK * i:BLK * (i + 1)],
                                                          psum[6 + i][:, :].unsqueeze(1))
                                ins.then_inc(s["y_free"], 1)
                            if pos == 9:
                                ht(0)
                            if pos == 11:
                                ht(1)
                dve.wait_ge(s["chunk_done"], rr * (NG * GCH) + (NG * GCH + CD0))
                for i in range(2):
                    ins = dve.tensor_copy(yall[:, NG, BLK * i:BLK * (i + 1)], psum[6 + i][:, :])
                ins.then_inc(s["fin_y"], 1)
                for i in range(2):
                    for c in range(NC):
                        R, k = ROWS[c], 3 * i + c
                        dve.wait_ge(s["sc_full"], rr * 6 + k + 1)
                        v = h[0:R, c, BLK * i:BLK * (i + 1)]
                        TT(v, v, psum[k % 2][0:R, :], ALU.add).then_inc(s["sc_free"], 1)
                TS(rg[:, :, :], rg[:, :, :], float(P), None, ALU.subtract).then_inc(s["rgdec"], 1)
                dve.wait_ge(s["rgdec"], rr + 1)
            q(TS(rs1[:, 0:1], rs[:, 0:1], 1.0, None, ALU.mult))
            TS(rs1[:, 0:1], rs[:, 0:1], 1.0, None, ALU.mult).then_inc(s["fin"], 1)

            dve.wait_ge(s["ss"], 14)
            root(3, 3)
            dve.wait_ge(s["ld_fin"], 16)
            for c in range(NC):
                R = ROWS[c]
                if c >= 2:
                    dve.wait_ge(s["out_y0"], 16)
                q(TS(fy[c % 2][0:R], h[0:R, c], rs[0:R, c:c + 1], None, ALU.mult))
                TT(fy[c % 2][0:R], fy[c % 2][0:R], gfin[0:R], ALU.mult).then_inc(s["fy"], 1)


_INS = [
    'x_prompt', 'x_sample', 'state_conv', 'state_ssd', 'state_s5_re', 'state_s5_im', 'cache_mem_k', 'cache_mem_v',
    'mem_prompt', 'norm_mix_g', 'w_in', 'conv_w', 'conv_b', 'ssd_dt_bias', 'ssd_a_log', 'ssd_d', 'ssd_norm_g',
    'w_ssd_branch', 's5_lambda_re', 's5_lambda_im', 's5_log_step', 's5_b_re', 's5_b_im', 's5_c_re', 's5_c_im', 's5_d',
    'w_glu', 'b_glu', 'w_mix_out', 'norm_mem_q_g', 'norm_mem_kv_g', 'w_mem_q', 'w_mem_k', 'w_mem_v', 'w_mem_o',
    'norm_ffn_g', 'w_router_group', 'b_router_group', 'w_router_expert', 'b_router_expert', 'w_exp_gate', 'w_exp_up',
    'w_exp_down', 'norm_final_g',
]
_OUTS = [
    ("yp", (1, NP, D)), ("ys", (NB, LS, D)), ("cvp", (1, 1, 3, CD)), ("ssdp", (1, 1, HEADS, HD, STATE)),
    ("rep", (1, 1, S5G, S5N)), ("imp", (1, 1, S5G, S5N)), ("mk", (1, 1, MEM, MH, MD)), ("mv", (1, 1, MEM, MH, MD)),
    ("cvs", (1, NB, 3, CD)), ("ssds", (1, NB, HEADS, HD, STATE)), ("res", (1, NB, S5G, S5N)), ("ims", (1, NB, S5G, S5N)),
]


def kernel(**inputs):
    import numpy as _np
    import concourse.bacc as _bacc
    from concourse import mybir as _mybir
    from concourse.bass_utils import run_bass_kernel_spmd as _run

    nc = _bacc.Bacc("TRN2", target_bir_lowering=False, num_devices=1)
    arrays, a, o = {}, {}, {}
    for name in _INS:
        x = _np.ascontiguousarray(inputs[name])
        arrays[f"in_{name}_dram"] = x
        a[name] = nc.dram_tensor(f"in_{name}_dram", x.shape, _mybir.dt.from_np(x.dtype), kind="ExternalInput").ap()
    for name, shape in _OUTS:
        o[name] = nc.dram_tensor(f"out_{name}_dram", shape, _mybir.dt.float32, kind="ExternalOutput").ap()
    layer(nc, a, o)
    r = _run(nc, [arrays], core_ids=[0])
    return tuple(r.results[0][f"out_{name}_dram"] for name, _ in _OUTS)
```

```python
from contextlib import ExitStack

import concourse.bass as bass
from concourse import mybir

F32 = mybir.dt.float32
F32R = mybir.dt.float32r
I32 = mybir.dt.int32
ACT = mybir.ActivationFunctionType
ALU = mybir.AluOpType
AX = mybir.AxisListType

P = 128
D = 1024
KT = D // P
NP, NS = 256, 64
T = NP + NS
NB, LS = 8, 8
ROWS = (128, 128, 64)
NC = 3
CD = 1536
CT = CD // P
HEADS, HD = 16, 64
STATE = 128
S5G, S5K, S5N = 64, 16, 64
NST = S5G * S5N // P
MEM, MH, MD = 256, 4, 256
NG, NE, TOPF = 4, 8, 512
EPS = 1e-6
TWO_PI = 6.283185307179586
PI = 3.1415925
BLK = 512
CH = 2048
RAW = 6
PAIR = 4
CHUNKS = [(x, part, half) for x, part in ((0, 0), (0, 1), (1, 0), (1, 1), (0, 2), (1, 2)) for half in range(2)]
NCH = len(CHUNKS)
GCH = NCH * NE // 2
CD0, LO0 = 8, RAW
RING = 6
STAT_SLOTS = 3
COL = {"z": 0, "xbc": D, "dt": D + CD, "u5": D + CD + HEADS, "ga": D + CD + HEADS + D, "gb": D + CD + HEADS + 2 * D}

V_MIX, V_SSD, V_Q, V_KV, V_FFN, V_D5, V_GLU, V_CW, V_CB = 0, 8, 16, 24, 32, 40, 48, 64, 112

BLOCKS = (
    [(f"u5{i}", "w_in", COL["u5"] + BLK * i) for i in range(2)]
    + [(f"xbc{i}", "w_in", COL["xbc"] + BLK * i) for i in range(3)]
    + [(f"mk{i}", "w_mem_k", BLK * i) for i in range(2)]
    + [(f"mv{i}", "w_mem_v", BLK * i) for i in range(2)]
    + [(f"z{i}", "w_in", COL["z"] + BLK * i) for i in range(2)]
    + [(f"ga{i}", "w_in", COL["ga"] + BLK * i) for i in range(2)]
    + [(f"sb{i}", "w_ssd_branch", BLK * i) for i in range(2)]
    + [(f"gb{i}", "w_in", COL["gb"] + BLK * i) for i in range(2)]
    + [("gv0", "w_glu", 0), ("gg0", "w_glu", D), ("gv1", "w_glu", BLK), ("gg1", "w_glu", D + BLK)]
    + [(f"mx{i}", "w_mix_out", BLK * i) for i in range(2)]
    + [(f"q{i}", "w_mem_q", BLK * i) for i in range(2)]
    + [(f"o{i}", "w_mem_o", BLK * i) for i in range(2)]
)
BIDX = {b[0]: n for n, b in enumerate(BLOCKS)}
SPLIT0 = BIDX["z0"]
UNITS = 2 * (len(BLOCKS) - SPLIT0)
UNIT_LAST = []
for _name, _, _ in BLOCKS[SPLIT0:]:
    _kind, _i = _name[:-1], int(_name[-1])
    UNIT_LAST += [f"{_kind}{2 * _i + _h}2" if _kind in ("mx", "o") else f"{_kind}{4 * _i + 2 * _h + 1}" for _h in range(2)]

FILL = (
    [("xbc", m) for m in range(CT)]
    + [("mk", m) for m in range(KT)]
    + [("mv", 2 * n + c) for n in range(2) for c in range(2)]
)


LATE = {24: ["ko00", "ko01"], 25: ["ko10", "ko11"], 26: ["dtT"], 27: ["dt3"], 29: ["cs"]}


def plan():
    j = ["par"]
    j += [f"x{c}{h}" for c in range(NC) for h in range(2)]
    j += [f"m{c}{h}" for c in range(2) for h in range(2)]
    j += ["s5h", "cvs"]
    j += [f"u5{m}" for m in range(KT)]
    j += [f"bt{q}" for q in range(4)] + [f"ct{q}" for q in range(4)]
    for st in range(NST):
        j += [f"bu{st}r", f"bu{st}i"]
        if st < len(FILL):
            j.append(f"{FILL[st][0]}{FILL[st][1]}")
        j += LATE.get(st, [])
    j += ["s5o0", "s5o1"] + [f"nc{q}" for q in range(3)]
    j += ["ecs"] + [f"ecp{q}" for q in range(2)]
    for c in range(NC):
        j += [f"tr{c}0", f"tr{c}1", f"tb{c}", f"cb{c}"]
    j += ["s00", "s01"]
    j += [f"csb0{c}" for c in range(NC)] + ["h00a", "h00b"]
    for q in range(4):
        if q < 3:
            j += [f"csb{q + 1}{c}" for c in range(NC)]
        for t in (2 * q, 2 * q + 1):
            j.append(f"yi{t}")
            if t < KT - 1:
                j += [f"h0{t + 1}a", f"h0{t + 1}b"]
            j += [f"yx{t}", f"ns{t}a", f"ns{t}b"]
    j += ["s10", "s11", "hl0", "hl1"]
    j += [f"z{m}" for m in range(KT)] + ["ssy"]
    j += [f"ga{m}" for m in range(KT)] + [f"sb{m}" for m in range(KT)] + [f"gb{m}" for m in range(KT)]
    for h in range(2):
        j += [f"gv{m}" for m in range(4 * h, 4 * h + 4)] + [f"gg{m}" for m in range(4 * h, 4 * h + 4)]
    j += [f"mx{u}{c}" for u in range(4) for c in range(NC)]
    j += [f"hq{c}{h}" for c in range(NC) for h in range(2)]
    j += [f"q{m}" for m in range(KT)]
    j += ["sc00", "sc01"]
    for k in range(2 * MH):
        j.append("pt%d%d" % divmod(k, MH))
        if k + 2 < 2 * MH:
            j.append("sc%d%d" % divmod(k + 2, MH))
        j.append("ao%d%d" % divmod(k, MH))
    j += [f"kt0{i}" for i in range(4)]
    for b in range(NB):
        if b < NB - 1:
            j += [f"kt{b + 1}{i}" for i in range(4)]
        if b:
            j.append(f"ot{b - 1}")
        j.append(f"sp{b}")
    j.append(f"ot{NB - 1}")
    j += [f"o{u}{c}" for u in range(4) for c in range(NC)]
    j += [f"ft{c}{h}" for c in range(NC) for h in range(2)]
    j += ["lg", "rk"]
    return j


PLAN = plan()
RB = 6
BANK = {job: (n % RB, n // RB) for n, job in enumerate(PLAN)}
assert len(BANK) == len(PLAN)
LAST = {f"{kind}{i}": f"{kind}{4 * i + 3}" for kind, n in (("u5", 2), ("xbc", 3), ("mk", 2)) for i in range(n)}
LAST.update({f"mv{i}": f"mv{2 * i + 1}" for i in range(2)})

SEMS = (
    "ld_par ld_x ld_mem ld_small ld_s5 ld_st0 ld_st1 ld_st2 ld_st3 ld_k0 ld_k1 ld_v0 ld_v1 ld_h ld_fin "
    "dve act pool consts rows ss var rs0 xn s5w s5c s5par bx cx inj "
    "tab_half tab_ready tab_used scan s5rot sl y5_full y5_free convout xc "
    "dtx sp_e dt_ready cs_in wdec etot bblk csd csm mt y_done ysq yr yn glu_used "
    "whi wlo hn_hi hn_lo yb_hi yb_lo u5_hi u5_lo mrg_hi mrg_lo q_hi q_lo ao_hi ao_lo hn2 nmax pexp sb_full ob_full osb zeroed rt_a rt_e rt_oh npass "
    "fin_y pg gx_full gx_free xhi xlo chunk_done hi lo sil hh t_full hthi htlo y_free sc_full sc_free rgdec fin fy "
    "out_v out_k out_s5 out_cv out_st0 out_st1 out_st2 out_st3 out_hl out_y0 out_y1 out_y2"
).split()


def layer(nc, a, o):
    ctx = ExitStack()
    with ctx:
        def sb(name, shape, dt=F32):
            return ctx.enter_context(nc.sbuf_tensor(name, shape, dt))

        def sem(name):
            return ctx.enter_context(nc.semaphore(name))

        ring_at = (nc.sbuf_base + 31) // 32 * 32
        ring = sb("ring", [P, RING * 4096])
        work_at = (nc.sbuf_base + 31) // 32 * 32
        work = sb("work", [P, 23820])

        def rounded(name, at, cols):
            return nc.alloc_sbuf_tensor_at(name, [P, cols], F32R, offset=at)

        usplit = rounded("usplit", ring_at + 4 * STAT_SLOTS * 4096, 4 * CH)
        ops = {at: rounded(f"ops{at}", work_at + 4 * at, KT * T) for at in (0, 2560, 9216, 13056, 15360, 15616, 18176)}
        wsplit = rounded("wsplit", ring_at, PAIR * 2 * CH)
        xsplit = rounded("xsplit", work_at + 4 * 9984, 2 * D)
        hsplit = rounded("hsplit", work_at + 4 * 14080, 4 * TOPF)
        slots = [ring[:, 4096 * i:4096 * (i + 1)] for i in range(RING)]

        def w(at, *dims):
            n = 1
            for d in dims:
                n *= d
            v = work[:, at:at + n]
            return view(v, dims)

        def r(at, *dims):
            n = 1
            for d in dims:
                n *= d
            at += STAT_SLOTS * 4096
            return view(ring[:, at:at + n], dims)

        def view(v, dims):
            names = "abcd"[:len(dims)]
            if len(dims) == 1:
                return v
            kw = {names[i]: dims[i] for i in range(len(dims) - 1)}
            return v.rearrange(f"p ({' '.join(names)}) -> p {' '.join(names)}", **kw)

        ident = sb("ident", [P, P])
        ones = sb("ones", [P, P])
        upto = sb("upto", [P, P])
        before = sb("before", [P, P])
        upto_s = sb("upto_s", [NS, NB, LS])
        same_s = sb("same_s", [NS, NB, LS])
        neg = sb("neg", [P, P])
        neg_s = sb("neg_s", [NS, NB, LS])
        iota = sb("iota", [P, P])
        half2 = sb("half2", [P, 2])
        sel16 = sb("sel16", [P, 4, 2])
        grp2 = sb("grp2", [P, 2])
        start = sb("start", [P, T])
        vec = sb("vec", [P, 124])
        lam = sb("lam", [P, 104])
        hglu = sb("hglu", [P, KT])
        e = sb("e", [P, 8, 2, NST])
        s5p = sb("s5p", [P, 16, NST])
        wdt = sb("wdt", [P, KT, HEADS])
        wr = sb("wr", [P, KT, NG + NG * NE])
        rbias = sb("rbias", [P, NG + NG * NE])
        dtb = sb("dtb", [P, HEADS])
        alog = sb("alog", [P, HEADS])
        cst = sb("cst", [P, CT, 3 * NB])
        last3 = sb("last3", [P, CT, 27])
        ss = sb("ss", [P, 5])
        var = sb("var", [P, 5])
        rs0 = sb("rs0", [P, 5])
        rs1 = sb("rs1", [P, 5])
        rs = sb("rs", [P, 5])
        rg = sb("rg", [P, NC, NG])
        comb = sb("comb", [P, NC, NE])
        np_i = sb("np_i", [P, 1], I32)
        cg = sb("cg", [P, NG * NE])

        psum = [ctx.enter_context(nc.psum_tensor(f"bank{i}", [P, 512], F32)) for i in range(8)]
        s = {n: sem(n) for n in SEMS}
        full = [sem(f"full{i}") for i in range(RB)]
        free = [sem(f"free{i}") for i in range(RB)]
        w_in_sem = [sem(f"w_slot{i}") for i in range(STAT_SLOTS)]
        raw_in = [sem(f"raw_in{i}") for i in range(RAW)]

        def bank(job):
            return psum[BANK[job][0]]

        def got(eng, job):
            b, turn = BANK[job]
            eng.wait_ge(full[b], turn + 1)

        def done(eng, job):
            b, turn = BANK[job]
            eng.wait_ge(free[b], turn + 1)

        def emptied(ins, job):
            ins.then_inc(free[BANK[job][0]], 1)

        def unit_raw(u):
            n = SPLIT0 + u // 2
            return slots[n % STAT_SLOTS].rearrange("p (k n) -> p k n", k=KT)[:, :, 256 * (u % 2):256 * (u % 2) + 256]

        def unit_of(name, half=0):
            return 2 * (BIDX[name] - SPLIT0) + half

        block = ctx.enter_context(nc.Block())

        xt = r(0, NC, D)
        hnT = w(0, KT, T)
        u5T = w(2560, KT, T)
        kT = w(5120, KT, MEM)
        vm = w(7168, 2, D)
        xn = [w(5120, D), w(6144, D)]
        st_nat = w(7168, 2, 2, P)
        cv_nat = w(7680, CD)
        memraw = w(9216, 2, D)
        junk = w(11264, D)
        lamrow = w(12288, 3, P)
        vecrow = w(12672, P)
        ddrow = w(12800, P)
        lsrow = w(12928, 2)
        dd8 = w(12930, 2)
        xcT = w(9216, CT, T)
        mnT = w(13056, KT, MEM)
        bnat = w(15104, 2, NST, S5K)
        bx = w(16128, 2, NST, 2, S5K)
        cnat = w(18176, 2, KT, S5N)
        cx = w(19200, 2, KT, 2, S5N)
        tmp512 = w(21248, 512)
        inj = w(22784, 2, NB, NST)
        h0s = w(21760, 2, NB, NST)
        tab = [r(2560 * i, 2, 4, T) for i in range(2)]
        bT = r(5120, KT, 2, P)
        cT = r(7168, KT, 2, P)
        tabtmp = r(9216, 2, 4, 32)
        tabtmp2 = w(16384, 2, 4, P)
        cvin = [r(10240 + 347 * i, 347) for i in range(2)]
        cvout = [r(10934 + 344 * i, 344) for i in range(2)]
        sl = r(11622, 2, 9 * NST)
        ub = [w(15104 + 640 * i, 2, T) for i in range(2)]
        m1 = w(16384, 2, T)
        m2 = w(17024, 2, T)
        wb = [w(17664 + 640 * i, 2, T) for i in range(2)]
        n1 = w(18944, 2, T)
        n2 = w(19584, 2, T)
        sbuf = [w(20224 + 640 * i, 2, T) for i in range(3)]
        rm = [w(22144 + 320 * i, T) for i in range(2)]
        kout = w(13056, 2, D)
        s5out = w(15104, 6, P)
        ncout = w(16128, CD)
        xdt = r(0, NC, D)
        wx = r(3072, NC, D)
        bblk = r(6144, 2, NB, P)
        hbuf = [r(8192, NB, P), r(10240, NB, P), w(15616, NB, P), w(16640, NB, P)]
        h0T = r(9216, NB, P)
        s0T = r(11264, D)
        hl = r(8192, D)
        hlo = r(10240, KT, P)
        y = w(13056, KT, T)
        ecs = w(17664, KT, 192)
        btok = w(19200, NC, 2, P)
        cbT = w(19968, NC, 2, P)
        dm = [[w(20736 + 1280 * i, 4, P), w(21248 + 1280 * i, 4, P), w(21760 + 1280 * i, 4, NS)] for i in range(2)]
        ytmp = w(23300, 192)
        dsm = sb("dsm", [P, 12, NC, HEADS])
        dtx, dte, dtl, dtm, dt_, dtA, csk, tot, wend, etot = (dsm[:, i] for i in range(10))
        anegb = dsm[:, 10, 0]
        dtS = r(10240, T)
        zs = [w(20736 + 320 * i, T) for i in range(2)]
        ysq = w(9216, KT, T)
        yv, yr0, yr1, rb = (w(21376 + 320 * i, T) for i in range(4))
        mrg = w(15616, KT, T)
        thB = w(9216, KT, T)
        val = w(11776, 4, T)
        th = [w(18176 + 320 * i, T) for i in range(2)]
        h = w(20736, NC, D)
        uhi = [usplit[:, 2 * CH * i:2 * CH * i + CH].rearrange("p (k n) -> p k n", k=KT) for i in range(2)]
        ulo = [usplit[:, 2 * CH * i + CH:2 * CH * (i + 1)].rearrange("p (k n) -> p k n", k=KT) for i in range(2)]

        def op(at):
            return view(ops[at][:, :], (KT, T))

        hn_hi, hn_lo = op(18176), op(0)
        yb_hi, yb_lo = op(9216), op(13056)
        u5_hi, u5_lo = op(13056), op(2560)
        mrg_hi, mrg_lo = op(0), op(15616)
        q_hi, q_lo = op(15360), op(0)
        ao_hi, ao_lo = op(0), op(15360)
        hn = w(17920, D)
        hn2T = w(0, KT, T)
        qT = w(2560, KT, T)
        kv = [w(9216, 2, 2, D), view(slots[5], (2, 2, D))]
        kbT = [w(13312, KT, MEM), w(5120, KT, MEM)]
        aoT = w(15360, KT, T)
        pr = [w(18944, MEM), w(17920, MEM)]
        pT = [w(19200, 2, P), w(18176, 2, P)]
        oS = w(19456, MEM)
        att = w(19712, 2, 4)
        tn = w(0, NC, D)
        tT = w(11008, KT, T)
        pg = w(3072, NC, NG * P)
        xg = w(4608, NG, KT, P)
        yall = w(3584, NG + 1, D)
        pgT = w(8704, NG, T)
        tT = w(11008, KT, T)
        xhi, xlo = (view(xsplit[:, D * i:D * (i + 1)], (KT, P)) for i in range(2))
        sil = [w(12032 + 512 * i, TOPF) for i in range(2)]
        hh = [w(13056 + 512 * i, TOPF) for i in range(2)]
        hthi, htlo = ([view(hsplit[:, TOPF * (2 * j + i):TOPF * (2 * j + i + 1)], (4, P)) for i in range(2)]
                      for j in range(2))
        raw = [ring[:, PAIR * 2 * CH + CH * i:PAIR * 2 * CH + CH * (i + 1)] for i in range(4)]
        raw += [w(16128 + CH * i, CH) for i in range(2)]
        whi = [wsplit[:, 2 * CH * i:2 * CH * i + CH] for i in range(PAIR)]
        wlo = [wsplit[:, 2 * CH * i + CH:2 * CH * (i + 1)] for i in range(PAIR)]
        rt = w(18176, 24, NC, NE)
        rtl = w(18176 + 576, NC, NG + NG * NE)
        rte = w(18176 + 704, NC, NG * NE)
        gfin = w(0, D)
        fy = [w(1024 + 1024 * i, D) for i in range(2)]

        def wblock(name, c0):
            return a[name][0][:, c0:c0 + BLK].rearrange("(k p) n -> p k n", p=P)

        def blk(name):
            return slots[BIDX[name] % STAT_SLOTS].rearrange("p (k n) -> p k n", k=KT)

        def load_passes(eng):
            eng.wait_ge(s["npass"], 1)
            return eng.value_load(np_i[0:1, 0:1], min_val=1, max_val=NC)

        def squares(act, n0):
            for c in range(NC):
                R = ROWS[c]
                act.activation(hn[0:R], h[0:R, c], ACT.Square, accum_out=ss[0:R, c:c + 1]).then_inc(s["ss"], 1)
                act.wait_ge(s["ss"], n0 + c + 1)

        def keep_last(act, st):
            act.wait_ge(s["s5rot"], st + 1)
            v = sl.rearrange("p r (q s) -> p r q s", q=9)
            act.activation(v[:, :, 0:1, st], sbuf[st % 3][:, :, NP - 1:NP], ACT.Copy)
            act.activation(v[:, :, 1:9, st], sbuf[st % 3][:, :, NP:T].rearrange("p r (b l) -> p r b l", b=NB)[:, :, :, LS - 1],
                           ACT.Copy).then_inc(s["sl"], 1)

        @block.sync
        def _(sp):
            sp.dma_start(xt[:, 0:2, :], a["x_prompt"][0].rearrange("(c p) d -> p c d", p=P)).then_inc(s["ld_x"], 16)
            sp.dma_start(xt[0:NS, 2, :], a["x_sample"].rearrange("b l d -> (b l) d")).then_inc(s["ld_x"], 16)

            def load_block(n):
                name, weight, c0 = BLOCKS[n]
                m = n - STAT_SLOTS
                if m >= SPLIT0:
                    sp.wait_ge(s["wlo"], 2 * (m - SPLIT0) + 2)
                elif m >= 0:
                    got(sp, LAST[BLOCKS[m][0]])
                sp.dma_start(slots[n % STAT_SLOTS].rearrange("p (k n) -> p k n", k=KT), wblock(weight, c0)).then_inc(
                    w_in_sem[n % STAT_SLOTS], 16)

            for n in range(2):
                load_block(n)
            sp.dma_start(memraw, a["mem_prompt"][0].rearrange("(c p) d -> p c d", p=P)).then_inc(s["ld_mem"], 16)
            for n in range(2, BIDX["ga0"] + 1):
                load_block(n)
            sp.wait_ge(s["y5_full"], NST)
            done(sp, "s5o1")
            for t in range(KT):
                if t == 2:
                    sp.wait_ge(s["out_s5"], 96)
                    sp.wait_ge(s["out_cv"], 32)
                if t >= 4:
                    sp.wait_ge(s[f"out_st{t % 4}"], 16 * (t // 4))
                sp.dma_start(hbuf[t % 4], a["state_ssd"][0].rearrange("b (t h) p n -> t (h p) b n", h=2)[t]).then_inc(
                    s[f"ld_st{t % 4}"], 16)
            for n in range(BIDX["ga1"], len(BLOCKS)):
                load_block(n)
                if BLOCKS[n][0] == "gb1":
                    sp.wait_ge(s["yn"], KT)
                    sp.dma_start(h[:, 0:2, :], a["x_prompt"][0].rearrange("(c p) d -> p c d", p=P)).then_inc(s["ld_h"], 16)
                    sp.dma_start(h[0:NS, 2, :], a["x_sample"].rearrange("b l d -> (b l) d")).then_inc(s["ld_h"], 16)
            sp.wait_ge(s["glu_used"], KT)
            sp.wait_ge(s["out_hl"], 16)
            for i in range(4):
                sp.wait_ge(s[f"out_st{i}"], 32)
            for b in range(NB):
                for i, (name, short) in enumerate((("cache_mem_k", "k"), ("cache_mem_v", "v"))):
                    if b >= 2:
                        if i == 0:
                            got(sp, f"kt{b - 2}3")
                        else:
                            sp.wait_ge(s["ob_full"], b - 1)
                    sp.dma_start(kv[b % 2][:, i], a[name][0, b].rearrange("(c p) h d -> p c (h d)", p=P)).then_inc(
                        s[f"ld_{short}{b % 2}"], 16)
            got(sp, f"o3{NC - 1}")
            sp.wait_ge(s["ob_full"], NB)
            for name, v in (("chunk_done", CD0), ("lo", LO0), ("hh", 2), ("hthi", 1), ("htlo", 1), ("y_free", 1), ("xlo", 1),
                            ("sc_free", 1)):
                sp.sem_inc(s[name], v)
            npass = load_passes(sp)
            with sp.Fori(0, npass) as rr:
                with sp.Fori(0, NG) as g:
                    for two in range(NE // 2):
                        for pos, (x, part, half) in enumerate(CHUNKS):
                            n = (rr * NG + g) * GCH + two * NCH + pos
                            slot, ex = pos % RAW, 2 * two + x
                            sp.wait_ge(s["lo"], n + 1)
                            if part < 2:
                                src = a[("w_exp_gate", "w_exp_up")[part]][0, bass.ds(g, 1), ex, 512 * half:512 * (half + 1)]
                            else:
                                src = a["w_exp_down"][0, bass.ds(g, 1), ex, 256 * half:256 * (half + 1)]
                            sp.dma_start(raw[slot].rearrange("p (k n) -> p k n", k=4 if part < 2 else 2),
                                         src.rearrange("g (k p) f -> p (g k) f", p=P)).then_inc(raw_in[slot], 16)
            sp.wait_ge(s["fin"], 1)
            sp.dma_start(gfin, a["norm_final_g"].rearrange("(a d) -> a d", a=1).to_broadcast([P, D])).then_inc(s["ld_fin"], 16)

        @block.gpsimd
        def _(pool):
            n = [0]

            def q(ins):
                n[0] += 1
                ins.then_inc(s["pool"], 1)
                pool.wait_ge(s["pool"], n[0])

            def keep(v, pattern, base, cm, fill, op=ALU.is_ge):
                q(pool.affine_select(out=v, in_=v, compare_op=op, fill=fill, base=base, pattern=pattern,
                                     channel_multiplier=cm))

            for v, c in ((ident, 0.0), (ones, 1.0), (upto, 1.0), (before, 1.0), (neg, 0.0), (half2, 0.0), (start, 1.0)):
                pool.memset(v[:, :], c)
            for v, c in ((upto_s, 1.0), (same_s, 1.0), (neg_s, 0.0), (sel16, 1.0), (dsm, 0.0), (rg, 0.0)):
                pool.memset(v.rearrange("p a b -> p (a b)") if len(v.shape) == 3 else v[:, :, :, :], c)
            pool.memset(ss[:, :], 1.0)
            q(pool.iota(iota[:, :], pattern=[[1, P]], base=0, channel_multiplier=0, allow_small_or_imprecise_dtypes=True))
            keep(ident[:, :], [[-1, P]], 0, 1, 1.0, ALU.not_equal)
            keep(upto[:, :], [[1, P]], 0, -1, 0.0)
            keep(before[:, :], [[1, P]], -1, -1, 0.0)
            keep(neg[:, :], [[1, P]], 0, -1, -1e30)
            keep(upto_s[:, :, :], [[LS, NB], [1, LS]], 0, -1, 0.0)
            keep(upto_s[:, :, :], [[-LS, NB], [0, LS]], 0, 1, 0.0)
            keep(neg_s[:, :, :], [[LS, NB], [1, LS]], 0, -1, -1e30)
            keep(neg_s[:, :, :], [[-LS, NB], [0, LS]], 0, 1, -1e30)
            keep(same_s[:, :, :], [[-LS, NB], [0, LS]], 0, 1, 0.0)
            keep(same_s[:, :, :], [[LS, NB], [0, LS]], LS - 1, -1, 0.0)
            keep(sel16[:, :, :], [[-32, 4], [-16, 2]], 0, 1, 0.0)
            keep(sel16[:, :, :], [[32, 4], [16, 2]], 15, -1, 0.0)
            q(pool.memset(half2[0:64, 0:1], 1.0))
            q(pool.memset(half2[64:128, 1:2], 1.0))
            q(pool.memset(start[:, 0:1], 0.0))
            pool.memset(start[:, NP:T].rearrange("p (b l) -> p b l", b=NB)[:, :, 0], 0.0).then_inc(s["consts"], 1)

            pool.wait_ge(s["s5par"], 1)

            def tables(oc):
                tb = tab[oc % 2]
                if oc >= 2:
                    pool.wait_ge(s["s5rot"], 4 * (oc - 1))
                    pool.wait_ge(s["tab_used"], 4 * (oc - 1))
                js = slice(4 * oc, 4 * oc + 4)
                pool.memset(tb[:, 0, :, 0:1], 1.0)
                q(pool.memset(tb[:, 1, :, 0:1], 0.0))
                q(pool.tensor_copy(tb[:, :, :, 1], e[:, 0, :, js]))
                for k in range(1, 6):
                    m = 2 ** k
                    new, old = tb[:, :, :, m:2 * m], tb[:, :, :, 0:m]
                    er = e[:, k, 0, js].unsqueeze(1).unsqueeze(3).to_broadcast([P, 2, 4, m])
                    ei = e[:, k, 1, js].unsqueeze(1).unsqueeze(3).to_broadcast([P, 2, 4, m])
                    pool.tensor_tensor(new, old, er, ALU.mult)
                    q(pool.tensor_tensor(tabtmp[:, :, :, 0:m], old, ei, ALU.mult))
                    pool.tensor_tensor(new[:, 0], new[:, 0], tabtmp[:, 1, :, 0:m], ALU.subtract)
                    q(pool.tensor_tensor(new[:, 1], new[:, 1], tabtmp[:, 0, :, 0:m], ALU.add))
                for ri in range(2):
                    ins = pool.tensor_copy(tb[:, ri, :, NP:T].rearrange("p j (b l) -> p j b l", b=NB),
                                           tb[:, ri, :, 0:LS].unsqueeze(2).to_broadcast([P, 4, NB, LS]))
                ins.then_inc(s["tab_half"], 1)

            tables(0)
            tables(1)
            for st in range(NST):
                tb, j = tab[st // 4 % 2], st % 4
                cs_ = tb[:, 0:1, j].to_broadcast([P, 2, T])
                sn_ = tb[:, 1:2, j].to_broadcast([P, 2, T])
                pool.wait_ge(s["scan"], 2 * st + 2)
                pool.wait_ge(s["tab_ready"], st // 4 + 1)
                if st:
                    pool.wait_ge(s["s5rot"], st)
                pool.tensor_tensor(n1, wb[st % 2], cs_, ALU.mult)
                q(pool.tensor_tensor(n2, wb[st % 2], sn_, ALU.mult))
                if st >= 3:
                    pool.wait_ge(s["y5_full"], st - 2)
                    pool.wait_ge(s["sl"], st - 2)
                pool.tensor_tensor(sbuf[st % 3][:, 0], n1[:, 0], n2[:, 1], ALU.subtract)
                pool.tensor_tensor(sbuf[st % 3][:, 1], n1[:, 1], n2[:, 0], ALU.add).then_inc(s["s5rot"], 1)
                if st % 4 == 3 and st // 4 + 2 < NST // 4:
                    tables(st // 4 + 2)

            done(pool, "mv3")
            pool.dma_start(o["mv"][0, 0].rearrange("(c p) a d -> p c (a d)", p=P), vm).then_inc(s["out_v"], 16)
            done(pool, "ko11")
            done(pool, "ko10")
            pool.dma_start(o["mk"][0, 0].rearrange("(c p) a d -> p c (a d)", p=P), kout).then_inc(s["out_k"], 16)
            done(pool, "s5o1")
            done(pool, "s5o0")
            for ri, part in enumerate(("re", "im")):
                pool.dma_start(o[part + "p"].rearrange("l b (s h) n -> (l b s) (h n)", h=2),
                               s5out[0:NST, ri]).then_inc(s["out_s5"], 16)
                for k in range(2):
                    pool.dma_start(o[part + "s"].rearrange("l b (s h) n -> (l b s) (h n)", h=2)[P * k:P * (k + 1)],
                                   s5out[:, 2 + 2 * ri + k]).then_inc(s["out_s5"], 16)
            done(pool, "nc2")
            done(pool, "nc1")
            pool.dma_start(o["cvp"].rearrange("l b t n -> (l b t) n"), ncout[0:3]).then_inc(s["out_cv"], 16)
            pool.dma_start(o["cvs"].rearrange("l b t n -> (l b t) n"), ncout[3:27]).then_inc(s["out_cv"], 16)
            for t in range(KT):
                done(pool, f"ns{t}b")
                pool.dma_start(o["ssds"][0].rearrange("b (t h) p n -> t (h p) b n", h=2)[t], hbuf[t % 4]).then_inc(
                    s[f"out_st{t % 4}"], 16)
            done(pool, "hl1")
            pool.dma_start(o["ssdp"][0, 0].rearrange("(t h) p n -> (h p) t n", h=2), hlo).then_inc(s["out_hl"], 16)
            for c in range(NC):
                pool.wait_ge(s["fy"], c + 1)
                if c < 2:
                    pool.dma_start(o["yp"][0, P * c:P * (c + 1)], fy[c % 2]).then_inc(s[f"out_y{c}"], 16)
                else:
                    pool.dma_start(o["ys"].rearrange("b l d -> (b l) d"), fy[c % 2][0:NS]).then_inc(s["out_y2"], 16)
            for name, v in (("out_v", 16), ("out_k", 16), ("out_s5", 96), ("out_cv", 32), ("out_hl", 16), ("out_st0", 32),
                            ("out_st1", 32), ("out_st2", 32), ("out_st3", 32), ("out_y0", 16), ("out_y1", 16), ("out_y2", 16)):
                pool.wait_ge(s[name], v)

        @block.scalar
        def _(act):
            n = [0]

            def q(ins):
                n[0] += 1
                ins.then_inc(s["act"], 1)
                act.wait_ge(s["act"], n[0])

            def rows(dst, src, sem_):
                act.dma_start(dst, src).then_inc(s[sem_], 16)

            for at, name in ((V_MIX, "norm_mix_g"), (V_SSD, "ssd_norm_g"), (V_Q, "norm_mem_q_g"), (V_KV, "norm_mem_kv_g"),
                             (V_FFN, "norm_ffn_g"), (V_D5, "s5_d"), (V_GLU, "b_glu")):
                k = a[name].shape[1] // P
                rows(vecrow[at:at + k], a[name][0].rearrange("(k p) -> k p", p=P), "ld_par")
            rows(vecrow[V_CW:V_CB], a["conv_w"][0].rearrange("t (k p) -> (t k) p", p=P), "ld_par")
            rows(vecrow[V_CB:124], a["conv_b"][0].rearrange("(k p) -> k p", p=P), "ld_par")
            rows(lamrow[0:NST, 0], a["s5_lambda_re"][0].rearrange("(s h) n -> s (h n)", h=2), "ld_par")
            rows(lamrow[0:NST, 1], a["s5_lambda_im"][0].rearrange("(s h) n -> s (h n)", h=2), "ld_par")
            rows(lsrow[0:NST], a["s5_log_step"][0].rearrange("(s h) -> s h", h=2), "ld_par")
            rows(dd8[0:KT], a["ssd_d"][0].rearrange("(s h) -> s h", h=2), "ld_par")
            for ri, name in enumerate(("s5_b_re", "s5_b_im")):
                rows(bnat[:, ri], a[name][0].rearrange("(s h) n k -> (h n) s k", h=2), "ld_s5")
            for ri, name in enumerate(("s5_c_re", "s5_c_im")):
                rows(cnat[:, ri], a[name][0].rearrange("(t i) k n -> (i k) t n", i=8), "ld_s5")
            for ri, name in enumerate(("state_s5_re", "state_s5_im")):
                rows(st_nat[:, ri], a[name][0].rearrange("(r b) (s h) n -> (b s) r (h n)", r=2, h=2), "ld_s5")
            rows(cv_nat[0:3 * NB], a["state_conv"][0].rearrange("b t n -> (b t) n"), "ld_s5")
            rows(wdt[:, :, :], a["w_in"][0][:, COL["dt"]:COL["dt"] + HEADS].rearrange("(k p) n -> p k n", p=P), "ld_small")
            rows(wr[:, :, 0:NG], a["w_router_group"][0].rearrange("(k p) n -> p k n", p=P), "ld_small")
            rows(wr[:, :, NG:], a["w_router_expert"][0].rearrange("(k p) n -> p k n", p=P), "ld_small")
            rows(dtb[:, :], a["ssd_dt_bias"].to_broadcast([P, HEADS]), "ld_small")
            rows(alog[:, :], a["ssd_a_log"].to_broadcast([P, HEADS]), "ld_small")
            rows(rbias[:, 0:NG], a["b_router_group"].to_broadcast([P, NG]), "ld_small")
            rows(rbias[:, NG:], a["b_router_expert"].to_broadcast([P, NG * NE]), "ld_small")

            def root(use, k=5):
                act.wait_ge(s["var"], use + 1)
                q(act.activation(rs0[:, 0:k], var[:, 0:k], ACT.Ln))
                act.activation(rs0[:, 0:k], rs0[:, 0:k], ACT.Exp, scale=-0.5).then_inc(s["rs0"], 1)

            act.wait_ge(s["consts"], 1)
            act.wait_ge(s["ld_x"], 32)
            for c in range(NC):
                R = ROWS[c]
                act.activation(junk[0:R], xt[0:R, c], ACT.Square, accum_out=ss[0:R, c:c + 1]).then_inc(s["ss"], 1)
                act.wait_ge(s["ss"], c + 1)
            act.wait_ge(s["ld_mem"], 16)
            for c in range(2):
                act.activation(junk, memraw[:, c], ACT.Square, accum_out=ss[:, 3 + c:4 + c]).then_inc(s["ss"], 1)
                act.wait_ge(s["ss"], 4 + c)
            root(0)
            act.wait_ge(s["s5w"], 1)
            act.activation(s5p[:, 0], lam[:, 2 * NST:3 * NST], ACT.Exp).then_inc(s["s5c"], 1)
            act.wait_ge(s["s5w"], 2)
            act.activation(s5p[:, 3], s5p[:, 1], ACT.Exp).then_inc(s["s5c"], 1)
            act.wait_ge(s["s5w"], 3)
            act.activation(e[:, 0, 1], s5p[:, 6], ACT.Sin)
            act.activation(e[:, 0, 0], s5p[:, 7], ACT.Sin).then_inc(s["s5c"], 1)
            got(act, "s5h")
            emptied(act.activation(h0s.rearrange("p r b s -> p (r b s)"), bank("s5h")[:, 0:512], ACT.Copy), "s5h")
            got(act, "cvs")
            emptied(act.activation(cst[:, :, :].rearrange("p k t -> p (k t)"), bank("cvs")[:, 0:CT * 24], ACT.Copy), "cvs")
            for m in range(KT):
                got(act, f"u5{m}")
                emptied(act.activation(u5T[:, m], bank(f"u5{m}")[:, 0:T], ACT.Copy), f"u5{m}")
            for t_, dst in (("bt", bT), ("ct", cT)):
                for i in range(4):
                    got(act, f"{t_}{i}")
                    emptied(act.activation(dst[:, 2 * i:2 * i + 2].rearrange("p t r n -> p (t r n)"),
                                           bank(f"{t_}{i}")[:, :], ACT.Copy), f"{t_}{i}")

            def fill_evac(kind, m):
                job = f"{kind}{m}"
                got(act, job)
                if kind == "xbc":
                    if m >= 2:
                        act.wait_ge(s["convout"], m - 1)
                    dst = cvin[m % 2]
                    act.activation(dst[:, 3:3 + NP], bank(job)[:, 0:NP], ACT.Copy)
                    emptied(act.activation(dst[:, 259:347].rearrange("p (b l) -> p b l", b=NB)[:, :, 3:11],
                                           bank(job)[:, NP:T].rearrange("p (b l) -> p b l", b=NB), ACT.Copy), job)
                elif kind == "mk":
                    emptied(act.activation(kT[:, m], bank(job)[:, 0:MEM], ACT.Copy), job)
                else:
                    emptied(act.activation(vm[:, m % 2, BLK * (m // 2):BLK * (m // 2 + 1)], bank(job)[:, :], ACT.Copy), job)

            def conv_silu(m):
                act.wait_ge(s["convout"], m + 1)
                v = cvout[m % 2]
                act.activation(xcT[:, m, 0:NP], v[:, 0:NP], ACT.Silu)
                src = v[:, 256:344].rearrange("p (b l) -> p b l", b=NB)[:, :, 3:11]
                act.activation(xcT[:, m, NP:T].rearrange("p (b l) -> p b l", b=NB), src, ACT.Silu).then_inc(s["xc"], 1)

            act.wait_ge(s["inj"], 1)
            for st in range(NST):
                got(act, f"bu{st}r")
                if st >= 2:
                    act.wait_ge(s["scan"], 2 * (st - 1))
                act.activation(rm[st % 2], start[:, :], ACT.Copy, scale=s5p[:, 3, st:st + 1])
                emptied(act.activation(ub[st % 2][:, 0], bank(f"bu{st}r")[:, 0:T], ACT.Copy), f"bu{st}r")
                got(act, f"bu{st}i")
                emptied(act.activation(ub[st % 2][:, 1], bank(f"bu{st}i")[:, 0:T], ACT.Copy), f"bu{st}i")
                if st < len(FILL):
                    fill_evac(*FILL[st])
                if st in (24, 25):
                    for hf in range(2):
                        job = f"ko{st - 24}{hf}"
                        got(act, job)
                        emptied(act.activation(kout[:, st - 24, 512 * hf:512 * hf + 512], bank(job)[:, :], ACT.Copy), job)
                if st == 26:
                    act.wait_ge(s["convout"], CT)
                    act.wait_ge(s["xc"], CT)
                    got(act, "dtT")
                    emptied(act.activation(dtS[0:HEADS], bank("dtT")[0:HEADS, 0:T], ACT.Copy), "dtT")
                if st == 28:
                    act.wait_ge(s["ld_small"], 16 * 7)
                    act.activation(anegb, alog[:, :], ACT.Exp).then_inc(s["sp_e"], 1)
                    act.wait_ge(s["dtx"], 1)
                    q(act.activation(dtl, dte, ACT.Exp))
                    act.activation(dtl, dtl, ACT.Ln, bias=1.0).then_inc(s["sp_e"], 1)
                if 1 <= st <= CT:
                    conv_silu(st - 1)
                if st >= 2:
                    keep_last(act, st - 2)
            keep_last(act, NST - 2)
            keep_last(act, NST - 1)
            got(act, "s5o0")
            emptied(act.activation(s5out[0:NST, 0:2].rearrange("p a n -> p (a n)"), bank("s5o0")[0:NST, 0:256], ACT.Copy), "s5o0")
            got(act, "s5o1")
            emptied(act.activation(s5out[:, 2:6].rearrange("p a n -> p (a n)"), bank("s5o1")[:, :], ACT.Copy), "s5o1")
            for i in range(3):
                got(act, f"nc{i}")
                emptied(act.activation(ncout[0:27, 512 * i:512 * i + 512], bank(f"nc{i}")[0:27, :], ACT.Copy), f"nc{i}")

            got(act, "ecs")
            act.wait_ge(s["cs_in"], 1)
            act.activation(wend, dtl, ACT.Exp).then_inc(s["wdec"], 1)
            act.activation(etot, tot, ACT.Exp).then_inc(s["etot"], 1)
            emptied(act.activation(ecs[:, :, P:192], bank("ecs")[:, :].rearrange("p (t l) -> p t l", t=KT), ACT.Exp), "ecs")
            for i in range(2):
                got(act, f"ecp{i}")
                emptied(act.activation(ecs[:, 4 * i:4 * i + 4, 0:P], bank(f"ecp{i}")[:, :].rearrange("p (t l) -> p t l", t=4),
                                       ACT.Exp), f"ecp{i}")
            for c in range(NC):
                R = ROWS[c]
                got(act, f"tb{c}")
                emptied(act.activation(btok[0:R, c].rearrange("p g n -> p (g n)"), bank(f"tb{c}")[0:R, 0:256], ACT.Copy), f"tb{c}")
                got(act, f"cb{c}")
                emptied(act.activation(cbT[0:R, c, :, 0:R], bank(f"cb{c}")[0:R, 0:2 * P].rearrange(
                    "p (g l) -> p g l", g=2)[:, :, 0:R], ACT.Copy), f"cb{c}")
            for g in range(2):
                got(act, f"s0{g}")
                emptied(act.activation(s0T[:, 512 * g:512 * g + 512], bank(f"s0{g}")[:, :], ACT.Copy), f"s0{g}")
            def decay(i):
                for c in range(NC):
                    act.wait_ge(s["csd"], 3 * i + c + 1)
                    d_ = dm[i % 2][c][0:ROWS[c]]
                    act.activation(d_, d_, ACT.Exp).then_inc(s["csm"], 1)

            decay(0)
            for i in range(4):
                for t in (2 * i, 2 * i + 1):
                    if t % 2 and i < 3:
                        decay(i + 1)
                    if t:
                        got(act, f"yx{t - 1}")
                    for hf, k in (("a", 0), ("b", 4)):
                        got(act, f"h0{t}{hf}")
                        emptied(act.activation(h0T[:, k:k + 4].rearrange("p b n -> p (b n)"), bank(f"h0{t}{hf}")[:, :],
                                               ACT.Copy), f"h0{t}{hf}")
            act.wait_ge(s["out_st1"], 32)
            for i in range(2):
                got(act, f"hl{i}")
                emptied(act.activation(hlo[:, 4 * i:4 * i + 4].rearrange("p t n -> p (t n)"), bank(f"hl{i}")[:, :],
                                       ACT.Copy), f"hl{i}")

            def split_unit(u):
                if u < UNITS:
                    n = SPLIT0 + u // 2
                    act.wait_ge(w_in_sem[n % STAT_SLOTS], 16 * (n // STAT_SLOTS + 1))
                    if u >= 2:
                        got(act, UNIT_LAST[u - 2])
                    act.activation(uhi[u % 2], unit_raw(u), ACT.Copy).then_inc(s["whi"], 1)

            got(act, "s11")
            done(act, "ns7b")
            split_unit(0)
            act.activation(hn_hi, hnT, ACT.Copy).then_inc(s["hn_hi"], 1)
            for m in range(KT):
                if m % 2 == 0:
                    split_unit(unit_of("z0") + m // 2 + 1)
                got(act, f"z{m}")
                if m >= 2:
                    act.wait_ge(s["y_done"], m - 1)
                emptied(act.activation(zs[m % 2], bank(f"z{m}")[:, 0:T], ACT.Silu), f"z{m}")
            for m in range(KT):
                act.wait_ge(s["y_done"], m + 1)
                act.activation(ysq[:, m], y[:, m], ACT.Square).then_inc(s["ysq"], 1)
            done(act, "ssy")
            q(act.activation(yr0, yv, ACT.Ln))
            act.activation(yr0, yr0, ACT.Exp, scale=-0.5).then_inc(s["yr"], 1)
            act.wait_ge(s["out_st2"], 32)
            act.wait_ge(s["out_st3"], 32)
            for m in range(KT):
                if m % 2 == 0:
                    split_unit(unit_of("ga0") + m // 2 + 1)
                if m == 2:
                    for k in range(KT):
                        act.wait_ge(s["yn"], k + 1)
                        act.activation(yb_hi[:, k], y[:, k], ACT.Copy).then_inc(s["yb_hi"], 1)
                got(act, f"ga{m}")
                emptied(act.activation(mrg[:, m], bank(f"ga{m}")[:, 0:T], ACT.Tanh, scale=0.5), f"ga{m}")
            for i in range(4):
                split_unit(unit_of("sb0") + i + 1)
            for m in range(KT):
                if m % 2 == 0:
                    split_unit(unit_of("gb0") + m // 2 + 1)
                got(act, f"gb{m}")
                emptied(act.activation(thB[:, m], bank(f"gb{m}")[:, 0:T], ACT.Tanh, scale=0.5), f"gb{m}")
                if m == 2:
                    act.wait_ge(s["y5_free"], KT)
                    act.activation(u5_hi, u5T, ACT.Copy).then_inc(s["u5_hi"], 1)

            def merged_hi(m):
                act.wait_ge(s["glu_used"], m + 1)
                act.activation(mrg_hi[:, m], mrg[:, m], ACT.Copy).then_inc(s["mrg_hi"], 1)

            for m in range(KT):
                if m % 4 == 0:
                    if m:
                        act.wait_ge(s["glu_used"], m)
                    for k in range(m, m + 4):
                        if k % 2 == 0:
                            split_unit(unit_of(f"gv{m // 4}") + (k - m) // 2 + 1)
                        got(act, f"gv{k}")
                        emptied(act.activation(val[:, k - m], bank(f"gv{k}")[:, 0:T], ACT.Identity,
                                               bias=vec[:, V_GLU + k:V_GLU + k + 1]), f"gv{k}")
                if m % 2 == 0:
                    split_unit(unit_of(f"gg{m // 4}") + m % 4 // 2 + 1)
                got(act, f"gg{m}")
                if m >= 2:
                    act.wait_ge(s["glu_used"], m - 1)
                emptied(act.activation(th[m % 2], bank(f"gg{m}")[:, 0:T], ACT.Tanh, scale=0.5, bias=hglu[:, m:m + 1]), f"gg{m}")
                if m:
                    merged_hi(m - 1)
            merged_hi(KT - 1)
            for i in range(4):
                split_unit(unit_of("mx0") + i + 1)

            done(act, f"mx3{NC - 1}")
            squares(act, 5)
            root(1, 3)
            for c in range(NC):
                for hf in range(2):
                    done(act, f"hq{c}{hf}")
                    v = (slice(None), slice(4 * hf, 4 * hf + 4), slice(P * c, P * c + ROWS[c]))
                    act.activation(q_hi[v], hn2T[v], ACT.Copy).then_inc(s["q_hi"], 1)
            for m in range(KT):
                if m % 2 == 0:
                    split_unit(unit_of("q0") + m // 2 + 1)
                got(act, f"q{m}")
                emptied(act.activation(qT[:, m], bank(f"q{m}")[:, 0:T], ACT.Copy, scale=1.0 / 16), f"q{m}")
            split_unit(unit_of("o0", 1))

            def exps(k, scores):
                act.wait_ge(s["nmax"], k + 1)
                act.activation(pr[k % 2], scores[:, 0:MEM], ACT.Exp, bias=att[:, k % 2, 0:1],
                               accum_out=att[:, k % 2, 1:2]).then_inc(s["pexp"], 1)

            def keys(b):
                for i in range(2):
                    got(act, f"kt{b}{2 * i}")
                    if b >= 2 and i == 0:
                        act.wait_ge(s["sb_full"], b - 1)
                    emptied(act.activation(kbT[b % 2][:, 4 * i:4 * i + 2].rearrange("p k m -> p (k m)"),
                                           bank(f"kt{b}{2 * i}")[:, :], ACT.Copy), f"kt{b}{2 * i}")

            exps(0, bank("sc00"))
            for k in range(2 * MH):
                c, hd = divmod(k, MH)
                if k < 7:
                    if k:
                        got(act, "pt%d%d" % divmod(k - 1, MH))
                    exps(k + 1, bank("sc%d%d" % divmod(k + 1, MH)))
                got(act, f"pt{c}{hd}")
                if k >= 2:
                    got(act, "ao%d%d" % divmod(k - 2, MH))
                emptied(act.activation(pT[k % 2].rearrange("p m l -> p (m l)"), bank(f"pt{c}{hd}")[:, 0:256], ACT.Copy),
                        f"pt{c}{hd}")
            keys(0)
            exps(8, psum[6])
            for b in range(NB):
                if b < NB - 1:
                    keys(b + 1)
                got(act, f"sp{b}")
                if b >= 2:
                    act.wait_ge(s["ob_full"], b - 1)
                else:
                    got(act, f"ao1{2 + b}")
                emptied(act.activation(pT[b % 2].rearrange("p m l -> p (m l)"), bank(f"sp{b}")[:, 0:256], ACT.Copy), f"sp{b}")
                if b < NB - 1:
                    exps(8 + b + 1, psum[6])
                if b == 1:
                    done(act, "ao13")
                    act.activation(ao_hi[:, :, 0:NP], aoT[:, :, 0:NP], ACT.Copy).then_inc(s["ao_hi"], 1)
            done(act, f"ot{NB - 1}")
            act.activation(ao_hi[:, :, NP:T], aoT[:, :, NP:T], ACT.Copy).then_inc(s["ao_hi"], 1)
            for i in range(1, 4):
                split_unit(unit_of("o0") + i + 1)
            done(act, f"o3{NC - 1}")
            squares(act, 8)
            root(2, 3)

            act.wait_ge(s["rt_a"], 1)
            act.activation(rt[:, 2, :, 0:NG], rt[:, 1, :, 0:NG], ACT.Exp).then_inc(s["rt_e"], 1)
            act.wait_ge(s["rt_a"], 2)
            act.activation(rt[:, 12, :, 0:1], rt[:, 11, :, 0:1], ACT.Exp).then_inc(s["rt_e"], 1)

            npass = load_passes(act)
            with act.Fori(0, npass) as rr:
                for k in range(KT):
                    act.wait_ge(s["gx_full"], rr * 13 + k + 1)
                    act.activation(xg[:, :, k], psum[k % 4][:, :].rearrange("p (g l) -> p g l", g=NG), ACT.Copy,
                                   scale=vec[:, V_FFN + k:V_FFN + k + 1]).then_inc(s["gx_free"], 1)
                for g in range(NG):
                    act.wait_ge(s["gx_full"], rr * 13 + KT + g + 1)
                    act.activation(pgT[:, g], psum[(KT + g) % 4][:, 0:T], ACT.Copy).then_inc(s["gx_free"], 1)
                act.wait_ge(s["gx_full"], rr * 13 + 13)
                act.activation(cg[:, :], psum[0][:, 0:NG * NE], ACT.Copy).then_inc(s["gx_free"], 1)
                with act.Fori(0, NG) as g:
                    base = (rr * NG + g) * GCH
                    act.wait_ge(s["chunk_done"], base - 4 + CD0)
                    act.wait_ge(s["xlo"], rr * NG + g + 1)
                    act.activation(xhi, xg[:, bass.ds(g, 1)].rearrange("p g k l -> p (g k) l"), ACT.Copy).then_inc(s["xhi"], 1)
                    for two in range(NE // 2):
                        b2 = base + two * NCH

                        def silu(x):
                            act.wait_ge(s["chunk_done"], b2 + (2, 6)[x] + CD0)
                            act.activation(sil[x], psum[x][:, :], ACT.Silu).then_inc(s["sil"], 1)

                        def ht(x):
                            act.wait_ge(s["t_full"], (rr * NG + g) * NE + 2 * two + x + 1)
                            act.activation(hthi[x].rearrange("p j n -> p (j n)"), psum[4][:, :], ACT.Copy).then_inc(s["hthi"], 1)

                        for pos in range(NCH):
                            act.wait_ge(raw_in[pos % RAW], ((rr * NG + g) * (GCH // RAW) + two * (NCH // RAW) + pos // RAW + 1) * 16)
                            act.wait_ge(s["chunk_done"], b2 + pos - PAIR + 1 + CD0)
                            act.activation(whi[pos % PAIR], raw[pos % RAW], ACT.Copy).then_inc(s["hi"], 1)
                            if pos == 5:
                                silu(0)
                            if pos == 9:
                                silu(1)
                                ht(0)
                            if pos == 11:
                                ht(1)
            act.wait_ge(s["fin"], 1)
            squares(act, 11)
            root(3, 3)

        @block.tensor
        def _(pe):
            at = [0]

            def take(job):
                assert PLAN[at[0]] == job, (PLAN[at[0]], job)
                at[0] += 1
                b, turn = BANK[job]
                if turn:
                    pe.wait_ge(free[b], turn)
                return psum[b]

            def end(ins, job):
                ins.then_inc(full[BANK[job][0]], 1)

            def tr(out, in_, rows=P):
                return nc.tensor.transpose(out, in_, ident[0:rows, 0:rows])

            def have(block_):
                k = BIDX[block_]
                pe.wait_ge(w_in_sem[k % STAT_SLOTS], 16 * (k // STAT_SLOTS + 1))

            def proj(kind, m, src, N):
                job = f"{kind}{m}"
                b = take(job)
                if m % 4 == 0:
                    have(f"{kind}{m // 4}")
                wv = blk(f"{kind}{m // 4}")
                for k in range(KT):
                    ins = nc.tensor.matmul(b[:, 0:N], wv[:, k, P * (m % 4):P * (m % 4 + 1)], src[:, k, 0:N],
                                           start=(k == 0), stop=(k == KT - 1))
                end(ins, job)

            def proj_tok(job, block_, src, c, R):
                b = take(job)
                wv = blk(block_)
                for k in range(KT):
                    ins = nc.tensor.matmul(b[0:R, :], src[:, k, P * c:P * c + R], wv[:, k, :],
                                           start=(k == 0), stop=(k == KT - 1))
                end(ins, job)

            pe.wait_ge(s["consts"], 1)
            b = take("par")
            pe.wait_ge(s["ld_par"], 16 * 13)
            pe.wait_ge(s["rows"], 1)
            nc.tensor.transpose(b[:, 0:124], vecrow[0:124], ident[0:124, 0:124])
            for i in range(3):
                tr(b[:, 128 + NST * i:128 + NST * (i + 1)], lamrow[0:NST, i], NST)
            end(tr(b[:, 224:232], ddrow[0:KT], KT), "par")
            for i, (kind, c) in enumerate([("x", c) for c in range(NC)] + [("m", c) for c in range(2)]):
                R = ROWS[c] if kind == "x" else P
                pe.wait_ge(s["xn"], i + 1)
                for hf in range(2):
                    b = take(f"{kind}{c}{hf}")
                    for j in range(4):
                        ins = tr(b[:, P * j:P * j + R], xn[i % 2][0:R, P * (4 * hf + j):P * (4 * hf + j + 1)], R)
                    end(ins, f"{kind}{c}{hf}")
            pe.wait_ge(s["ld_s5"], 16 * 7)
            b = take("s5h")
            for ri in range(2):
                for k in range(2):
                    ins = tr(b[:, 256 * ri + P * k:256 * ri + P * (k + 1)], st_nat[:, ri, k])
            end(ins, "s5h")
            b = take("cvs")
            for k in range(CT):
                ins = tr(b[:, 24 * k:24 * k + 24], cv_nat[0:24, P * k:P * (k + 1)], 24)
            end(ins, "cvs")
            done(pe, "x21")
            done(pe, "x20")
            for m in range(KT):
                proj("u5", m, hnT, T)
            for t_, src in (("bt", bx), ("ct", cx)):
                pe.wait_ge(s["bx"] if t_ == "bt" else s["cx"], 1)
                for i in range(4):
                    b = take(f"{t_}{i}")
                    for k in range(2):
                        for ri in range(2):
                            ft = 2 * i + k
                            v = src[:, ri].rearrange("p a b c -> p (a b c)")[:, P * ft:P * (ft + 1)]
                            ins = tr(b[:, P * (2 * k + ri):P * (2 * k + ri + 1)], v)
                    end(ins, f"{t_}{i}")
            for i in range(4):
                done(pe, f"bt{i}")
                done(pe, f"ct{i}")
            done(pe, "u57")
            done(pe, "m11")
            done(pe, "m10")

            def s5_out(st):
                ft, i = st // 4, st % 4
                yb = psum[6 + ft % 2]
                pe.wait_ge(s["s5rot"], st + 1)
                if i == 0 and ft >= 2:
                    pe.wait_ge(s["y5_free"], ft - 1)
                for ri in range(2):
                    ins = nc.tensor.matmul(yb[32 * i:32 * i + 32, 0:T], cT[:, ft, ri, 32 * i:32 * i + 32],
                                           sbuf[st % 3][:, ri], start=(ri == 0), stop=(ri == 1))
                ins.then_inc(s["y5_full"], 1)

            up = [upto[:, :], upto[:, :], upto_s[:, :, :].rearrange("p b l -> p (b l)")]
            al = [ones[:, :], ones[:, :], same_s[:, :, :].rearrange("p b l -> p (b l)")]
            for st in range(NST):
                ft, i = st // 4, st % 4
                for ri, c in enumerate("ri"):
                    b = take(f"bu{st}{c}")
                    end(nc.tensor.matmul(b[:, 0:T], bT[32 * i:32 * i + 32, ft, ri], u5T[32 * i:32 * i + 32, ft],
                                         start=True, stop=True), f"bu{st}{c}")
                if st < len(FILL):
                    kind, m = FILL[st]
                    if kind == "xbc":
                        proj("xbc", m, hnT, T)
                    elif kind == "mk":
                        proj("mk", m, mnT, MEM)
                    else:
                        if m % 2 == 0:
                            have(f"mv{m // 2}")
                        proj_tok(f"mv{m}", f"mv{m // 2}", mnT, m % 2, P)
                if st in (24, 25):
                    done(pe, "mk7")
                    m = st - 24
                    for hf in range(2):
                        b = take(f"ko{m}{hf}")
                        for j in range(4):
                            ins = tr(b[:, P * j:P * (j + 1)], kT[:, 4 * hf + j, P * m:P * (m + 1)])
                        end(ins, f"ko{m}{hf}")
                if st == 26:
                    b = take("dtT")
                    pe.wait_ge(s["ld_small"], 16 * 7)
                    for k in range(KT):
                        ins = nc.tensor.matmul(b[0:HEADS, 0:T], wdt[:, k], hnT[:, k], start=(k == 0), stop=(k == KT - 1))
                    end(ins, "dtT")
                if st == 27:
                    b = take("dt3")
                    done(pe, "dtT")
                    for c in range(NC):
                        R = ROWS[c]
                        ins = tr(b[0:R, HEADS * c:HEADS * (c + 1)], dtS[0:HEADS, P * c:P * c + R], HEADS)
                    end(ins, "dt3")
                if st == 29:
                    b = take("cs")
                    pe.wait_ge(s["dt_ready"], 1)
                    for c in range(NC):
                        R = ROWS[c]
                        nc.tensor.matmul(b[0:R, HEADS * c:HEADS * (c + 1)], up[c], dtA[0:R, c], start=True, stop=True)
                        ins = nc.tensor.matmul(b[0:R, 48 + HEADS * c:48 + HEADS * (c + 1)], al[c], dtA[0:R, c],
                                               start=True, stop=True)
                    end(ins, "cs")
                if st >= 2:
                    s5_out(st - 2)
            s5_out(NST - 2)
            s5_out(NST - 1)
            pe.wait_ge(s["sl"], NST)
            b = take("s5o0")
            for ri in range(2):
                ins = tr(b[0:NST, P * ri:P * (ri + 1)], sl[:, ri, 0:NST])
            end(ins, "s5o0")
            b = take("s5o1")
            for ri in range(2):
                for k in range(2):
                    ins = tr(b[:, P * (2 * ri + k):P * (2 * ri + k + 1)], sl[:, ri, NST + P * k:NST + P * (k + 1)])
            end(ins, "s5o1")
            pe.wait_ge(s["convout"], CT)
            for i in range(3):
                b = take(f"nc{i}")
                for j in range(4):
                    ins = tr(b[0:27, P * j:P * (j + 1)], last3[:, 4 * i + j])
                end(ins, f"nc{i}")

            def cum_rows(out, c, head, M):
                R = ROWS[c]
                return nc.tensor.matmul(out, dtA[0:R, c, head:head + 1].to_broadcast([R, M]), up[c], start=True, stop=True)

            b = take("ecs")
            for hd in range(HEADS):
                t, q_ = hd // 2, 64 * (hd % 2)
                ins = cum_rows(b[q_:q_ + 64, NS * t:NS * (t + 1)], 2, hd, HD)
            end(ins, "ecs")
            for i in range(2):
                b = take(f"ecp{i}")
                for hd in range(8 * i, 8 * i + 8):
                    t, q_ = hd // 2 - 4 * i, 64 * (hd % 2)
                    ins = cum_rows(b[q_:q_ + 64, P * t:P * (t + 1)], 1, hd, HD)
                end(ins, f"ecp{i}")
            pe.wait_ge(s["xc"], CT)
            for c in range(NC):
                R, c0 = ROWS[c], P * c
                for i in range(2):
                    b = take(f"tr{c}{i}")
                    for j in range(4):
                        ins = tr(b[0:R, P * j:P * (j + 1)], xcT[:, 4 * i + j, c0:c0 + R])
                    end(ins, f"tr{c}{i}")
                b = take(f"tb{c}")
                for g in range(2):
                    ins = tr(b[0:R, P * g:P * (g + 1)], xcT[:, 8 + g, c0:c0 + R])
                end(ins, f"tb{c}")
                b = take(f"cb{c}")
                for g in range(2):
                    ins = nc.tensor.matmul(b[0:R, P * g:P * g + R], xcT[:, 8 + g, c0:c0 + R], xcT[:, 10 + g, c0:c0 + R],
                                           start=True, stop=True)
                end(ins, f"cb{c}")
            done(pe, "tr21")
            done(pe, "tb2")
            for g in range(2):
                b = take(f"s0{g}")
                end(nc.tensor.matmul(b[:, :], btok[:, 0, g], wx[:, 0, 512 * g:512 * g + 512], start=True, stop=True), f"s0{g}")

            def decays(i):
                for c in range(NC):
                    R = ROWS[c]
                    b = take(f"csb{i}{c}")
                    for j in range(4):
                        ins = cum_rows(b[0:R, P * j:P * j + R], c, 4 * i + j, R)
                    end(ins, f"csb{i}{c}")

            def old_states(t):
                pe.wait_ge(s[f"ld_st{t % 4}"], 16 * (t // 4 + 1))
                for hf, k in (("a", 0), ("b", 4)):
                    b = take(f"h0{t}{hf}")
                    for j in range(4):
                        ins = tr(b[:, P * j:P * (j + 1)], hbuf[t % 4][:, k + j])
                    end(ins, f"h0{t}{hf}")

            decays(0)
            old_states(0)
            for i in range(4):
                g = i // 2
                if i < 3:
                    decays(i + 1)
                for t in (2 * i, 2 * i + 1):
                    b = take(f"yi{t}")
                    pe.wait_ge(s["mt"], 3 * i + 3)
                    for c in range(NC):
                        R, mt = ROWS[c], dm[i % 2][c]
                        for q_ in range(2):
                            hd = 2 * t + q_
                            ins = nc.tensor.matmul(b[64 * q_:64 * q_ + 64, P * c:P * c + R], xdt[0:R, c, HD * hd:HD * (hd + 1)],
                                                   mt[0:R, hd % 4, 0:R], start=True, stop=True)
                    end(ins, f"yi{t}")
                    if t < KT - 1:
                        old_states(t + 1)
                    b = take(f"yx{t}")
                    done(pe, "s01")
                    nc.tensor.matmul(b[:, 0:P], s0T[:, P * t:P * (t + 1)], xcT[:, 10 + g, P:2 * P], start=True, stop=True)
                    done(pe, f"h0{t}b")
                    for k in range(NB):
                        ins = nc.tensor.matmul(b[:, P + LS * k:P + LS * (k + 1)], h0T[:, k],
                                               xcT[:, 10 + g, NP + LS * k:NP + LS * (k + 1)], start=True, stop=True)
                    end(ins, f"yx{t}")
                    pe.wait_ge(s["bblk"], 1)
                    for hf, k in (("a", 0), ("b", 4)):
                        b = take(f"ns{t}{hf}")
                        end(nc.tensor.matmul(b[:, :], wx[0:NS, 2, P * t:P * (t + 1)], bblk[0:NS, g, k:k + 4],
                                             start=True, stop=True), f"ns{t}{hf}")
            for g in range(2):
                b = take(f"s1{g}")
                end(nc.tensor.matmul(b[:, :], btok[:, 1, g], wx[:, 1, 512 * g:512 * g + 512], start=True, stop=True), f"s1{g}")
            done(pe, "s11")
            for i in range(2):
                b = take(f"hl{i}")
                for j in range(4):
                    ins = tr(b[:, P * j:P * (j + 1)], hl[:, P * (4 * i + j):P * (4 * i + j + 1)])
                end(ins, f"hl{i}")
            def proj_split(kind, m, hi_, lo_):
                job, u = f"{kind}{m}", unit_of(f"{kind}0") + m // 2
                if kind in ("gv", "gg"):
                    u = unit_of(f"{kind}{m // 4}") + m % 4 // 2
                b = take(job)
                pe.wait_ge(s["wlo"], u + 1)
                for k in range(KT):
                    wh, wl = (v[u % 2][:, k, P * (m % 2):P * (m % 2 + 1)] for v in (uhi, ulo))
                    nc.tensor.matmul(b[:, 0:T], wh, hi_[:, k], start=(k == 0), stop=False)
                    nc.tensor.matmul(b[:, 0:T], wh, lo_[:, k], start=False, stop=False)
                    ins = nc.tensor.matmul(b[:, 0:T], wl, hi_[:, k], start=False, stop=(k == KT - 1))
                end(ins, job)

            def tok_split(kind, i, c, hi_, lo_):
                R, job, u = ROWS[c], f"{kind}{i}{c}", unit_of(f"{kind}0") + i
                b = take(job)
                pe.wait_ge(s["wlo"], u + 1)
                for k in range(KT):
                    th_, tl_ = (v[:, k, P * c:P * c + R] for v in (hi_, lo_))
                    nc.tensor.matmul(b[0:R, 0:256], th_, uhi[u % 2][:, k], start=(k == 0), stop=False)
                    nc.tensor.matmul(b[0:R, 0:256], th_, ulo[u % 2][:, k], start=False, stop=False)
                    ins = nc.tensor.matmul(b[0:R, 0:256], tl_, uhi[u % 2][:, k], start=False, stop=(k == KT - 1))
                end(ins, job)

            pe.wait_ge(s["hn_lo"], 1)
            for m in range(KT):
                proj_split("z", m, hn_hi, hn_lo)
            b = take("ssy")
            pe.wait_ge(s["ysq"], KT)
            for m in range(KT):
                ins = nc.tensor.matmul(b[:, 0:T], ones[:, :], ysq[:, m], start=(m == 0), stop=(m == KT - 1))
            end(ins, "ssy")
            for m in range(KT):
                proj_split("ga", m, hn_hi, hn_lo)
            pe.wait_ge(s["yb_lo"], KT)
            for m in range(KT):
                proj_split("sb", m, yb_hi, yb_lo)
            for m in range(KT):
                proj_split("gb", m, hn_hi, hn_lo)
            pe.wait_ge(s["u5_lo"], 1)
            for i in range(2):
                for kind in ("gv", "gg"):
                    for m in range(4 * i, 4 * i + 4):
                        proj_split(kind, m, u5_hi, u5_lo)

            pe.wait_ge(s["mrg_lo"], KT)
            for i in range(4):
                for c in range(NC):
                    tok_split("mx", i, c, mrg_hi, mrg_lo)

            def norm_tr(kind, use):
                for c in range(NC):
                    R = ROWS[c]
                    pe.wait_ge(s["hn2"], 3 * use + c + 1)
                    for hf in range(2):
                        b = take(f"{kind}{c}{hf}")
                        src = hn if kind == "hq" else tn[:, c]
                        for j in range(4):
                            ins = tr(b[:, P * j:P * j + R], src[0:R, P * (4 * hf + j):P * (4 * hf + j + 1)], R)
                        end(ins, f"{kind}{c}{hf}")
                done(pe, f"{kind}20")
                done(pe, f"{kind}21")

            norm_tr("hq", 0)
            pe.wait_ge(s["q_lo"], 2 * NC)
            for m in range(KT):
                proj_split("q", m, q_hi, q_lo)
            done(pe, "q7")

            def scores(k):
                c, hd = divmod(k, MH)
                b = take(f"sc{c}{hd}")
                for i in range(2):
                    ins = nc.tensor.matmul(b[:, 0:MEM], qT[:, 2 * hd + i, P * c:P * (c + 1)], kT[:, 2 * hd + i],
                                           start=(i == 0), stop=(i == 1))
                end(ins, f"sc{c}{hd}")

            scores(0)
            scores(1)
            for k in range(2 * MH):
                c, hd = divmod(k, MH)
                b = take(f"pt{c}{hd}")
                done(pe, f"sc{c}{hd}")
                for i in range(2):
                    ins = tr(b[:, P * i:P * (i + 1)], pr[k % 2][:, P * i:P * (i + 1)])
                end(ins, f"pt{c}{hd}")
                if k + 2 < 2 * MH:
                    scores(k + 2)
                b = take(f"ao{c}{hd}")
                done(pe, f"pt{c}{hd}")
                for dt_i in range(2):
                    for i in range(2):
                        ins = nc.tensor.matmul(b[:, P * dt_i:P * (dt_i + 1)],
                                               vm[:, i, MD * hd + P * dt_i:MD * hd + P * (dt_i + 1)], pT[k % 2][:, i],
                                               start=(i == 0), stop=(i == 1))
                end(ins, f"ao{c}{hd}")
            pe.wait_ge(s["zeroed"], 1)

            def keys(bb):
                K = kv[bb % 2][:, 0]
                pe.wait_ge(s[f"ld_k{bb % 2}"], 16 * (bb // 2 + 1))
                for i in range(4):
                    b = take(f"kt{bb}{i}")
                    for k in range(2):
                        for m in range(2):
                            ft = 2 * i + k
                            ins = tr(b[:, 256 * k + P * m:256 * k + P * (m + 1)], K[:, m, P * ft:P * (ft + 1)])
                    end(ins, f"kt{bb}{i}")

            def sample_scores(bb):
                for i in range(4):
                    done(pe, f"kt{bb}{i}")
                if bb:
                    pe.wait_ge(s["pexp"], 8 + bb)
                cols = slice(NP + LS * bb, NP + LS * (bb + 1))
                for hd in range(MH):
                    for k in range(2):
                        ins = nc.tensor.matmul(psum[6][32 * hd:32 * hd + LS, 0:MEM], qT[:, 2 * hd + k, cols],
                                               kbT[bb % 2][:, 2 * hd + k], start=(k == 0), stop=(k == 1))
                ins.then_inc(s["sb_full"], 1)

            def sample_out(bb):
                b = take(f"ot{bb}")
                pe.wait_ge(s["osb"], bb + 1)
                for k in range(2):
                    ins = tr(b[:, P * k:P * (k + 1)], oS[:, P * k:P * (k + 1)])
                end(ins, f"ot{bb}")

            keys(0)
            sample_scores(0)
            for bb in range(NB):
                V = kv[bb % 2][:, 1]
                if bb < NB - 1:
                    keys(bb + 1)
                if bb:
                    sample_out(bb - 1)
                b = take(f"sp{bb}")
                pe.wait_ge(s["pexp"], 8 + bb + 1)
                for k in range(2):
                    ins = tr(b[:, P * k:P * (k + 1)], pr[bb % 2][:, P * k:P * (k + 1)])
                end(ins, f"sp{bb}")
                if bb < NB - 1:
                    sample_scores(bb + 1)
                done(pe, f"sp{bb}")
                pe.wait_ge(s[f"ld_v{bb % 2}"], 16 * (bb // 2 + 1))
                if bb:
                    pe.wait_ge(s["osb"], bb)
                for hd in range(MH):
                    for k in range(2):
                        ins = nc.tensor.matmul(psum[7][32 * hd:32 * hd + LS, 0:MD], pT[bb % 2][:, k, 32 * hd:32 * hd + LS],
                                               V[:, k, MD * hd:MD * (hd + 1)], start=(k == 0), stop=(k == 1))
                ins.then_inc(s["ob_full"], 1)
            sample_out(NB - 1)
            done(pe, "ot7")
            done(pe, "ao13")
            pe.wait_ge(s["ao_lo"], 2)
            for i in range(4):
                for c in range(NC):
                    tok_split("o", i, c, ao_hi, ao_lo)
            norm_tr("ft", 1)
            b = take("lg")
            for c in range(NC):
                R = ROWS[c]
                for k in range(KT):
                    ins = nc.tensor.matmul(b[0:R, 36 * c:36 * (c + 1)], tT[:, k, P * c:P * c + R], wr[:, k],
                                           start=(k == 0), stop=(k == KT - 1))
            end(ins, "lg")
            b = take("rk")
            pe.wait_ge(s["rt_oh"], 1)
            oh = rt[:, 4, :, 0:NG]
            for c in range(NC):
                R = ROWS[c]
                for c2 in range(c):
                    nc.tensor.matmul(b[0:R, NG * c:NG * (c + 1)], ones[:, 0:R], oh[:, c2], start=(c2 == 0), stop=False)
                nc.tensor.matmul(b[0:R, NG * c:NG * (c + 1)], before[0:R, 0:R], oh[0:R, c], start=(c == 0), stop=True)
            for c in range(NC):
                ins = nc.tensor.matmul(b[:, 16:16 + NG], ones[0:ROWS[c], :], oh[0:ROWS[c], c], start=(c == 0), stop=(c == NC - 1))
            end(ins, "rk")
            assert at[0] == len(PLAN)

            for i in range(RB):
                last = max(j for j in range(len(PLAN)) if j % RB == i)
                pe.wait_ge(free[i], last // RB + 1)
            npass = load_passes(pe)
            with pe.Fori(0, npass) as rr:
                pe.wait_ge(s["pg"], rr + 1)
                for k in range(KT):
                    if k < 4:
                        pe.wait_ge(s["sc_free"], rr * 6 + 1)
                    else:
                        pe.wait_ge(s["gx_free"], rr * 13 + k - 3)
                    for c in range(NC):
                        R = ROWS[c]
                        ins = nc.tensor.matmul(psum[k % 4][:, :], tn[0:R, c, P * k:P * (k + 1)], pg[0:R, c],
                                               start=(c == 0), stop=(c == NC - 1))
                    ins.then_inc(s["gx_full"], 1)
                for g in range(NG):
                    pe.wait_ge(s["gx_free"], rr * 13 + KT + g - 3)
                    for c in range(NC):
                        R = ROWS[c]
                        ins = tr(psum[(KT + g) % 4][:, P * c:P * c + R], pg[0:R, c, P * g:P * (g + 1)], R)
                    ins.then_inc(s["gx_full"], 1)
                pe.wait_ge(s["gx_free"], rr * 13 + 9)
                for g in range(NG):
                    for c in range(NC):
                        R = ROWS[c]
                        ins = nc.tensor.matmul(psum[0][:, NE * g:NE * (g + 1)], pg[0:R, c, P * g:P * (g + 1)], comb[0:R, c],
                                               start=(c == 0), stop=(c == NC - 1))
                ins.then_inc(s["gx_full"], 1)
                with pe.Fori(0, NG) as g:
                    grp = rr * NG + g
                    base = grp * GCH
                    pe.wait_ge(s["gx_free"], rr * 13 + 13)
                    pe.wait_ge(s["xlo"], grp + 2)
                    for two in range(NE // 2):
                        b2, e2 = base + two * NCH, grp * NE + 2 * two

                        def split_product(bank_, hi_, lo_, wh, wl, start, stop):
                            nc.tensor.matmul(bank_, hi_, wh, start=start, stop=False)
                            nc.tensor.matmul(bank_, hi_, wl, start=False, stop=False)
                            return nc.tensor.matmul(bank_, lo_, wh, start=False, stop=stop)

                        def turn(x):
                            pe.wait_ge(s["hh"], e2 + x + 3)
                            pe.wait_ge(s["hthi"], e2 + x + 1)
                            pe.wait_ge(s["htlo"], e2 + x + 1)
                            for j in range(4):
                                ins = tr(psum[4][:, P * j:P * (j + 1)], hh[x][:, P * j:P * (j + 1)])
                            ins.then_inc(s["t_full"], 1)

                        for pos, (x, part, half) in enumerate(CHUNKS):
                            pe.wait_ge(s["lo"], b2 + pos + 1 + LO0)
                            k_ = 4 if part < 2 else 2
                            wh, wl = (v[pos % PAIR].rearrange("p (k n) -> p k n", k=k_) for v in (whi, wlo))
                            if part < 2:
                                if part == 0 and half == 0:
                                    pe.wait_ge(s["hh"], e2 + x + 1)
                                for k in range(4):
                                    kk = 4 * half + k
                                    ins = split_product(psum[2 * part + x][:, :], xhi[:, kk], xlo[:, kk], wh[:, k], wl[:, k],
                                                        kk == 0, kk == KT - 1)
                            else:
                                if half == 0:
                                    pe.wait_ge(s["htlo"], e2 + x + 2)
                                    if two == 0 and x == 0:
                                        pe.wait_ge(s["y_free"], grp + 2)
                                for j in range(2):
                                    jj = 2 * half + j
                                    for n_ in range(2):
                                        ins = split_product(psum[6 + n_][:, :], hthi[x][:, jj], htlo[x][:, jj],
                                                            wh[:, j, BLK * n_:BLK * (n_ + 1)], wl[:, j, BLK * n_:BLK * (n_ + 1)],
                                                            two == 0 and x == 0 and jj == 0,
                                                            two == NE // 2 - 1 and x == 1 and jj == 3)
                            ins.then_inc(s["chunk_done"], 1)
                            if pos == 5:
                                turn(0)
                            if pos == 8:
                                turn(1)
                pe.wait_ge(s["fin_y"], rr + 1)
                for i in range(2):
                    for c in range(NC):
                        R, k = ROWS[c], 3 * i + c
                        if k >= 2:
                            pe.wait_ge(s["sc_free"], rr * 6 + k)
                        for g in range(NG):
                            ins = nc.tensor.matmul(psum[k % 2][0:R, :], pgT[:, g, P * c:P * c + R],
                                                   yall[:, g + 1, BLK * i:BLK * (i + 1)], start=(g == 0), stop=(g == NG - 1))
                        ins.then_inc(s["sc_full"], 1)
                pe.wait_ge(s["sc_free"], rr * 6 + 7)

        @block.vector
        def _(dve):
            n = [0]

            def q(ins):
                n[0] += 1
                ins.then_inc(s["dve"], 1)
                dve.wait_ge(s["dve"], n[0])

            TT, TS, STT = dve.tensor_tensor, dve.tensor_scalar, dve.scalar_tensor_tensor

            def root(use, k=5):
                TS(var[:, 0:k], ss[:, 0:k], 1.0 / D, EPS, ALU.mult, ALU.add).then_inc(s["var"], 1)
                dve.wait_ge(s["var"], use + 1)
                dve.wait_ge(s["rs0"], use + 1)
                q(TT(rs1[:, 0:k], rs0[:, 0:k], rs0[:, 0:k], ALU.mult))
                q(TT(rs1[:, 0:k], rs1[:, 0:k], var[:, 0:k], ALU.mult))
                q(TS(rs1[:, 0:k], rs1[:, 0:k], -0.5, 1.5, ALU.mult, ALU.add))
                q(TT(rs[:, 0:k], rs0[:, 0:k], rs1[:, 0:k], ALU.mult))

            dve.wait_ge(s["consts"], 1)
            dve.wait_ge(s["ld_par"], 16 * 13)
            q(dve.tensor_reduce(grp2[:, :], sel16[:, :, :].rearrange("p i a -> p a i"), AX.X, ALU.add))
            dve.memset(cvin[0][:, 0:3], 0.0)
            dve.memset(cvin[1][:, 0:3], 0.0)
            dve.tensor_copy(lamrow[0:NST, 2].rearrange("p (h n) -> p h n", h=2), lsrow[0:NST].unsqueeze(2).to_broadcast([NST, 2, 64]))
            dve.tensor_copy(ddrow[0:KT].rearrange("p (h n) -> p h n", h=2),
                            dd8[0:KT].unsqueeze(2).to_broadcast([KT, 2, 64])).then_inc(s["rows"], 1)
            got(dve, "par")
            dve.tensor_copy(vec[:, :], bank("par")[:, 0:124])
            emptied(dve.tensor_copy(lam[:, :], bank("par")[:, 128:232]), "par")
            done(dve, "par")
            TS(hglu[:, :], vec[:, V_GLU + KT:V_GLU + 2 * KT], 0.5, None, ALU.mult).then_inc(s["s5w"], 1)
            dve.wait_ge(s["ss"], 5)
            root(0)
            for i, (kind, c) in enumerate([("x", c) for c in range(NC)] + [("m", c) for c in range(2)]):
                R = ROWS[c] if kind == "x" else P
                src = xt[0:R, c] if kind == "x" else memraw[:, c]
                if i >= 2:
                    j = i - 2
                    got(dve, f"x{j}1")
                TS(xn[i % 2][0:R], src, rs[0:R, i:i + 1], None, ALU.mult).then_inc(s["xn"], 1)
                dst, v0 = (hnT, V_MIX) if kind == "x" else (mnT, V_KV)
                for hf in range(2):
                    job = f"{kind}{c}{hf}"
                    got(dve, job)
                    emptied(TT(dst[:, 4 * hf:4 * hf + 4, P * c:P * c + R],
                               bank(job)[:, :].rearrange("p (k l) -> p k l", k=4)[:, :, 0:R],
                               vec[:, v0 + 4 * hf:v0 + 4 * hf + 4].unsqueeze(2).to_broadcast([P, 4, R]), ALU.mult), job)

            (step, xr, xi, mag, k_, t0, red, redc, lbr, lbi, cr, ci, den, t1, t2, t3) = (s5p[:, i] for i in range(16))
            lr, li = lam[:, 0:NST], lam[:, NST:2 * NST]
            dve.wait_ge(s["s5c"], 1)
            q(TT(xi, li, step, ALU.mult))
            TT(xr, lr, step, ALU.mult).then_inc(s["s5w"], 1)
            magic = 12582912.0
            q(TS(k_, xi, 1.0 / TWO_PI, magic, ALU.mult, ALU.add))
            q(TS(k_, k_, magic, None, ALU.subtract))
            q(STT(out=red, in0=k_, scalar=-6.28125, in1=xi, op0=ALU.mult, op1=ALU.add))
            q(STT(out=red, in0=k_, scalar=-(TWO_PI - 6.28125), in1=red, op0=ALU.mult, op1=ALU.add))
            q(TS(red, red, PI, -PI, ALU.min, ALU.max))
            q(TS(redc, red, TWO_PI / 4, None, ALU.add))
            q(TS(t0, redc, PI, -TWO_PI, ALU.is_gt, ALU.mult))
            q(TT(redc, redc, t0, ALU.add))
            TS(redc, redc, PI, -PI, ALU.min, ALU.max).then_inc(s["s5w"], 1)
            dve.wait_ge(s["s5c"], 3)
            er, ei = e[:, 0, 0], e[:, 0, 1]
            q(TT(lbr, mag, er, ALU.mult))
            q(TT(lbi, mag, ei, ALU.mult))
            for k in range(1, 8):
                q(TT(t1, e[:, k - 1, 0], e[:, k - 1, 0], ALU.mult))
                q(TT(t2, e[:, k - 1, 1], e[:, k - 1, 1], ALU.mult))
                q(TT(e[:, k, 0], t1, t2, ALU.subtract))
                if k < 7:
                    q(STT(out=e[:, k, 1], in0=e[:, k - 1, 0], scalar=2.0, in1=e[:, k - 1, 1], op0=ALU.mult, op1=ALU.mult))
                else:
                    STT(out=e[:, k, 1], in0=e[:, k - 1, 0], scalar=2.0, in1=e[:, k - 1, 1], op0=ALU.mult, op1=ALU.mult)\
                        .then_inc(s["s5par"], 1)
            dve.wait_ge(s["s5par"], 1)
            q(TT(t1, lr, lr, ALU.mult))
            q(TT(t2, li, li, ALU.mult))
            q(TT(den, t1, t2, ALU.add))
            q(dve.reciprocal(den, den))
            q(TS(t0, lbr, 1.0, None, ALU.subtract))
            q(TT(t1, t0, lr, ALU.mult))
            q(TT(t2, lbi, li, ALU.mult))
            q(TT(t1, t1, t2, ALU.add))
            q(TT(cr, t1, den, ALU.mult))
            q(TT(t1, lbi, lr, ALU.mult))
            q(TT(t2, t0, li, ALU.mult))
            q(TT(t1, t1, t2, ALU.subtract))
            q(TT(ci, t1, den, ALU.mult))
            dve.wait_ge(s["ld_s5"], 16 * 7)
            crb, cib = (v.unsqueeze(2).to_broadcast([P, NST, S5K]) for v in (cr, ci))
            tm = view(tmp512, (NST, S5K))
            tm2 = view(junk[:, 0:512], (NST, S5K))
            for ri in range(2):
                q(TT(tm, bnat[:, ri], crb, ALU.mult))
                q(TT(tm2, bnat[:, 1 - ri], cib, ALU.mult))
                q(TT(tm, tm, tm2, ALU.subtract if ri == 0 else ALU.add))
                for h_ in range(2):
                    ins = TS(bx[:, ri, :, h_], tm, half2[:, h_:h_ + 1], None, ALU.mult)
                    if ri == 1 and h_ == 1:
                        ins.then_inc(s["bx"], 1)
                    else:
                        q(ins)
            for ri in range(2):
                for h_ in range(2):
                    ins = TS(cx[:, ri, :, h_], cnat[:, ri], grp2[:, h_:h_ + 1], 1.0 if ri == 0 else -1.0, ALU.mult, ALU.mult)
            ins.then_inc(s["cx"], 1)
            done(dve, "s5h")
            lb = [v.unsqueeze(1).to_broadcast([P, NB, NST]) for v in (lbr, lbi)]
            tj = view(tmp512[:, 0:256], (NB, NST))
            for ri in range(2):
                q(TT(inj[:, ri], h0s[:, ri], lb[0], ALU.mult))
                q(TT(tj, h0s[:, 1 - ri], lb[1], ALU.mult))
                ins = TT(inj[:, ri], inj[:, ri], tj, ALU.subtract if ri == 0 else ALU.add)
                if ri == 0:
                    q(ins)
            ins.then_inc(s["inj"], 1)
            dve.wait_ge(s["inj"], 1)

            def conv(m):
                job = f"xbc{m}"
                done(dve, job)
                vi, vo = cvin[m % 2], cvout[m % 2]
                if m >= 2:
                    dve.wait_ge(s["xc"], m - 1)
                q(dve.tensor_copy(vi[:, 259:347].rearrange("p (b l) -> p b l", b=NB)[:, :, 0:3],
                                  cst[:, m].rearrange("p (b t) -> p b t", b=NB)))
                q(TS(vo, vi[:, 0:344], vec[:, V_CW + m:V_CW + m + 1], vec[:, V_CB + m:V_CB + m + 1], ALU.mult, ALU.add))
                for k in range(1, 4):
                    q(STT(out=vo, in0=vi[:, k:k + 344], scalar=vec[:, V_CW + CT * k + m:V_CW + CT * k + m + 1], in1=vo,
                          op0=ALU.mult, op1=ALU.add))
                dve.tensor_copy(last3[:, m, 0:3], vi[:, 256:259])
                dve.tensor_copy(last3[:, m, 3:27].rearrange("p (b t) -> p b t", b=NB),
                                vi[:, 259:347].rearrange("p (b l) -> p b l", b=NB)[:, :, 8:11]).then_inc(s["convout"], 1)

            def y5_read(ft):
                dve.wait_ge(s["y5_full"], 4 * ft + 4)
                STT(out=u5T[:, ft], in0=u5T[:, ft], scalar=vec[:, V_D5 + ft:V_D5 + ft + 1], in1=psum[6 + ft % 2][:, 0:T],
                    op0=ALU.mult, op1=ALU.add).then_inc(s["y5_free"], 1)

            def double_tables(oc):
                dve.wait_ge(s["tab_half"], oc + 1)
                if oc >= 2:
                    dve.wait_ge(s["scan"], 8 * oc)
                tb, js = tab[oc % 2], slice(4 * oc, 4 * oc + 4)
                for k in (6, 7):
                    m = 2 ** k
                    new, old = tb[:, :, :, m:2 * m], tb[:, :, :, 0:m]
                    er = e[:, k, 0, js].unsqueeze(1).unsqueeze(3).to_broadcast([P, 2, 4, m])
                    ei = e[:, k, 1, js].unsqueeze(1).unsqueeze(3).to_broadcast([P, 2, 4, m])
                    TT(new, old, er, ALU.mult)
                    q(TT(tabtmp2[:, :, :, 0:m], old, ei, ALU.mult))
                    TT(new[:, 0], new[:, 0], tabtmp2[:, 1, :, 0:m], ALU.subtract)
                    ins = TT(new[:, 1], new[:, 1], tabtmp2[:, 0, :, 0:m], ALU.add)
                    if k == 6:
                        q(ins)
                ins.then_inc(s["tab_ready"], 1)
                dve.wait_ge(s["tab_ready"], oc + 1)

            for i in range(4):
                got(dve, f"bt{i}")
            double_tables(0)
            for st in range(NST):
                tb, j = tab[st // 4 % 2], st % 4
                cs_ = tb[:, 0:1, j].to_broadcast([P, 2, T])
                sn_ = tb[:, 1:2, j].to_broadcast([P, 2, T])
                done(dve, f"bu{st}i")
                done(dve, f"bu{st}r")
                if st:
                    dve.wait_ge(s["scan"], 2 * st)
                TT(m1, ub[st % 2], cs_, ALU.mult)
                q(TT(m2, ub[st % 2], sn_, ALU.mult))
                TT(m1[:, 0], m1[:, 0], m2[:, 1], ALU.add).then_inc(s["tab_used"], 1)
                q(TT(m1[:, 1], m1[:, 1], m2[:, 0], ALU.subtract))
                first = m1[:, :, NP:T].rearrange("p r (b l) -> p r b l", b=NB)[:, :, :, 0]
                q(TT(first, first, inj[:, :, :, st], ALU.add))
                if st >= 2:
                    dve.wait_ge(s["s5rot"], st - 1)
                for ri in range(2):
                    ins = dve.tensor_tensor_scan(wb[st % 2][:, ri], rm[st % 2], m1[:, ri], 0.0, ALU.mult, ALU.add)
                    ins.then_inc(s["scan"], 1)
                if 1 <= st <= CT:
                    conv(st - 1)
                if st % 4 == 3 and st < NST - 1:
                    double_tables(st // 4 + 1)
                if st % 4 == 2 and st > 4:
                    y5_read(st // 4 - 1)
                if st == 27:
                    got(dve, "dt3")
                    dve.wait_ge(s["ld_small"], 16 * 7)
                    TT(dtx[:, 0:2], bank("dt3")[:, 0:32].rearrange("p (c n) -> p c n", c=2),
                       dtb[:, :].unsqueeze(1).to_broadcast([P, 2, HEADS]), ALU.add)
                    emptied(TT(dtx[0:NS, 2], bank("dt3")[0:NS, 32:48], dtb[0:NS, :], ALU.add), "dt3")
                    done(dve, "dt3")
                    q(TS(dtm, dtx, -1.0, None, ALU.mult))
                    TT(dte, dtx, dtm, ALU.min).then_inc(s["dtx"], 1)
                if st == 28:
                    dve.wait_ge(s["dtx"], 1)
                    q(TS(dtm, dtx, 0.0, None, ALU.max))
                    dve.wait_ge(s["sp_e"], 2)
                    q(TT(dt_, dtm, dtl, ALU.add))
                    STT(out=dtA, in0=dt_, scalar=-1.0, in1=anegb.unsqueeze(1).to_broadcast([P, NC, HEADS]),
                        op0=ALU.mult, op1=ALU.mult).then_inc(s["dt_ready"], 1)
                if st == 29:
                    got(dve, "cs")
                    for dst, c0 in ((csk, 0), (tot, 48)):
                        dve.tensor_copy(dst[:, 0:2], bank("cs")[:, c0:c0 + 32].rearrange("p (c n) -> p c n", c=2))
                        ins = dve.tensor_copy(dst[0:NS, 2], bank("cs")[0:NS, c0 + 32:c0 + 48])
                    emptied(ins, "cs")
                    done(dve, "cs")
                    TT(dtl, tot, csk, ALU.subtract).then_inc(s["cs_in"], 1)
            y5_read(KT - 1)

            dve.wait_ge(s["wdec"], 1)
            q(TT(wend, wend, dt_, ALU.mult))
            dve.wait_ge(s["s5rot"], NST)
            dve.wait_ge(s["sl"], NST)
            for c in range(NC):
                R = ROWS[c]
                for i in range(2):
                    job = f"tr{c}{i}"
                    got(dve, job)
                    src = bank(job)[0:R, :].rearrange("p (n d) -> p n d", n=8)
                    cols, hs = slice(512 * i, 512 * i + 512), slice(8 * i, 8 * i + 8)
                    TT(xdt[0:R, c, cols].rearrange("p (n d) -> p n d", n=8), src,
                       dt_[0:R, c, hs].unsqueeze(2).to_broadcast([R, 8, HD]), ALU.mult)
                    emptied(TT(wx[0:R, c, cols].rearrange("p (n d) -> p n d", n=8), src,
                               wend[0:R, c, hs].unsqueeze(2).to_broadcast([R, 8, HD]), ALU.mult), job)
            done(dve, "tb2")
            for g in range(2):
                ins = TT(bblk[0:NS, g], btok[0:NS, 2, g].unsqueeze(1).to_broadcast([NS, NB, P]),
                         same_s[:, :, 0:1].to_broadcast([NS, NB, P]), ALU.mult)
            ins.then_inc(s["bblk"], 1)
            done(dve, "cb2")
            done(dve, "ecp1")
            done(dve, "s01")
            dve.wait_ge(s["out_k"], 16)
            dve.wait_ge(s["out_s5"], 96)
            dve.wait_ge(s["etot"], 1)

            def gaps(i):
                for c in range(NC):
                    R, job, d_ = ROWS[c], f"csb{i}{c}", dm[i % 2][c][0:ROWS[c]]
                    got(dve, job)
                    if i >= 2:
                        got(dve, f"yi{2 * i - 3}")
                    emptied(TT(d_, bank(job)[0:R, :].rearrange("p (n l) -> p n l", n=4)[:, :, 0:R],
                               csk[0:R, c, 4 * i:4 * i + 4].unsqueeze(2).to_broadcast([R, 4, R]), ALU.subtract), job)
                    done(dve, job)
                    mask = neg[:, :] if c < 2 else neg_s[:, :, :].rearrange("p b l -> p (b l)")
                    TT(d_, d_, mask.unsqueeze(1).to_broadcast([R, 4, R]), ALU.add).then_inc(s["csd"], 1)

            gaps(0)
            for i in range(4):
                g = i // 2
                for c in range(NC):
                    R, d_ = ROWS[c], dm[i % 2][c][0:ROWS[c]]
                    dve.wait_ge(s["csm"], 3 * i + c + 1)
                    TT(d_, d_, cbT[0:R, c, g, 0:R].unsqueeze(1).to_broadcast([R, 4, R]), ALU.mult).then_inc(s["mt"], 1)
                if i < 3:
                    gaps(i + 1)
                for t in (2 * i, 2 * i + 1):
                    hb = hbuf[t % 4]
                    got(dve, f"h0{t}b")
                    q(TT(hb, hb, ecs[:, t, P:192].rearrange("p (b l) -> p b l", b=NB)[:, :, LS - 1:LS].to_broadcast([P, NB, P]),
                         ALU.mult))
                    got(dve, f"yi{t}")
                    emptied(STT(out=y[:, t], in0=xcT[:, t], scalar=lam[:, 96 + t:97 + t], in1=bank(f"yi{t}")[:, 0:T],
                                op0=ALU.mult, op1=ALU.add), f"yi{t}")
                    got(dve, f"yx{t}")
                    emptied(TT(ytmp, ecs[:, t], bank(f"yx{t}")[:, 0:192], ALU.mult), f"yx{t}")
                    done(dve, f"yx{t}")
                    q(TT(y[:, t, P:T], y[:, t, P:T], ytmp, ALU.add))
                    for hf, k in (("a", 0), ("b", 4)):
                        job = f"ns{t}{hf}"
                        got(dve, job)
                        emptied(TT(hb[:, k:k + 4], hb[:, k:k + 4], bank(job)[:, :].rearrange("p (b n) -> p b n", b=4),
                                   ALU.add), job)
            dve.wait_ge(s["out_st0"], 32)
            for g in range(2):
                cols = slice(512 * g, 512 * g + 512)
                q(TT(hl[:, cols].rearrange("p (n d) -> p n d", n=8), s0T[:, cols].rearrange("p (n d) -> p n d", n=8),
                     etot[:, 1, 8 * g:8 * g + 8].unsqueeze(2).to_broadcast([P, 8, HD]), ALU.mult))
                got(dve, f"s1{g}")
                emptied(TT(hl[:, cols], hl[:, cols], bank(f"s1{g}")[:, :], ALU.add), f"s1{g}")
            def split_unit(u):
                if u < UNITS:
                    dve.wait_ge(s["whi"], u + 1)
                    TT(ulo[u % 2], unit_raw(u), uhi[u % 2].bitcast(F32), ALU.subtract).then_inc(s["wlo"], 1)

            def low(part, high, whole, v, count):
                dve.wait_ge(s[part + "_hi"], count)
                TT(v(high[1]), v(whole), v(high[0]).bitcast(F32), ALU.subtract).then_inc(s[part + "_lo"], 1)

            split_unit(0)
            low("hn", (hn_hi, hn_lo), hnT, lambda x: x, 1)
            for m in range(KT):
                if m % 2 == 0:
                    split_unit(unit_of("z0") + m // 2 + 1)
                done(dve, f"z{m}")
                TT(y[:, m], y[:, m], zs[m % 2], ALU.mult).then_inc(s["y_done"], 1)
            got(dve, "ssy")
            emptied(TS(yv, bank("ssy")[:, 0:T], 1.0 / D, EPS, ALU.mult, ALU.add), "ssy")
            dve.wait_ge(s["yr"], 1)
            q(TT(yr1, yr0, yr0, ALU.mult))
            q(TT(yr1, yr1, yv, ALU.mult))
            q(TS(yr1, yr1, -0.5, 1.5, ALU.mult, ALU.add))
            q(TT(rb, yr0, yr1, ALU.mult))
            for m in range(KT):
                STT(out=y[:, m], in0=y[:, m], scalar=vec[:, V_SSD + m:V_SSD + m + 1], in1=rb, op0=ALU.mult, op1=ALU.mult)\
                    .then_inc(s["yn"], 1)
            split_unit(unit_of("ga0", 1))
            for m in range(KT):
                low("yb", (yb_hi, yb_lo), y, lambda x: x[:, m], m + 1)
            for i in range(1, 4):
                split_unit(unit_of("ga0") + i + 1)
            for m in range(KT):
                if m % 2 == 0:
                    split_unit(unit_of("sb0") + m // 2 + 1)
                got(dve, f"sb{m}")
                done(dve, f"ga{m}")
                emptied(STT(out=mrg[:, m], in0=mrg[:, m], scalar=1.0, in1=bank(f"sb{m}")[:, 0:T], op0=ALU.add, op1=ALU.mult),
                        f"sb{m}")
            done(dve, "sb7")
            split_unit(unit_of("gb0", 1))
            split_unit(unit_of("gb1", 0))
            low("u5", (u5_hi, u5_lo), u5T, lambda x: x, 1)
            split_unit(unit_of("gb1", 1))
            split_unit(unit_of("gv0", 0))
            for m in range(KT):
                if m % 4 == 0:
                    for i in range(2):
                        split_unit(unit_of(f"gv{m // 4}") + i + 1)
                if m % 2 == 0:
                    split_unit(unit_of(f"gg{m // 4}") + m % 4 // 2 + 1)
                v = val[:, m % 4]
                done(dve, f"gg{m}")
                q(STT(out=v, in0=th[m % 2], scalar=1.0, in1=v, op0=ALU.add, op1=ALU.mult))
                q(STT(out=v, in0=thB[:, m], scalar=1.0, in1=v, op0=ALU.add, op1=ALU.mult))
                STT(out=mrg[:, m], in0=v, scalar=0.5, in1=mrg[:, m], op0=ALU.mult, op1=ALU.add).then_inc(s["glu_used"], 1)
                if m:
                    low("mrg", (mrg_hi, mrg_lo), mrg, lambda x: x[:, m - 1], m)
            low("mrg", (mrg_hi, mrg_lo), mrg, lambda x: x[:, KT - 1], KT)
            dve.wait_ge(s["ld_h"], 32)
            for i in range(4):
                split_unit(unit_of("mx0") + i + 1)
                for c in range(NC):
                    R, job = ROWS[c], f"mx{i}{c}"
                    got(dve, job)
                    v = h[0:R, c, 256 * i:256 * (i + 1)]
                    emptied(STT(out=v, in0=bank(job)[0:R, 0:256], scalar=0.5, in1=v, op0=ALU.mult, op1=ALU.add), job)

            def norm(kind, use, gain, dst):
                dve.wait_ge(s["ss"], 5 + 3 * use)
                root(use, 3)
                for c in range(NC):
                    R = ROWS[c]
                    if kind == "hq" and c:
                        got(dve, f"hq{c - 1}1")
                    TS((hn if kind == "hq" else tn[:, c])[0:R], h[0:R, c], rs[0:R, c:c + 1], None, ALU.mult).then_inc(s["hn2"], 1)
                    for hf in range(2):
                        job = f"{kind}{c}{hf}"
                        got(dve, job)
                        emptied(TT(dst[:, 4 * hf:4 * hf + 4, P * c:P * c + R],
                                   bank(job)[:, :].rearrange("p (k l) -> p k l", k=4)[:, :, 0:R],
                                   vec[:, gain + 4 * hf:gain + 4 * hf + 4].unsqueeze(2).to_broadcast([P, 4, R]), ALU.mult), job)

            norm("hq", 1, V_Q, hn2T)
            for c in range(NC):
                for hf in range(2):
                    low("q", (q_hi, q_lo), hn2T, lambda x: x[:, 4 * hf:4 * hf + 4, P * c:P * c + ROWS[c]], 2 * c + hf + 1)
            for i in range(4):
                split_unit(unit_of("q0") + i + 1)
            split_unit(unit_of("o0", 1))

            def minus_max(k, src):
                q(dve.reduce_max(att[:, k % 2, 3:4], src[:, 0:MEM], AX.X))
                TS(att[:, k % 2, 0:1], att[:, k % 2, 3:4], -1.0, None, ALU.mult).then_inc(s["nmax"], 1)

            def inverse(k):
                dve.wait_ge(s["pexp"], k + 1)
                q(dve.reciprocal(att[:, k % 2, 2:3], att[:, k % 2, 1:2]))
                return att[:, k % 2, 2:3]

            def head_out(k):
                c, hd = divmod(k, MH)
                got(dve, f"ao{c}{hd}")
                emptied(dve.tensor_copy(aoT[:, 2 * hd:2 * hd + 2, P * c:P * (c + 1)],
                                        bank(f"ao{c}{hd}")[:, 0:256].rearrange("p (k l) -> p k l", k=2)), f"ao{c}{hd}")

            dve.memset(psum[6][:, :], 0.0)
            dve.memset(psum[7][:, :], 0.0).then_inc(s["zeroed"], 1)
            got(dve, "sc00")
            minus_max(0, bank("sc00"))
            for k in range(2 * MH):
                c, hd = divmod(k, MH)
                if k < 7:
                    job = "sc%d%d" % divmod(k + 1, MH)
                    got(dve, job)
                    minus_max(k + 1, bank(job))
                inv = inverse(k)
                emptied(TS(pr[k % 2], pr[k % 2], inv, None, ALU.mult), f"sc{c}{hd}")
                if k:
                    head_out(k - 1)
            head_out(7)

            def keys(b):
                for i in range(2):
                    job = f"kt{b}{2 * i + 1}"
                    got(dve, job)
                    if b >= 2 and i == 0:
                        dve.wait_ge(s["sb_full"], b - 1)
                    emptied(dve.tensor_copy(kbT[b % 2][:, 4 * i + 2:4 * i + 4].rearrange("p k m -> p (k m)"),
                                            bank(job)[:, :]), job)

            def sample_out(b):
                got(dve, f"ot{b}")
                emptied(dve.tensor_copy(
                    aoT[:, :, NP + LS * b:NP + LS * (b + 1)].rearrange("p (h k) l -> p k h l", k=2),
                    bank(f"ot{b}")[:, 0:256].rearrange("p (k h l) -> p k h l", k=2, h=MH)[:, :, :, 0:LS]), f"ot{b}")

            keys(0)
            dve.wait_ge(s["sb_full"], 1)
            minus_max(8, psum[6])
            for b in range(NB):
                if b < NB - 1:
                    keys(b + 1)
                if b:
                    sample_out(b - 1)
                inv = inverse(8 + b)
                if b < NB - 1:
                    dve.wait_ge(s["sb_full"], b + 2)
                    minus_max(8 + b + 1, psum[6])
                dve.wait_ge(s["ob_full"], b + 1)
                TS(oS, psum[7][:, 0:MD], inv, None, ALU.mult).then_inc(s["osb"], 1)
                if b == 2:
                    low("ao", (ao_hi, ao_lo), aoT, lambda x: x[:, :, 0:NP], 1)
            sample_out(NB - 1)
            low("ao", (ao_hi, ao_lo), aoT, lambda x: x[:, :, NP:T], 2)
            for i in range(4):
                if i:
                    split_unit(unit_of("o0") + i + 1)
                for c in range(NC):
                    R, job = ROWS[c], f"o{i}{c}"
                    got(dve, job)
                    v = h[0:R, c, 256 * i:256 * (i + 1)]
                    emptied(TT(v, v, bank(job)[0:R, 0:256], ALU.add), job)
            norm("ft", 2, V_FFN, tT)

            q(dve.memset(rtl, 0.0))
            got(dve, "lg")
            TT(rtl[:, 0:2], bank("lg")[:, 0:72].rearrange("p (c n) -> p c n", c=2),
               rbias[:, :].unsqueeze(1).to_broadcast([P, 2, 36]), ALU.add)
            emptied(TT(rtl[0:NS, 2], bank("lg")[0:NS, 72:108], rbias[0:NS, :], ALU.add), "lg")
            done(dve, "lg")

            def top(i):
                return rt[:, i, :, 0:1]

            def wide(v, k):
                return v.to_broadcast([P, NC, k])

            def first_max(src, k, mx, out):
                q(dve.tensor_reduce(top(mx), src, AX.X, ALU.max))
                q(TT(rt[:, 3, :, 0:k], src, wide(top(mx), k), ALU.is_equal))
                q(STT(out=rt[:, 5, :, 0:k], in0=rt[:, 3, :, 0:k], scalar=-99.0,
                      in1=iota[:, 0:k].unsqueeze(1).to_broadcast([P, NC, k]), op0=ALU.mult, op1=ALU.add))
                q(dve.tensor_reduce(top(6), rt[:, 5, :, 0:k], AX.X, ALU.min))
                return TT(rt[:, out, :, 0:k], rt[:, 5, :, 0:k], wide(top(6), k), ALU.is_equal)

            lgG, lgE = rtl[:, :, 0:NG], rtl[:, :, NG:]
            first_max(lgG, NG, 0, 4).then_inc(s["rt_oh"], 1)
            dve.wait_ge(s["rt_oh"], 1)
            oh = rt[:, 4, :, 0:NG]
            TT(rt[:, 1, :, 0:NG], lgG, wide(top(0), NG), ALU.subtract).then_inc(s["rt_a"], 1)
            q(TT(rte.rearrange("p c (g e) -> p c g e", g=NG), lgE.rearrange("p c (g e) -> p c g e", g=NG),
                 oh.unsqueeze(3).to_broadcast([P, NC, NG, NE]), ALU.mult))
            q(dve.tensor_reduce(rt[:, 8], rte.rearrange("p c (g e) -> p c e g", g=NG), AX.X, ALU.add))
            q(first_max(rt[:, 8], NE, 9, 10))
            q(STT(out=rt[:, 13], in0=rt[:, 10], scalar=-1e30, in1=rt[:, 8], op0=ALU.mult, op1=ALU.add))
            q(first_max(rt[:, 13], NE, 14, 15))
            TT(top(11), top(14), top(9), ALU.subtract).then_inc(s["rt_a"], 1)
            dve.wait_ge(s["rt_e"], 1)
            q(dve.tensor_reduce(top(7), rt[:, 2, :, 0:NG], AX.X, ALU.add))
            q(dve.reciprocal(top(7), top(7)))
            dve.wait_ge(s["rt_e"], 2)
            q(TS(top(16), top(12), 1.0, None, ALU.add))
            q(dve.reciprocal(top(16), top(16)))
            q(TT(top(16), top(16), top(7), ALU.mult))
            q(TT(top(17), top(16), top(12), ALU.mult))
            q(TT(comb[:, :, :], rt[:, 10], wide(top(16), NE), ALU.mult))
            q(TT(rt[:, 18], rt[:, 15], wide(top(17), NE), ALU.mult))
            q(TT(comb[:, :, :], comb[:, :, :], rt[:, 18], ALU.add))
            got(dve, "rk")
            STT(out=rg[:, 0:2, :], in0=bank("rk")[:, 0:8].rearrange("p (c g) -> p c g", c=2), scalar=1.0, in1=oh[:, 0:2],
                op0=ALU.add, op1=ALU.mult)
            STT(out=rg[0:NS, 2, :], in0=bank("rk")[0:NS, 8:12], scalar=1.0, in1=oh[0:NS, 2], op0=ALU.add, op1=ALU.mult)
            emptied(dve.reduce_max(rt[:, 19, 0, 0:1], bank("rk")[:, 16:16 + NG], AX.X), "rk")
            done(dve, "rk")
            q(TS(rg[:, :, :], rg[:, :, :], 1.0, None, ALU.subtract))
            q(TS(rt[:, 20, 0, 0:1], rt[:, 19, 0, 0:1], float(P), 1.0, ALU.is_gt, ALU.add))
            q(TS(rt[:, 21, 0, 0:1], rt[:, 19, 0, 0:1], float(2 * P), None, ALU.is_gt))
            TT(np_i[:, :], rt[:, 20, 0, 0:1], rt[:, 21, 0, 0:1], ALU.add).then_inc(s["npass"], 1)

            npass = load_passes(dve)
            with dve.Fori(0, npass) as rr:
                for c in range(NC):
                    for g in range(NG):
                        ins = TS(pg[:, c, P * g:P * (g + 1)], iota[:, :], rg[:, c, g:g + 1], None, ALU.is_equal)
                ins.then_inc(s["pg"], 1)
                with dve.Fori(0, NG) as g:
                    grp = rr * NG + g
                    base = grp * GCH
                    dve.wait_ge(s["gx_free"], rr * 13 + 13)
                    dve.wait_ge(s["xhi"], grp + 1)
                    TT(xlo, xg[:, bass.ds(g, 1)].rearrange("p g k l -> p (g k) l"), xhi.bitcast(F32), ALU.subtract).then_inc(
                        s["xlo"], 1)
                    for two in range(NE // 2):
                        b2, e2 = base + two * NCH, grp * NE + 2 * two

                        def hidden(x):
                            dve.wait_ge(s["chunk_done"], b2 + (4, 8)[x] + CD0)
                            dve.wait_ge(s["sil"], e2 + x + 1)
                            STT(out=hh[x], in0=sil[x], scalar=cg[:, bass.ds(g * NE + 2 * two + x, 1)], in1=psum[2 + x][:, :],
                                op0=ALU.mult, op1=ALU.mult).then_inc(s["hh"], 1)

                        def ht(x):
                            dve.wait_ge(s["hthi"], e2 + x + 2)
                            TT(htlo[x].rearrange("p j n -> p (j n)"), psum[4][:, :],
                               hthi[x].rearrange("p j n -> p (j n)").bitcast(F32), ALU.subtract).then_inc(s["htlo"], 1)

                        for pos in range(NCH):
                            if pos == 7:
                                hidden(0)
                            if pos == 11:
                                hidden(1)
                            dve.wait_ge(s["hi"], b2 + pos + 1)
                            TT(wlo[pos % PAIR], raw[pos % RAW], whi[pos % PAIR].bitcast(F32), ALU.subtract).then_inc(s["lo"], 1)
                            if two == 0 and pos == 3:
                                dve.wait_ge(s["chunk_done"], base + CD0)
                                for i in range(2):
                                    ins = dve.tensor_copy(yall[:, bass.ds(g, 1), BLK * i:BLK * (i + 1)],
                                                          psum[6 + i][:, :].unsqueeze(1))
                                ins.then_inc(s["y_free"], 1)
                            if pos == 9:
                                ht(0)
                            if pos == 11:
                                ht(1)
                dve.wait_ge(s["chunk_done"], rr * (NG * GCH) + (NG * GCH + CD0))
                for i in range(2):
                    ins = dve.tensor_copy(yall[:, NG, BLK * i:BLK * (i + 1)], psum[6 + i][:, :])
                ins.then_inc(s["fin_y"], 1)
                for i in range(2):
                    for c in range(NC):
                        R, k = ROWS[c], 3 * i + c
                        dve.wait_ge(s["sc_full"], rr * 6 + k + 1)
                        v = h[0:R, c, BLK * i:BLK * (i + 1)]
                        TT(v, v, psum[k % 2][0:R, :], ALU.add).then_inc(s["sc_free"], 1)
                TS(rg[:, :, :], rg[:, :, :], float(P), None, ALU.subtract).then_inc(s["rgdec"], 1)
                dve.wait_ge(s["rgdec"], rr + 1)
            q(TS(rs1[:, 0:1], rs[:, 0:1], 1.0, None, ALU.mult))
            TS(rs1[:, 0:1], rs[:, 0:1], 1.0, None, ALU.mult).then_inc(s["fin"], 1)

            dve.wait_ge(s["ss"], 14)
            root(3, 3)
            dve.wait_ge(s["ld_fin"], 16)
            for c in range(NC):
                R = ROWS[c]
                if c >= 2:
                    dve.wait_ge(s["out_y0"], 16)
                q(TS(fy[c % 2][0:R], h[0:R, c], rs[0:R, c:c + 1], None, ALU.mult))
                TT(fy[c % 2][0:R], fy[c % 2][0:R], gfin[0:R], ALU.mult).then_inc(s["fy"], 1)


_INS = [
    'x_prompt', 'x_sample', 'state_conv', 'state_ssd', 'state_s5_re', 'state_s5_im', 'cache_mem_k', 'cache_mem_v',
    'mem_prompt', 'norm_mix_g', 'w_in', 'conv_w', 'conv_b', 'ssd_dt_bias', 'ssd_a_log', 'ssd_d', 'ssd_norm_g',
    'w_ssd_branch', 's5_lambda_re', 's5_lambda_im', 's5_log_step', 's5_b_re', 's5_b_im', 's5_c_re', 's5_c_im', 's5_d',
    'w_glu', 'b_glu', 'w_mix_out', 'norm_mem_q_g', 'norm_mem_kv_g', 'w_mem_q', 'w_mem_k', 'w_mem_v', 'w_mem_o',
    'norm_ffn_g', 'w_router_group', 'b_router_group', 'w_router_expert', 'b_router_expert', 'w_exp_gate', 'w_exp_up',
    'w_exp_down', 'norm_final_g',
]
_OUTS = [
    ("yp", (1, NP, D)), ("ys", (NB, LS, D)), ("cvp", (1, 1, 3, CD)), ("ssdp", (1, 1, HEADS, HD, STATE)),
    ("rep", (1, 1, S5G, S5N)), ("imp", (1, 1, S5G, S5N)), ("mk", (1, 1, MEM, MH, MD)), ("mv", (1, 1, MEM, MH, MD)),
    ("cvs", (1, NB, 3, CD)), ("ssds", (1, NB, HEADS, HD, STATE)), ("res", (1, NB, S5G, S5N)), ("ims", (1, NB, S5G, S5N)),
]


def kernel(**inputs):
    import numpy as _np
    import concourse.bacc as _bacc
    from concourse import mybir as _mybir
    from concourse.bass_utils import run_bass_kernel_spmd as _run

    nc = _bacc.Bacc("TRN2", target_bir_lowering=False, num_devices=1)
    arrays, a, o = {}, {}, {}
    for name in _INS:
        x = _np.ascontiguousarray(inputs[name])
        arrays[f"in_{name}_dram"] = x
        a[name] = nc.dram_tensor(f"in_{name}_dram", x.shape, _mybir.dt.from_np(x.dtype), kind="ExternalInput").ap()
    for name, shape in _OUTS:
        o[name] = nc.dram_tensor(f"out_{name}_dram", shape, _mybir.dt.float32, kind="ExternalOutput").ap()
    layer(nc, a, o)
    r = _run(nc, [arrays], core_ids=[0])
    return tuple(r.results[0][f"out_{name}_dram"] for name, _ in _OUTS)
```

```python
from contextlib import ExitStack

import concourse.bass as bass
from concourse import mybir

F32 = mybir.dt.float32
F32R = mybir.dt.float32r
I32 = mybir.dt.int32
ACT = mybir.ActivationFunctionType
ALU = mybir.AluOpType
AX = mybir.AxisListType

P = 128
D = 1024
KT = D // P
NP, NS = 256, 64
T = NP + NS
NB, LS = 8, 8
ROWS = (128, 128, 64)
NC = 3
CD = 1536
CT = CD // P
HEADS, HD = 16, 64
STATE = 128
S5G, S5K, S5N = 64, 16, 64
NST = S5G * S5N // P
MEM, MH, MD = 256, 4, 256
NG, NE, TOPF = 4, 8, 512
EPS = 1e-6
TWO_PI = 6.283185307179586
PI = 3.1415925
BLK = 512
CH = 2048
RAW = 6
PAIR = 4
CHUNKS = [(x, part, half) for x, part in ((0, 0), (0, 1), (1, 0), (1, 1), (0, 2), (1, 2)) for half in range(2)]
NCH = len(CHUNKS)
GCH = NCH * NE // 2
AHEAD = PAIR
CD0, LO0 = 8, RAW
RING = 6
STAT_SLOTS = 3
COL = {"z": 0, "xbc": D, "dt": D + CD, "u5": D + CD + HEADS, "ga": D + CD + HEADS + D, "gb": D + CD + HEADS + 2 * D}

V_MIX, V_SSD, V_Q, V_KV, V_FFN, V_D5, V_GLU, V_CW, V_CB = 0, 8, 16, 24, 32, 40, 48, 64, 112

BLOCKS = (
    [(f"u5{i}", "w_in", COL["u5"] + BLK * i) for i in range(2)]
    + [(f"xbc{i}", "w_in", COL["xbc"] + BLK * i) for i in range(3)]
    + [(f"mk{i}", "w_mem_k", BLK * i) for i in range(2)]
    + [(f"mv{i}", "w_mem_v", BLK * i) for i in range(2)]
    + [("z0", "w_in", COL["z"])]
    + [("zout", None, 0)]
    + [("z1", "w_in", COL["z"] + BLK)]
    + [(f"ga{i}", "w_in", COL["ga"] + BLK * i) for i in range(2)]
    + [(f"sb{i}", "w_ssd_branch", BLK * i) for i in range(2)]
    + [(f"gb{i}", "w_in", COL["gb"] + BLK * i) for i in range(2)]
    + [("gv0", "w_glu", 0), ("gg0", "w_glu", D), ("gv1", "w_glu", BLK), ("gg1", "w_glu", D + BLK)]
    + [(f"mx{i}", "w_mix_out", BLK * i) for i in range(2)]
    + [(f"q{i}", "w_mem_q", BLK * i) for i in range(2)]
    + [(f"o{i}", "w_mem_o", BLK * i) for i in range(2)]
)
BIDX = {b[0]: n for n, b in enumerate(BLOCKS)}
SPLIT0 = BIDX["z1"]
UNITS = 2 * (len(BLOCKS) - SPLIT0)
UNIT_LAST = []
for _name, _, _ in BLOCKS[SPLIT0:]:
    _kind, _i = _name[:-1], int(_name[-1])
    UNIT_LAST += [f"{_kind}{2 * _i + _h}2" if _kind in ("mx", "o") else f"{_kind}{4 * _i + 2 * _h + 1}" for _h in range(2)]

FILL = (
    [("xbc", m) for m in range(CT)]
    + [("mk", m) for m in range(KT)]
    + [("mv", 2 * n + c) for n in range(2) for c in range(2)]
)


LATE = {24: ["ko00", "ko01"], 25: ["ko10", "ko11"], 26: ["dtT"], 27: ["dt3"], 29: ["cs"]}


def plan():
    j = ["par"]
    j += [f"x{c}{h}" for c in range(NC) for h in range(2)]
    j += [f"u5{m}" for m in range(KT)]
    j += ["s5h", "cvs"]
    j += [f"bt{q}" for q in range(4)] + [f"ct{q}" for q in range(4)]
    j += [f"m{c}{h}" for c in range(2) for h in range(2)]
    for st in range(NST):
        j += [f"bu{st}r", f"bu{st}i"]
        if st < len(FILL):
            j.append(f"{FILL[st][0]}{FILL[st][1]}")
        j += LATE.get(st, [])
    j += ["z0", "s5o0", "s5o1", "z1"] + [f"nc{q}" for q in range(3)]
    j += ["ecs"] + [f"ecp{q}" for q in range(2)]
    j.append("z2")
    for c in range(NC):
        j += [f"tr{c}0", f"tr{c}1", f"tb{c}", f"cb{c}"]
    j.append("z3")
    j += ["s00", "s01"]
    j += [f"csb0{c}" for c in range(NC)] + ["h00a", "h00b"]
    for q in range(4):
        if q < 3:
            j += [f"csb{q + 1}{c}" for c in range(NC)]
        for t in (2 * q, 2 * q + 1):
            j.append(f"yi{t}")
            if t < KT - 1:
                j += [f"h0{t + 1}a", f"h0{t + 1}b"]
            j += [f"yx{t}", f"ns{t}a", f"ns{t}b"]
    j += ["s10", "s11", "hl0", "hl1"]
    j += [f"z{m}" for m in range(4, KT)]
    j += [f"ga{m}" for m in range(4)] + ["ssy"]
    j += [f"ga{m}" for m in range(4, KT)] + [f"sb{m}" for m in range(KT)] + [f"gb{m}" for m in range(KT)]
    for h in range(2):
        j += [f"gv{m}" for m in range(4 * h, 4 * h + 4)] + [f"gg{m}" for m in range(4 * h, 4 * h + 4)]
    j += [f"mx{u}{c}" for u in range(4) for c in range(NC)]
    j += [f"hq{c}{h}" for c in range(NC) for h in range(2)]
    j += [f"q{m}" for m in range(KT)]
    j += ["sc00", "sc01"]
    for k in range(2 * MH):
        j.append("pt%d%d" % divmod(k, MH))
        if k + 2 < 2 * MH:
            j.append("sc%d%d" % divmod(k + 2, MH))
        j.append("ao%d%d" % divmod(k, MH))
    j += [f"kt0{i}" for i in range(4)]
    for b in range(NB):
        if b < NB - 1:
            j += [f"kt{b + 1}{i}" for i in range(4)]
        if b:
            j.append(f"ot{b - 1}")
        j.append(f"sp{b}")
    j.append(f"ot{NB - 1}")
    j += [f"o{u}{c}" for u in range(4) for c in range(NC)]
    j += [f"ft{c}{h}" for c in range(NC) for h in range(2)]
    j += ["lg", "rk"]
    return j


PLAN = plan()
RB = 6
BANK = {job: (n % RB, n // RB) for n, job in enumerate(PLAN)}
assert len(BANK) == len(PLAN)
LAST = {f"{kind}{i}": f"{kind}{4 * i + 3}" for kind, n in (("u5", 2), ("xbc", 3), ("mk", 2), ("z", 1)) for i in range(n)}
LAST.update({f"mv{i}": f"mv{2 * i + 1}" for i in range(2)})

SEMS = (
    "ld_par ld_x ld_mem ld_small ld_s5 ld_st0 ld_st1 ld_st2 ld_st3 ld_k0 ld_k1 ld_v0 ld_v1 ld_h ld_fin "
    "dve act pool consts rows ss var rs0 xn s5w s5c s5par bx cx inj "
    "tab_half tab_ready tab_used scan s5rot sl y5_full y5_free convout xc "
    "zs dtx sp_e dt_ready cs_in wdec etot bblk csd csm mt y_done ysq yr yn glu_used "
    "whi wlo hn_hi hn_lo yb_hi yb_lo u5_hi u5_lo mrg_hi mrg_lo q_hi q_lo ao_hi ao_lo hn2 nmax pexp sb_full ob_full osb zeroed rt_a rt_e rt_oh npass "
    "y_half loads pg gx_full gx_free xhi chunk_done hi lo sil hh t_full hthi htlo y_free sc_full sc_free rgdec fin fy "
    "out_v out_k out_s5 out_cv out_st0 out_st1 out_st2 out_st3 out_hl out_y0 out_y1 out_y2"
).split()


def layer(nc, a, o):
    ctx = ExitStack()
    with ctx:
        def sb(name, shape, dt=F32):
            return ctx.enter_context(nc.sbuf_tensor(name, shape, dt))

        def sem(name):
            return ctx.enter_context(nc.semaphore(name))

        ring_at = (nc.sbuf_base + 31) // 32 * 32
        ring = sb("ring", [P, RING * 4096])
        work_at = (nc.sbuf_base + 31) // 32 * 32
        work = sb("work", [P, 23820])

        def rounded(name, at, cols):
            return nc.alloc_sbuf_tensor_at(name, [P, cols], F32R, offset=at)

        usplit = rounded("usplit", ring_at + 4 * STAT_SLOTS * 4096, 4 * CH)
        ops = {at: rounded(f"ops{at}", work_at + 4 * at, KT * T) for at in (0, 2560, 9216, 13056, 15360, 15616, 18176)}
        wsplit = rounded("wsplit", ring_at, PAIR * 2 * CH)
        xsplit = rounded("xsplit", work_at + 4 * 9984, 2 * D)
        hsplit = rounded("hsplit", work_at + 4 * 14080, 4 * TOPF)
        slots = [ring[:, 4096 * i:4096 * (i + 1)] for i in range(RING)]

        def w(at, *dims):
            n = 1
            for d in dims:
                n *= d
            v = work[:, at:at + n]
            return view(v, dims)

        def r(at, *dims):
            n = 1
            for d in dims:
                n *= d
            at += STAT_SLOTS * 4096
            return view(ring[:, at:at + n], dims)

        def view(v, dims):
            names = "abcd"[:len(dims)]
            if len(dims) == 1:
                return v
            kw = {names[i]: dims[i] for i in range(len(dims) - 1)}
            return v.rearrange(f"p ({' '.join(names)}) -> p {' '.join(names)}", **kw)

        ident = sb("ident", [P, P])
        ones = sb("ones", [P, P])
        upto = sb("upto", [P, P])
        before = sb("before", [P, P])
        upto_s = sb("upto_s", [NS, NB, LS])
        same_s = sb("same_s", [NS, NB, LS])
        neg = sb("neg", [P, P])
        neg_s = sb("neg_s", [NS, NB, LS])
        iota = sb("iota", [P, P])
        half2 = sb("half2", [P, 2])
        sel16 = sb("sel16", [P, 4, 2])
        grp2 = sb("grp2", [P, 2])
        start = sb("start", [P, T])
        vec = sb("vec", [P, 124])
        lam = sb("lam", [P, 104])
        hglu = sb("hglu", [P, KT])
        e = sb("e", [P, 8, 2, NST])
        s5p = sb("s5p", [P, 16, NST])
        wdt = sb("wdt", [P, KT, HEADS])
        wr = sb("wr", [P, KT, NG + NG * NE])
        rbias = sb("rbias", [P, NG + NG * NE])
        dtb = sb("dtb", [P, HEADS])
        alog = sb("alog", [P, HEADS])
        cst = sb("cst", [P, CT, 3 * NB])
        last3 = sb("last3", [P, CT, 27])
        ss = sb("ss", [P, 5])
        var = sb("var", [P, 5])
        rs0 = sb("rs0", [P, 5])
        rs1 = sb("rs1", [P, 5])
        rs = sb("rs", [P, 5])
        rg = sb("rg", [P, NC, NG])
        comb = sb("comb", [P, NC, NE])
        np_i = sb("np_i", [P, 1], I32)
        cg = sb("cg", [P, NG * NE])

        psum = [ctx.enter_context(nc.psum_tensor(f"bank{i}", [P, 512], F32)) for i in range(8)]
        s = {n: sem(n) for n in SEMS}
        full = [sem(f"full{i}") for i in range(RB)]
        free = [sem(f"free{i}") for i in range(RB)]
        w_in_sem = [sem(f"w_slot{i}") for i in range(STAT_SLOTS)]
        raw_in = [sem(f"raw_in{i}") for i in range(RAW)]

        def bank(job):
            return psum[BANK[job][0]]

        def got(eng, job):
            b, turn = BANK[job]
            eng.wait_ge(full[b], turn + 1)

        def done(eng, job):
            b, turn = BANK[job]
            eng.wait_ge(free[b], turn + 1)

        def emptied(ins, job):
            ins.then_inc(free[BANK[job][0]], 1)

        def loads(n):
            return 16 * sum(b[1] is not None for b in BLOCKS[n % STAT_SLOTS:n + 1:STAT_SLOTS])

        def unit_raw(u):
            n = SPLIT0 + u // 2
            return slots[n % STAT_SLOTS].rearrange("p (k n) -> p k n", k=KT)[:, :, 256 * (u % 2):256 * (u % 2) + 256]

        def unit_of(name, half=0):
            return 2 * (BIDX[name] - SPLIT0) + half

        block = ctx.enter_context(nc.Block())

        xt = r(0, NC, D)
        hnT = w(0, KT, T)
        u5T = w(2560, KT, T)
        kT = w(5120, KT, MEM)
        vm = w(7168, 2, D)
        xn = [w(5120, D), w(6144, D)]
        st_nat = w(7168, 2, 2, P)
        cv_nat = w(7680, CD)
        memraw = w(9216, 2, D)
        junk = w(11264, D)
        lamrow = w(12288, 3, P)
        vecrow = w(12672, P)
        ddrow = w(12800, P)
        lsrow = w(12928, 2)
        dd8 = w(12930, 2)
        xcT = w(9216, CT, T)
        mnT = w(13056, KT, MEM)
        bnat = w(15104, 2, NST, S5K)
        bx = w(16128, 2, NST, 2, S5K)
        cnat = w(18176, 2, KT, S5N)
        cx = w(19200, 2, KT, 2, S5N)
        tmp512 = w(21248, 512)
        inj = w(22784, 2, NB, NST)
        h0s = w(21760, 2, NB, NST)
        tab = [r(2560 * i, 2, 4, T) for i in range(2)]
        bT = r(5120, KT, 2, P)
        cT = r(7168, KT, 2, P)
        tabtmp = r(9216, 2, 4, 16)
        tabtmp2 = w(16384, 2, 4, P)
        cvin = [r(10240 + 347 * i, 347) for i in range(2)]
        cvout = [r(10934 + 344 * i, 344) for i in range(2)]
        sl = r(11622, 2, 9 * NST)
        ub = [w(15104 + 640 * i, 2, T) for i in range(2)]
        m1 = w(16384, 2, T)
        m2 = w(17024, 2, T)
        wb = [w(17664 + 640 * i, 2, T) for i in range(2)]
        n1 = w(18944, 2, T)
        n2 = w(19584, 2, T)
        sbuf = [w(20224 + 640 * i, 2, T) for i in range(3)]
        rm = [w(22144 + 320 * i, T) for i in range(2)]
        kout = w(13056, 2, D)
        s5out = w(15104, 6, P)
        ncout = w(16128, CD)
        xdt = r(0, NC, D)
        wx = r(3072, NC, D)
        bblk = r(6144, 2, NB, P)
        hbuf = [r(8192, NB, P), r(10240, NB, P), w(15616, NB, P), w(16640, NB, P)]
        h0T = r(9216, NB, P)
        s0T = r(11264, D)
        hl = r(8192, D)
        hlo = r(10240, KT, P)
        y = w(13056, KT, T)
        ecs = w(17664, KT, 192)
        btok = w(19200, NC, 2, P)
        cbT = w(19968, NC, 2, P)
        dm = [[w(20736 + 1280 * i, 4, P), w(21248 + 1280 * i, 4, P), w(21760 + 1280 * i, 4, NS)] for i in range(2)]
        ytmp = w(23300, 192)
        dsm = sb("dsm", [P, 12, NC, HEADS])
        dtx, dte, dtl, dtm, dt_, dtA, csk, tot, wend, etot = (dsm[:, i] for i in range(10))
        anegb = dsm[:, 10, 0]
        dtS = r(10240, T)
        zT = view(slots[BIDX["zout"] % STAT_SLOTS][:, 0:KT * T], (KT, T))
        ysq = w(9216, KT, T)
        yv, yr0, yr1, rb = (w(21376 + 320 * i, T) for i in range(4))
        mrg = w(15616, KT, T)
        thB = w(9216, KT, T)
        val = w(11776, 4, T)
        th = [w(18176 + 320 * i, T) for i in range(2)]
        h = w(20736, NC, D)
        uhi = [usplit[:, 2 * CH * i:2 * CH * i + CH].rearrange("p (k n) -> p k n", k=KT) for i in range(2)]
        ulo = [usplit[:, 2 * CH * i + CH:2 * CH * (i + 1)].rearrange("p (k n) -> p k n", k=KT) for i in range(2)]

        def op(at):
            return view(ops[at][:, :], (KT, T))

        hn_hi, hn_lo = op(18176), op(0)
        yb_hi, yb_lo = op(9216), op(13056)
        u5_hi, u5_lo = op(13056), op(2560)
        mrg_hi, mrg_lo = op(0), op(15616)
        q_hi, q_lo = op(15360), op(0)
        ao_hi, ao_lo = op(0), op(15360)
        hn2 = [w(17920 + D * i, D) for i in range(2)]
        hn2T = w(0, KT, T)
        qT = w(2560, KT, T)
        kv = [w(9216, 2, 2, D), view(slots[5], (2, 2, D))]
        kbT = [w(13312, KT, MEM), w(5120, KT, MEM)]
        aoT = w(15360, KT, T)
        pr = [w(18944, MEM), w(17920, MEM)]
        pT = [w(19200, 2, P), w(18176, 2, P)]
        oS = w(19456, MEM)
        att = w(19712, 2, 4)
        tn = w(0, NC, D)
        tT = w(11008, KT, T)
        pg = w(3072, NC, P)
        pgT = w(3456, T)
        ysum = w(4608, D)
        tT = w(11008, KT, T)
        xhi, xlo = (view(xsplit[:, D * i:D * (i + 1)], (KT, P)) for i in range(2))
        sil = [w(12032 + 512 * i, TOPF) for i in range(2)]
        hh = [w(13056 + 512 * i, TOPF) for i in range(2)]
        hthi, htlo = ([view(hsplit[:, TOPF * (2 * j + i):TOPF * (2 * j + i + 1)], (4, P)) for i in range(2)]
                      for j in range(2))
        raw = [ring[:, at:at + CH] for at in (20480, 22528, 16384, 18432)]
        raw += [w(16128 + CH * i, CH) for i in range(2)]
        whi = [wsplit[:, 2 * CH * i:2 * CH * i + CH] for i in range(PAIR)]
        wlo = [wsplit[:, 2 * CH * i + CH:2 * CH * (i + 1)] for i in range(PAIR)]
        rt = w(18176, 24, NC, NE)
        rtl = w(18176 + 576, NC, NG + NG * NE)
        rte = w(18176 + 704, NC, NG * NE)
        gfin = w(0, D)
        fy = [w(1024 + 1024 * i, D) for i in range(2)]

        def wblock(name, c0):
            return a[name][0][:, c0:c0 + BLK].rearrange("(k p) n -> p k n", p=P)

        def blk(name):
            return slots[BIDX[name] % STAT_SLOTS].rearrange("p (k n) -> p k n", k=KT)

        def load_passes(eng):
            eng.wait_ge(s["npass"], 1)
            return eng.value_load(np_i[0:1, 0:1], min_val=1, max_val=NC)

        def squares(act, n0):
            for c in range(NC):
                R = ROWS[c]
                act.activation(hn2[0][0:R], h[0:R, c], ACT.Square, accum_out=ss[0:R, c:c + 1]).then_inc(s["ss"], 1)
                act.wait_ge(s["ss"], n0 + c + 1)

        def keep_last(act, st):
            act.wait_ge(s["s5rot"], st + 1)
            v = sl.rearrange("p r (q s) -> p r q s", q=9)
            act.activation(v[:, :, 0:1, st], sbuf[st % 3][:, :, NP - 1:NP], ACT.Copy)
            act.activation(v[:, :, 1:9, st], sbuf[st % 3][:, :, NP:T].rearrange("p r (b l) -> p r b l", b=NB)[:, :, :, LS - 1],
                           ACT.Copy).then_inc(s["sl"], 1)

        @block.sync
        def _(sp):
            sp.dma_start(xt[:, 0:2, :], a["x_prompt"][0].rearrange("(c p) d -> p c d", p=P)).then_inc(s["ld_x"], 16)
            sp.dma_start(xt[0:NS, 2, :], a["x_sample"].rearrange("b l d -> (b l) d")).then_inc(s["ld_x"], 16)

            sp.dma_start(memraw, a["mem_prompt"][0].rearrange("(c p) d -> p c d", p=P)).then_inc(s["ld_mem"], 16)

            def load_block(n):
                name, weight, c0 = BLOCKS[n]
                m = n - STAT_SLOTS
                if name == "zout":
                    return
                if m >= 0 and BLOCKS[m][0] == "zout":
                    sp.wait_ge(s["y_done"], KT)
                elif m >= SPLIT0:
                    sp.wait_ge(s["wlo"], 2 * (m - SPLIT0) + 2)
                elif m >= 0:
                    got(sp, LAST[BLOCKS[m][0]])
                sp.dma_start(slots[n % STAT_SLOTS].rearrange("p (k n) -> p k n", k=KT), wblock(weight, c0)).then_inc(
                    w_in_sem[n % STAT_SLOTS], 16)

            sp.wait_ge(s["ld_par"], 16 * 13)
            load_block(0)
            sp.wait_ge(s["ld_s5"], 16 * 7)
            for n in range(1, BIDX["z1"] + 1):
                load_block(n)
            sp.wait_ge(s["y5_full"], NST)
            done(sp, "s5o1")
            for t in range(KT):
                if t == 2:
                    sp.wait_ge(s["out_s5"], 96)
                    sp.wait_ge(s["out_cv"], 32)
                if t == 4:
                    load_block(BIDX["ga0"])
                if t >= 4:
                    sp.wait_ge(s[f"out_st{t % 4}"], 16 * (t // 4))
                sp.dma_start(hbuf[t % 4], a["state_ssd"][0].rearrange("b (t h) p n -> t (h p) b n", h=2)[t]).then_inc(
                    s[f"ld_st{t % 4}"], 16)
            for n in range(BIDX["ga1"], len(BLOCKS)):
                load_block(n)
                if BLOCKS[n][0] == "gb1":
                    sp.wait_ge(s["yn"], KT)
                    sp.dma_start(h[:, 0:2, :], a["x_prompt"][0].rearrange("(c p) d -> p c d", p=P)).then_inc(s["ld_h"], 16)
                    sp.dma_start(h[0:NS, 2, :], a["x_sample"].rearrange("b l d -> (b l) d")).then_inc(s["ld_h"], 16)
            sp.wait_ge(s["glu_used"], KT)
            sp.wait_ge(s["out_hl"], 16)
            for i in range(4):
                sp.wait_ge(s[f"out_st{i}"], 32)
            for b in range(NB):
                for i, (name, short) in enumerate((("cache_mem_k", "k"), ("cache_mem_v", "v"))):
                    if b >= 2:
                        if i == 0:
                            got(sp, f"kt{b - 2}3")
                        else:
                            sp.wait_ge(s["ob_full"], b - 1)
                    sp.dma_start(kv[b % 2][:, i], a[name][0, b].rearrange("(c p) h d -> p c (h d)", p=P)).then_inc(
                        s[f"ld_{short}{b % 2}"], 16)
            sp.wait_ge(s["ob_full"], NB)
            for name, v in (("chunk_done", CD0), ("lo", LO0), ("hh", 2), ("hthi", 1), ("htlo", 1), ("gx_free", 1),
                            ("sc_free", 1)):
                sp.sem_inc(s[name], v)

            def load_chunk(g, skip, two, pos):
                x, part, half = CHUNKS[pos]
                slot, ex = pos % RAW, 2 * two + x
                if part < 2:
                    src = a[("w_exp_gate", "w_exp_up")[part]][0, skip:][bass.ds(g, 1), ex, 512 * half:512 * (half + 1)]
                else:
                    src = a["w_exp_down"][0, skip:][bass.ds(g, 1), ex, 256 * half:256 * (half + 1)]
                sp.dma_start(raw[slot].rearrange("p (k n) -> p k n", k=4 if part < 2 else 2),
                             src.rearrange("g (k p) f -> p (g k) f", p=P)).then_inc(raw_in[slot], 16)

            def load_group(rr, g, after, skip):
                for m in range(AHEAD, AHEAD + GCH):
                    sp.wait_ge(s["lo"], (rr * NG + g) * GCH + m + 1)
                    sp.sem_inc(s["loads"], 1)
                    load_chunk(g if m < GCH else after, 0 if m < GCH else skip, m % GCH // NCH, m % NCH)

            for pos in range(AHEAD):
                if pos == 2:
                    got(sp, f"o3{NC - 1}")
                load_chunk(0, 0, 0, pos)
            npass = load_passes(sp)
            with sp.Fori(0, npass) as rr:
                with sp.Fori(0, NG - 1) as g:
                    load_group(rr, g, g, 1)
                load_group(rr, NG - 1, 0, 0)
            sp.wait_ge(s["fin"], 1)
            sp.dma_start(gfin, a["norm_final_g"].rearrange("(a d) -> a d", a=1).to_broadcast([P, D])).then_inc(s["ld_fin"], 16)

        @block.gpsimd
        def _(pool):
            n = [0]

            def q(ins):
                n[0] += 1
                ins.then_inc(s["pool"], 1)
                pool.wait_ge(s["pool"], n[0])

            def keep(v, pattern, base, cm, fill, op=ALU.is_ge):
                q(pool.affine_select(out=v, in_=v, compare_op=op, fill=fill, base=base, pattern=pattern,
                                     channel_multiplier=cm))

            for v, c in ((ident, 0.0), (ones, 1.0), (upto, 1.0), (before, 1.0), (neg, 0.0), (half2, 0.0), (start, 1.0)):
                pool.memset(v[:, :], c)
            for v, c in ((upto_s, 1.0), (same_s, 1.0), (neg_s, 0.0), (sel16, 1.0), (dsm, 0.0), (rg, 0.0)):
                pool.memset(v.rearrange("p a b -> p (a b)") if len(v.shape) == 3 else v[:, :, :, :], c)
            pool.memset(ss[:, :], 1.0)
            q(pool.iota(iota[:, :], pattern=[[1, P]], base=0, channel_multiplier=0, allow_small_or_imprecise_dtypes=True))
            keep(ident[:, :], [[-1, P]], 0, 1, 1.0, ALU.not_equal)
            keep(upto[:, :], [[1, P]], 0, -1, 0.0)
            keep(before[:, :], [[1, P]], -1, -1, 0.0)
            keep(neg[:, :], [[1, P]], 0, -1, -1e30)
            keep(upto_s[:, :, :], [[LS, NB], [1, LS]], 0, -1, 0.0)
            keep(upto_s[:, :, :], [[-LS, NB], [0, LS]], 0, 1, 0.0)
            keep(neg_s[:, :, :], [[LS, NB], [1, LS]], 0, -1, -1e30)
            keep(neg_s[:, :, :], [[-LS, NB], [0, LS]], 0, 1, -1e30)
            keep(same_s[:, :, :], [[-LS, NB], [0, LS]], 0, 1, 0.0)
            keep(same_s[:, :, :], [[LS, NB], [0, LS]], LS - 1, -1, 0.0)
            keep(sel16[:, :, :], [[-32, 4], [-16, 2]], 0, 1, 0.0)
            keep(sel16[:, :, :], [[32, 4], [16, 2]], 15, -1, 0.0)
            q(pool.memset(half2[0:64, 0:1], 1.0))
            q(pool.memset(half2[64:128, 1:2], 1.0))
            q(pool.memset(start[:, 0:1], 0.0))
            pool.memset(start[:, NP:T].rearrange("p (b l) -> p b l", b=NB)[:, :, 0], 0.0).then_inc(s["consts"], 1)

            pool.wait_ge(s["s5par"], 1)

            def tables(oc, part):
                tb = tab[oc % 2]
                js = slice(4 * oc, 4 * oc + 4)
                if part == 0:
                    if oc >= 2:
                        pool.wait_ge(s["s5rot"], 4 * (oc - 1))
                        pool.wait_ge(s["tab_used"], 4 * (oc - 1))
                    pool.memset(tb[:, 0, :, 0:1], 1.0)
                    q(pool.memset(tb[:, 1, :, 0:1], 0.0))
                    q(pool.tensor_copy(tb[:, :, :, 1], e[:, 0, :, js]))
                for k in ((1, 2), (3, 4))[part]:
                    m = 2 ** k
                    new, old = tb[:, :, :, m:2 * m], tb[:, :, :, 0:m]
                    er = e[:, k, 0, js].unsqueeze(1).unsqueeze(3).to_broadcast([P, 2, 4, m])
                    ei = e[:, k, 1, js].unsqueeze(1).unsqueeze(3).to_broadcast([P, 2, 4, m])
                    pool.tensor_tensor(new, old, er, ALU.mult)
                    q(pool.tensor_tensor(tabtmp[:, :, :, 0:m], old, ei, ALU.mult))
                    pool.tensor_tensor(new[:, 0], new[:, 0], tabtmp[:, 1, :, 0:m], ALU.subtract)
                    ins = pool.tensor_tensor(new[:, 1], new[:, 1], tabtmp[:, 0, :, 0:m], ALU.add)
                    if k < 4:
                        q(ins)
                    else:
                        ins.then_inc(s["tab_half"], 1)

            for oc in range(2):
                tables(oc, 0)
                tables(oc, 1)
            for st in range(NST):
                tb, j = tab[st // 4 % 2], st % 4
                cs_ = tb[:, 0:1, j].to_broadcast([P, 2, T])
                sn_ = tb[:, 1:2, j].to_broadcast([P, 2, T])
                pool.wait_ge(s["scan"], 2 * st + 2)
                pool.wait_ge(s["tab_ready"], st // 4 + 1)
                if st:
                    pool.wait_ge(s["s5rot"], st)
                pool.tensor_tensor(n1, wb[st % 2], cs_, ALU.mult)
                q(pool.tensor_tensor(n2, wb[st % 2], sn_, ALU.mult))
                if st >= 3:
                    pool.wait_ge(s["y5_full"], st - 2)
                    pool.wait_ge(s["sl"], st - 2)
                pool.tensor_tensor(sbuf[st % 3][:, 0], n1[:, 0], n2[:, 1], ALU.subtract)
                pool.tensor_tensor(sbuf[st % 3][:, 1], n1[:, 1], n2[:, 0], ALU.add).then_inc(s["s5rot"], 1)
                if j < 2 and 4 <= st < NST - 4:
                    tables(st // 4 + 1, j)

            done(pool, "mv3")
            pool.dma_start(o["mv"][0, 0].rearrange("(c p) a d -> p c (a d)", p=P), vm).then_inc(s["out_v"], 16)
            done(pool, "ko11")
            done(pool, "ko10")
            pool.dma_start(o["mk"][0, 0].rearrange("(c p) a d -> p c (a d)", p=P), kout).then_inc(s["out_k"], 16)
            done(pool, "s5o1")
            done(pool, "s5o0")
            for ri, part in enumerate(("re", "im")):
                pool.dma_start(o[part + "p"].rearrange("l b (s h) n -> (l b s) (h n)", h=2),
                               s5out[0:NST, ri]).then_inc(s["out_s5"], 16)
                for k in range(2):
                    pool.dma_start(o[part + "s"].rearrange("l b (s h) n -> (l b s) (h n)", h=2)[P * k:P * (k + 1)],
                                   s5out[:, 2 + 2 * ri + k]).then_inc(s["out_s5"], 16)
            done(pool, "nc2")
            done(pool, "nc1")
            pool.dma_start(o["cvp"].rearrange("l b t n -> (l b t) n"), ncout[0:3]).then_inc(s["out_cv"], 16)
            pool.dma_start(o["cvs"].rearrange("l b t n -> (l b t) n"), ncout[3:27]).then_inc(s["out_cv"], 16)
            for t in range(KT):
                done(pool, f"ns{t}b")
                pool.dma_start(o["ssds"][0].rearrange("b (t h) p n -> t (h p) b n", h=2)[t], hbuf[t % 4]).then_inc(
                    s[f"out_st{t % 4}"], 16)
            done(pool, "hl1")
            pool.dma_start(o["ssdp"][0, 0].rearrange("(t h) p n -> (h p) t n", h=2), hlo).then_inc(s["out_hl"], 16)
            for c in range(NC):
                pool.wait_ge(s["fy"], c + 1)
                if c < 2:
                    pool.dma_start(o["yp"][0, P * c:P * (c + 1)], fy[c % 2]).then_inc(s[f"out_y{c}"], 16)
                else:
                    pool.dma_start(o["ys"].rearrange("b l d -> (b l) d"), fy[c % 2][0:NS]).then_inc(s["out_y2"], 16)
            for name, v in (("out_v", 16), ("out_k", 16), ("out_s5", 96), ("out_cv", 32), ("out_hl", 16), ("out_st0", 32),
                            ("out_st1", 32), ("out_st2", 32), ("out_st3", 32), ("out_y0", 16), ("out_y1", 16), ("out_y2", 16)):
                pool.wait_ge(s[name], v)

        @block.scalar
        def _(act):
            n = [0]

            def q(ins):
                n[0] += 1
                ins.then_inc(s["act"], 1)
                act.wait_ge(s["act"], n[0])

            def rows(dst, src, sem_):
                act.dma_start(dst, src).then_inc(s[sem_], 16)

            for at, name in ((V_MIX, "norm_mix_g"), (V_SSD, "ssd_norm_g"), (V_Q, "norm_mem_q_g"), (V_KV, "norm_mem_kv_g"),
                             (V_FFN, "norm_ffn_g"), (V_D5, "s5_d"), (V_GLU, "b_glu")):
                k = a[name].shape[1] // P
                rows(vecrow[at:at + k], a[name][0].rearrange("(k p) -> k p", p=P), "ld_par")
            rows(vecrow[V_CW:V_CB], a["conv_w"][0].rearrange("t (k p) -> (t k) p", p=P), "ld_par")
            rows(vecrow[V_CB:124], a["conv_b"][0].rearrange("(k p) -> k p", p=P), "ld_par")
            rows(lamrow[0:NST, 0], a["s5_lambda_re"][0].rearrange("(s h) n -> s (h n)", h=2), "ld_par")
            rows(lamrow[0:NST, 1], a["s5_lambda_im"][0].rearrange("(s h) n -> s (h n)", h=2), "ld_par")
            rows(lsrow[0:NST], a["s5_log_step"][0].rearrange("(s h) -> s h", h=2), "ld_par")
            rows(dd8[0:KT], a["ssd_d"][0].rearrange("(s h) -> s h", h=2), "ld_par")
            def root(use, cols=slice(0, NC)):
                act.wait_ge(s["var"], use + 1)
                act.activation(rs0[:, cols], var[:, cols], ACT.Sqrt).then_inc(s["rs0"], 1)

            act.wait_ge(s["consts"], 1)
            act.wait_ge(s["ld_x"], 32)
            for c in range(NC):
                R = ROWS[c]
                act.activation(junk[0:R], xt[0:R, c], ACT.Square, accum_out=ss[0:R, c:c + 1]).then_inc(s["ss"], 1)
                act.wait_ge(s["ss"], c + 1)
            root(0)
            for ri, name in enumerate(("s5_b_re", "s5_b_im")):
                rows(bnat[:, ri], a[name][0].rearrange("(s h) n k -> (h n) s k", h=2), "ld_s5")
            for ri, name in enumerate(("s5_c_re", "s5_c_im")):
                rows(cnat[:, ri], a[name][0].rearrange("(t i) k n -> (i k) t n", i=8), "ld_s5")
            for ri, name in enumerate(("state_s5_re", "state_s5_im")):
                rows(st_nat[:, ri], a[name][0].rearrange("(r b) (s h) n -> (b s) r (h n)", r=2, h=2), "ld_s5")
            rows(cv_nat[0:3 * NB], a["state_conv"][0].rearrange("b t n -> (b t) n"), "ld_s5")
            rows(wdt[:, :, :], a["w_in"][0][:, COL["dt"]:COL["dt"] + HEADS].rearrange("(k p) n -> p k n", p=P), "ld_small")
            rows(wr[:, :, 0:NG], a["w_router_group"][0].rearrange("(k p) n -> p k n", p=P), "ld_small")
            rows(wr[:, :, NG:], a["w_router_expert"][0].rearrange("(k p) n -> p k n", p=P), "ld_small")
            rows(dtb[:, :], a["ssd_dt_bias"].to_broadcast([P, HEADS]), "ld_small")
            rows(alog[:, :], a["ssd_a_log"].to_broadcast([P, HEADS]), "ld_small")
            rows(rbias[:, 0:NG], a["b_router_group"].to_broadcast([P, NG]), "ld_small")
            rows(rbias[:, NG:], a["b_router_expert"].to_broadcast([P, NG * NE]), "ld_small")

            act.wait_ge(s["ld_mem"], 16)
            for c in range(2):
                act.activation(junk, memraw[:, c], ACT.Square, accum_out=ss[:, 3 + c:4 + c]).then_inc(s["ss"], 1)
                act.wait_ge(s["ss"], 4 + c)
            act.wait_ge(s["s5w"], 1)
            act.activation(s5p[:, 0], lam[:, 2 * NST:3 * NST], ACT.Exp).then_inc(s["s5c"], 1)
            act.wait_ge(s["s5w"], 2)
            act.activation(s5p[:, 3], s5p[:, 1], ACT.Exp).then_inc(s["s5c"], 1)
            act.wait_ge(s["s5w"], 3)
            act.activation(e[:, 0, 1], s5p[:, 6], ACT.Sin)
            act.activation(e[:, 0, 0], s5p[:, 7], ACT.Sin).then_inc(s["s5c"], 1)
            for m in range(KT):
                got(act, f"u5{m}")
                emptied(act.activation(u5T[:, m], bank(f"u5{m}")[:, 0:T], ACT.Copy), f"u5{m}")
            got(act, "s5h")
            emptied(act.activation(h0s.rearrange("p r b s -> p (r b s)"), bank("s5h")[:, 0:512], ACT.Copy), "s5h")
            got(act, "cvs")
            emptied(act.activation(cst[:, :, :].rearrange("p k t -> p (k t)"), bank("cvs")[:, 0:CT * 24], ACT.Copy), "cvs")
            for t_, dst in (("bt", bT), ("ct", cT)):
                for i in range(4):
                    got(act, f"{t_}{i}")
                    emptied(act.activation(dst[:, 2 * i:2 * i + 2].rearrange("p t r n -> p (t r n)"),
                                           bank(f"{t_}{i}")[:, :], ACT.Copy), f"{t_}{i}")
            root(1, slice(NC, NC + 2))

            def fill_evac(kind, m):
                job = f"{kind}{m}"
                got(act, job)
                if kind == "xbc":
                    if m >= 2:
                        act.wait_ge(s["convout"], m - 1)
                    dst = cvin[m % 2]
                    act.activation(dst[:, 3:3 + NP], bank(job)[:, 0:NP], ACT.Copy)
                    emptied(act.activation(dst[:, 259:347].rearrange("p (b l) -> p b l", b=NB)[:, :, 3:11],
                                           bank(job)[:, NP:T].rearrange("p (b l) -> p b l", b=NB), ACT.Copy), job)
                elif kind == "mk":
                    emptied(act.activation(kT[:, m], bank(job)[:, 0:MEM], ACT.Copy), job)
                else:
                    emptied(act.activation(vm[:, m % 2, BLK * (m // 2):BLK * (m // 2 + 1)], bank(job)[:, :], ACT.Copy), job)

            def conv_silu(m):
                act.wait_ge(s["convout"], m + 1)
                v = cvout[m % 2]
                act.activation(xcT[:, m, 0:NP], v[:, 0:NP], ACT.Silu)
                src = v[:, 256:344].rearrange("p (b l) -> p b l", b=NB)[:, :, 3:11]
                act.activation(xcT[:, m, NP:T].rearrange("p (b l) -> p b l", b=NB), src, ACT.Silu).then_inc(s["xc"], 1)

            act.wait_ge(s["inj"], 1)
            for st in range(NST):
                got(act, f"bu{st}r")
                if st >= 2:
                    act.wait_ge(s["scan"], 2 * (st - 1))
                act.activation(rm[st % 2], start[:, :], ACT.Copy, scale=s5p[:, 3, st:st + 1])
                emptied(act.activation(ub[st % 2][:, 0], bank(f"bu{st}r")[:, 0:T], ACT.Copy), f"bu{st}r")
                got(act, f"bu{st}i")
                emptied(act.activation(ub[st % 2][:, 1], bank(f"bu{st}i")[:, 0:T], ACT.Copy), f"bu{st}i")
                if st < len(FILL):
                    fill_evac(*FILL[st])
                if st in (24, 25):
                    for hf in range(2):
                        job = f"ko{st - 24}{hf}"
                        got(act, job)
                        emptied(act.activation(kout[:, st - 24, 512 * hf:512 * hf + 512], bank(job)[:, :], ACT.Copy), job)
                if st == 26:
                    act.wait_ge(s["convout"], CT)
                    act.wait_ge(s["xc"], CT)
                    got(act, "dtT")
                    emptied(act.activation(dtS[0:HEADS], bank("dtT")[0:HEADS, 0:T], ACT.Copy), "dtT")
                if st == 28:
                    act.wait_ge(s["ld_small"], 16 * 7)
                    act.activation(anegb, alog[:, :], ACT.Exp).then_inc(s["sp_e"], 1)
                    act.wait_ge(s["dtx"], 1)
                    q(act.activation(dtl, dte, ACT.Exp))
                    act.activation(dtl, dtl, ACT.Ln, bias=1.0).then_inc(s["sp_e"], 1)
                if 2 <= st <= CT + 1:
                    conv_silu(st - 2)
                if st >= 2:
                    keep_last(act, st - 2)
            keep_last(act, NST - 2)
            keep_last(act, NST - 1)
            def keep_z(m):
                got(act, f"z{m}")
                emptied(act.activation(zT[:, m], bank(f"z{m}")[:, 0:T], ACT.Copy), f"z{m}")

            keep_z(0)
            got(act, "s5o0")
            emptied(act.activation(s5out[0:NST, 0:2].rearrange("p a n -> p (a n)"), bank("s5o0")[0:NST, 0:256], ACT.Copy), "s5o0")
            got(act, "s5o1")
            emptied(act.activation(s5out[:, 2:6].rearrange("p a n -> p (a n)"), bank("s5o1")[:, :], ACT.Copy), "s5o1")
            keep_z(1)
            for i in range(3):
                got(act, f"nc{i}")
                emptied(act.activation(ncout[0:27, 512 * i:512 * i + 512], bank(f"nc{i}")[0:27, :], ACT.Copy), f"nc{i}")

            got(act, "ecs")
            act.wait_ge(s["cs_in"], 1)
            act.activation(wend, dtl, ACT.Exp).then_inc(s["wdec"], 1)
            act.activation(etot, tot, ACT.Exp).then_inc(s["etot"], 1)
            emptied(act.activation(ecs[:, :, P:192], bank("ecs")[:, :].rearrange("p (t l) -> p t l", t=KT), ACT.Exp), "ecs")
            for i in range(2):
                got(act, f"ecp{i}")
                emptied(act.activation(ecs[:, 4 * i:4 * i + 4, 0:P], bank(f"ecp{i}")[:, :].rearrange("p (t l) -> p t l", t=4),
                                       ACT.Exp), f"ecp{i}")
            keep_z(2)
            for c in range(NC):
                R = ROWS[c]
                got(act, f"tb{c}")
                emptied(act.activation(btok[0:R, c].rearrange("p g n -> p (g n)"), bank(f"tb{c}")[0:R, 0:256], ACT.Copy), f"tb{c}")
                got(act, f"cb{c}")
                emptied(act.activation(cbT[0:R, c, :, 0:R], bank(f"cb{c}")[0:R, 0:2 * P].rearrange(
                    "p (g l) -> p g l", g=2)[:, :, 0:R], ACT.Copy), f"cb{c}")
            keep_z(3)
            for g in range(2):
                got(act, f"s0{g}")
                emptied(act.activation(s0T[:, 512 * g:512 * g + 512], bank(f"s0{g}")[:, :], ACT.Copy), f"s0{g}")
            def decay(i):
                for c in range(NC):
                    act.wait_ge(s["csd"], 3 * i + c + 1)
                    d_ = dm[i % 2][c][0:ROWS[c]]
                    act.activation(d_, d_, ACT.Exp).then_inc(s["csm"], 1)

            decay(0)
            for i in range(4):
                for t in (2 * i, 2 * i + 1):
                    if t % 2 and i < 3:
                        decay(i + 1)
                    if t:
                        got(act, f"yx{t - 1}")
                    for hf, k in (("a", 0), ("b", 4)):
                        got(act, f"h0{t}{hf}")
                        emptied(act.activation(h0T[:, k:k + 4].rearrange("p b n -> p (b n)"), bank(f"h0{t}{hf}")[:, :],
                                               ACT.Copy), f"h0{t}{hf}")

            def split_unit(u):
                if u < UNITS:
                    n = SPLIT0 + u // 2
                    act.wait_ge(w_in_sem[n % STAT_SLOTS], loads(n))
                    if u >= 2:
                        got(act, UNIT_LAST[u - 2])
                    act.activation(uhi[u % 2], unit_raw(u), ACT.Copy).then_inc(s["whi"], 1)

            got(act, "s11")
            done(act, "ns7b")
            split_unit(0)
            for k in range(KT):
                act.activation(hn_hi[:, k], hnT[:, k], ACT.Copy).then_inc(s["hn_hi"], 1)
            act.wait_ge(s["out_st1"], 32)
            for i in range(2):
                got(act, f"hl{i}")
                emptied(act.activation(hlo[:, 4 * i:4 * i + 4].rearrange("p t n -> p (t n)"), bank(f"hl{i}")[:, :],
                                       ACT.Copy), f"hl{i}")
            act.activation(zT[:, 0:4], zT[:, 0:4], ACT.Silu).then_inc(s["zs"], 1)
            for m in range(4, KT):
                if m % 2 == 0:
                    split_unit((m - 4) // 2 + 1)
                got(act, f"z{m}")
                emptied(act.activation(zT[:, m], bank(f"z{m}")[:, 0:T], ACT.Silu), f"z{m}")
            for m in range(KT):
                act.wait_ge(s["y_done"], m + 1)
                act.activation(ysq[:, m], y[:, m], ACT.Square).then_inc(s["ysq"], 1)
            act.wait_ge(s["out_st2"], 32)
            act.wait_ge(s["out_st3"], 32)
            for m in range(KT):
                if m % 2 == 0:
                    split_unit(unit_of("ga0") + m // 2 + 1)
                if m == 4:
                    done(act, "ssy")
                    act.activation(yr0, yv, ACT.Sqrt).then_inc(s["yr"], 1)
                if m == 6:
                    for k in range(KT):
                        act.wait_ge(s["yn"], k + 1)
                        act.activation(yb_hi[:, k], y[:, k], ACT.Copy).then_inc(s["yb_hi"], 1)
                got(act, f"ga{m}")
                emptied(act.activation(mrg[:, m], bank(f"ga{m}")[:, 0:T], ACT.Tanh, scale=0.5), f"ga{m}")
            for i in range(4):
                split_unit(unit_of("sb0") + i + 1)
            for m in range(KT):
                if m % 2 == 0:
                    split_unit(unit_of("gb0") + m // 2 + 1)
                got(act, f"gb{m}")
                emptied(act.activation(thB[:, m], bank(f"gb{m}")[:, 0:T], ACT.Tanh, scale=0.5), f"gb{m}")
                if m == 2:
                    act.wait_ge(s["y5_free"], KT)
                    act.activation(u5_hi, u5T, ACT.Copy).then_inc(s["u5_hi"], 1)

            def merged_hi(m):
                act.wait_ge(s["glu_used"], m + 1)
                act.activation(mrg_hi[:, m], mrg[:, m], ACT.Copy).then_inc(s["mrg_hi"], 1)

            for m in range(KT):
                if m % 4 == 0:
                    if m:
                        act.wait_ge(s["glu_used"], m)
                    for k in range(m, m + 4):
                        if k % 2 == 0:
                            split_unit(unit_of(f"gv{m // 4}") + (k - m) // 2 + 1)
                        got(act, f"gv{k}")
                        emptied(act.activation(val[:, k - m], bank(f"gv{k}")[:, 0:T], ACT.Identity,
                                               bias=vec[:, V_GLU + k:V_GLU + k + 1]), f"gv{k}")
                if m % 2 == 0:
                    split_unit(unit_of(f"gg{m // 4}") + m % 4 // 2 + 1)
                got(act, f"gg{m}")
                if m >= 2:
                    act.wait_ge(s["glu_used"], m - 1)
                emptied(act.activation(th[m % 2], bank(f"gg{m}")[:, 0:T], ACT.Tanh, scale=0.5, bias=hglu[:, m:m + 1]), f"gg{m}")
                if m:
                    merged_hi(m - 1)
            merged_hi(KT - 1)
            for i in range(4):
                split_unit(unit_of("mx0") + i + 1)

            done(act, f"mx3{NC - 1}")
            squares(act, 5)
            root(2)
            for c in range(NC):
                for hf in range(2):
                    done(act, f"hq{c}{hf}")
                    v = (slice(None), slice(4 * hf, 4 * hf + 4), slice(P * c, P * c + ROWS[c]))
                    act.activation(q_hi[v], hn2T[v], ACT.Copy).then_inc(s["q_hi"], 1)
            for m in range(KT):
                if m % 2 == 0:
                    split_unit(unit_of("q0") + m // 2 + 1)
                got(act, f"q{m}")
                emptied(act.activation(qT[:, m], bank(f"q{m}")[:, 0:T], ACT.Copy, scale=1.0 / 16), f"q{m}")
            split_unit(unit_of("o0", 1))

            def exps(k, scores):
                act.wait_ge(s["nmax"], k + 1)
                act.activation(pr[k % 2], scores[:, 0:MEM], ACT.Exp, bias=att[:, k % 2, 0:1],
                               accum_out=att[:, k % 2, 1:2]).then_inc(s["pexp"], 1)

            def keys(b):
                for i in range(2):
                    got(act, f"kt{b}{2 * i}")
                    if b >= 2 and i == 0:
                        act.wait_ge(s["sb_full"], b - 1)
                    emptied(act.activation(kbT[b % 2][:, 4 * i:4 * i + 2].rearrange("p k m -> p (k m)"),
                                           bank(f"kt{b}{2 * i}")[:, :], ACT.Copy), f"kt{b}{2 * i}")

            exps(0, bank("sc00"))
            for k in range(2 * MH):
                c, hd = divmod(k, MH)
                if k < 7:
                    if k:
                        got(act, "pt%d%d" % divmod(k - 1, MH))
                    exps(k + 1, bank("sc%d%d" % divmod(k + 1, MH)))
                got(act, f"pt{c}{hd}")
                if k >= 2:
                    got(act, "ao%d%d" % divmod(k - 2, MH))
                emptied(act.activation(pT[k % 2].rearrange("p m l -> p (m l)"), bank(f"pt{c}{hd}")[:, 0:256], ACT.Copy),
                        f"pt{c}{hd}")
            keys(0)
            exps(8, psum[6])
            for b in range(NB):
                if b < NB - 1:
                    keys(b + 1)
                got(act, f"sp{b}")
                if b >= 2:
                    act.wait_ge(s["ob_full"], b - 1)
                else:
                    got(act, f"ao1{2 + b}")
                emptied(act.activation(pT[b % 2].rearrange("p m l -> p (m l)"), bank(f"sp{b}")[:, 0:256], ACT.Copy), f"sp{b}")
                if b < NB - 1:
                    exps(8 + b + 1, psum[6])
                if b == 1:
                    done(act, "ao13")
                    act.activation(ao_hi[:, :, 0:NP], aoT[:, :, 0:NP], ACT.Copy).then_inc(s["ao_hi"], 1)
            done(act, f"ot{NB - 1}")
            act.activation(ao_hi[:, :, NP:T], aoT[:, :, NP:T], ACT.Copy).then_inc(s["ao_hi"], 1)
            for i in range(1, 4):
                split_unit(unit_of("o0") + i + 1)
            done(act, f"o3{NC - 1}")
            squares(act, 8)
            root(3)

            def chunk_hi(pos, turn):
                act.wait_ge(raw_in[pos % RAW], turn)
                act.activation(whi[pos % PAIR], raw[pos % RAW], ACT.Copy).then_inc(s["hi"], 1)

            for pos in range(AHEAD):
                chunk_hi(pos, 16)
            act.wait_ge(s["rt_a"], 1)
            act.activation(rt[:, 2, :, 0:NG], rt[:, 1, :, 0:NG], ACT.Exp).then_inc(s["rt_e"], 1)
            act.wait_ge(s["rt_a"], 2)
            act.activation(rt[:, 12, :, 0:1], rt[:, 11, :, 0:1], ACT.Exp).then_inc(s["rt_e"], 1)

            npass = load_passes(act)
            with act.Fori(0, npass) as rr:
                def tokens_hi(grp, half):
                    act.wait_ge(s["gx_full"], grp * 3 + half + 1)
                    for j in range(4):
                        k = 4 * half + j
                        ins = act.activation(xhi[:, k], psum[5][:, P * j:P * (j + 1)], ACT.Copy, scale=vec[:, V_FFN + k:V_FFN + k + 1])
                    ins.then_inc(s["xhi"], 1)

                def slots_in(grp, g, skip):
                    act.wait_ge(s["gx_full"], grp * 3 + 3)
                    act.activation(pgT, psum[5][:, 0:T], ACT.Copy)
                    act.activation(cg[:, NE * skip:][:, bass.ds(g * NE, NE)], psum[5][:, T:T + NE], ACT.Copy).then_inc(s["gx_free"], 1)

                def group(g, last):
                    grp = rr * NG + g
                    base = grp * GCH
                    for two in range(NE // 2):
                        b2 = base + two * NCH

                        def silu(x):
                            act.wait_ge(s["chunk_done"], b2 + (2, 6)[x] + CD0)
                            act.activation(sil[x], psum[x][:, :], ACT.Silu).then_inc(s["sil"], 1)

                        def ht(x):
                            act.wait_ge(s["t_full"], grp * NE + 2 * two + x + 1)
                            act.activation(hthi[x].rearrange("p j n -> p (j n)"), psum[4][:, :], ACT.Copy).then_inc(s["hthi"], 1)

                        for pos in range(NCH):
                            act.wait_ge(s["chunk_done"], b2 + pos + 1 + CD0)
                            m = pos + AHEAD
                            chunk_hi(m, (grp * (GCH // RAW) + two * (NCH // RAW) + m // RAW + 1) * 16)
                            if pos == 1:
                                silu(0)
                            if pos == 5:
                                silu(1)
                                ht(0)
                            if pos == 7:
                                if two == NE // 2 - 1 and not last:
                                    tokens_hi(grp + 1, 0)
                                ht(1)
                            if pos == 9 and two == NE // 2 - 1 and not last:
                                tokens_hi(grp + 1, 1)
                    if not last:
                        slots_in(grp + 1, g, 1)

                for half in range(2):
                    tokens_hi(rr * NG, half)
                slots_in(rr * NG, 0, 0)
                with act.Fori(0, NG - 1) as g:
                    group(g, False)
                group(NG - 1, True)
            act.wait_ge(s["fin"], 1)
            squares(act, 11)
            root(4)

        @block.tensor
        def _(pe):
            at = [0]

            def take(job):
                assert PLAN[at[0]] == job, (PLAN[at[0]], job)
                at[0] += 1
                b, turn = BANK[job]
                if turn:
                    pe.wait_ge(free[b], turn)
                return psum[b]

            def end(ins, job):
                ins.then_inc(full[BANK[job][0]], 1)

            def tr(out, in_, rows=P):
                return nc.tensor.transpose(out, in_, ident[0:rows, 0:rows])

            def have(block_):
                k = BIDX[block_]
                pe.wait_ge(w_in_sem[k % STAT_SLOTS], loads(k))

            def proj(kind, m, src, N):
                job = f"{kind}{m}"
                b = take(job)
                if m % 4 == 0:
                    have(f"{kind}{m // 4}")
                wv = blk(f"{kind}{m // 4}")
                for k in range(KT):
                    ins = nc.tensor.matmul(b[:, 0:N], wv[:, k, P * (m % 4):P * (m % 4 + 1)], src[:, k, 0:N],
                                           start=(k == 0), stop=(k == KT - 1))
                end(ins, job)

            def proj_tok(job, block_, src, c, R):
                b = take(job)
                wv = blk(block_)
                for k in range(KT):
                    ins = nc.tensor.matmul(b[0:R, :], src[:, k, P * c:P * c + R], wv[:, k, :],
                                           start=(k == 0), stop=(k == KT - 1))
                end(ins, job)

            pe.wait_ge(s["consts"], 1)
            b = take("par")
            pe.wait_ge(s["ld_par"], 16 * 13)
            pe.wait_ge(s["rows"], 1)
            nc.tensor.transpose(b[:, 0:124], vecrow[0:124], ident[0:124, 0:124])
            for i in range(3):
                tr(b[:, 128 + NST * i:128 + NST * (i + 1)], lamrow[0:NST, i], NST)
            end(tr(b[:, 224:232], ddrow[0:KT], KT), "par")

            def norm_in(i, kind, c):
                R = ROWS[c] if kind == "x" else P
                pe.wait_ge(s["xn"], i + 1)
                for hf in range(2):
                    b = take(f"{kind}{c}{hf}")
                    for j in range(4):
                        ins = tr(b[:, P * j:P * j + R], xn[i % 2][0:R, P * (4 * hf + j):P * (4 * hf + j + 1)], R)
                    end(ins, f"{kind}{c}{hf}")

            for c in range(NC):
                norm_in(c, "x", c)
            done(pe, "x21")
            done(pe, "x20")
            for m in range(KT):
                proj("u5", m, hnT, T)
            pe.wait_ge(s["ld_s5"], 16 * 7)
            b = take("s5h")
            for ri in range(2):
                for k in range(2):
                    ins = tr(b[:, 256 * ri + P * k:256 * ri + P * (k + 1)], st_nat[:, ri, k])
            end(ins, "s5h")
            b = take("cvs")
            for k in range(CT):
                ins = tr(b[:, 24 * k:24 * k + 24], cv_nat[0:24, P * k:P * (k + 1)], 24)
            end(ins, "cvs")
            for t_, src in (("bt", bx), ("ct", cx)):
                pe.wait_ge(s["bx"] if t_ == "bt" else s["cx"], 1)
                for i in range(4):
                    b = take(f"{t_}{i}")
                    for k in range(2):
                        for ri in range(2):
                            ft = 2 * i + k
                            v = src[:, ri].rearrange("p a b c -> p (a b c)")[:, P * ft:P * (ft + 1)]
                            ins = tr(b[:, P * (2 * k + ri):P * (2 * k + ri + 1)], v)
                    end(ins, f"{t_}{i}")
            for c in range(2):
                norm_in(NC + c, "m", c)
            for i in range(4):
                done(pe, f"bt{i}")
                done(pe, f"ct{i}")
            done(pe, "u57")
            done(pe, "m11")
            done(pe, "m10")

            def s5_out(st):
                ft, i = st // 4, st % 4
                yb = psum[6 + ft % 2]
                pe.wait_ge(s["s5rot"], st + 1)
                if i == 0 and ft >= 2:
                    pe.wait_ge(s["y5_free"], ft - 1)
                for ri in range(2):
                    ins = nc.tensor.matmul(yb[32 * i:32 * i + 32, 0:T], cT[:, ft, ri, 32 * i:32 * i + 32],
                                           sbuf[st % 3][:, ri], start=(ri == 0), stop=(ri == 1))
                ins.then_inc(s["y5_full"], 1)

            up = [upto[:, :], upto[:, :], upto_s[:, :, :].rearrange("p b l -> p (b l)")]
            al = [ones[:, :], ones[:, :], same_s[:, :, :].rearrange("p b l -> p (b l)")]
            for st in range(NST):
                ft, i = st // 4, st % 4
                for ri, c in enumerate("ri"):
                    b = take(f"bu{st}{c}")
                    end(nc.tensor.matmul(b[:, 0:T], bT[32 * i:32 * i + 32, ft, ri], u5T[32 * i:32 * i + 32, ft],
                                         start=True, stop=True), f"bu{st}{c}")
                if st < len(FILL):
                    kind, m = FILL[st]
                    if kind == "xbc":
                        proj("xbc", m, hnT, T)
                    elif kind == "mk":
                        proj("mk", m, mnT, MEM)
                    else:
                        if m % 2 == 0:
                            have(f"mv{m // 2}")
                        proj_tok(f"mv{m}", f"mv{m // 2}", mnT, m % 2, P)
                if st in (24, 25):
                    done(pe, "mk7")
                    m = st - 24
                    for hf in range(2):
                        b = take(f"ko{m}{hf}")
                        for j in range(4):
                            ins = tr(b[:, P * j:P * (j + 1)], kT[:, 4 * hf + j, P * m:P * (m + 1)])
                        end(ins, f"ko{m}{hf}")
                if st == 26:
                    b = take("dtT")
                    pe.wait_ge(s["ld_small"], 16 * 7)
                    for k in range(KT):
                        ins = nc.tensor.matmul(b[0:HEADS, 0:T], wdt[:, k], hnT[:, k], start=(k == 0), stop=(k == KT - 1))
                    end(ins, "dtT")
                if st == 27:
                    b = take("dt3")
                    done(pe, "dtT")
                    for c in range(NC):
                        R = ROWS[c]
                        ins = tr(b[0:R, HEADS * c:HEADS * (c + 1)], dtS[0:HEADS, P * c:P * c + R], HEADS)
                    end(ins, "dt3")
                if st == 29:
                    b = take("cs")
                    pe.wait_ge(s["dt_ready"], 1)
                    for c in range(NC):
                        R = ROWS[c]
                        nc.tensor.matmul(b[0:R, HEADS * c:HEADS * (c + 1)], up[c], dtA[0:R, c], start=True, stop=True)
                        ins = nc.tensor.matmul(b[0:R, 48 + HEADS * c:48 + HEADS * (c + 1)], al[c], dtA[0:R, c],
                                               start=True, stop=True)
                    end(ins, "cs")
                if st >= 2:
                    s5_out(st - 2)
            s5_out(NST - 2)
            s5_out(NST - 1)
            proj("z", 0, hnT, T)
            pe.wait_ge(s["sl"], NST)
            b = take("s5o0")
            for ri in range(2):
                ins = tr(b[0:NST, P * ri:P * (ri + 1)], sl[:, ri, 0:NST])
            end(ins, "s5o0")
            b = take("s5o1")
            for ri in range(2):
                for k in range(2):
                    ins = tr(b[:, P * (2 * ri + k):P * (2 * ri + k + 1)], sl[:, ri, NST + P * k:NST + P * (k + 1)])
            end(ins, "s5o1")
            proj("z", 1, hnT, T)
            pe.wait_ge(s["convout"], CT)
            for i in range(3):
                b = take(f"nc{i}")
                for j in range(4):
                    ins = tr(b[0:27, P * j:P * (j + 1)], last3[:, 4 * i + j])
                end(ins, f"nc{i}")

            def cum_rows(out, c, head, M):
                R = ROWS[c]
                return nc.tensor.matmul(out, dtA[0:R, c, head:head + 1].to_broadcast([R, M]), up[c], start=True, stop=True)

            b = take("ecs")
            for hd in range(HEADS):
                t, q_ = hd // 2, 64 * (hd % 2)
                ins = cum_rows(b[q_:q_ + 64, NS * t:NS * (t + 1)], 2, hd, HD)
            end(ins, "ecs")
            for i in range(2):
                b = take(f"ecp{i}")
                for hd in range(8 * i, 8 * i + 8):
                    t, q_ = hd // 2 - 4 * i, 64 * (hd % 2)
                    ins = cum_rows(b[q_:q_ + 64, P * t:P * (t + 1)], 1, hd, HD)
                end(ins, f"ecp{i}")
            proj("z", 2, hnT, T)
            pe.wait_ge(s["xc"], CT)
            for c in range(NC):
                R, c0 = ROWS[c], P * c
                for i in range(2):
                    b = take(f"tr{c}{i}")
                    for j in range(4):
                        ins = tr(b[0:R, P * j:P * (j + 1)], xcT[:, 4 * i + j, c0:c0 + R])
                    end(ins, f"tr{c}{i}")
                b = take(f"tb{c}")
                for g in range(2):
                    ins = tr(b[0:R, P * g:P * (g + 1)], xcT[:, 8 + g, c0:c0 + R])
                end(ins, f"tb{c}")
                b = take(f"cb{c}")
                for g in range(2):
                    ins = nc.tensor.matmul(b[0:R, P * g:P * g + R], xcT[:, 8 + g, c0:c0 + R], xcT[:, 10 + g, c0:c0 + R],
                                           start=True, stop=True)
                end(ins, f"cb{c}")
            proj("z", 3, hnT, T)
            done(pe, "tr21")
            done(pe, "tb2")
            for g in range(2):
                b = take(f"s0{g}")
                end(nc.tensor.matmul(b[:, :], btok[:, 0, g], wx[:, 0, 512 * g:512 * g + 512], start=True, stop=True), f"s0{g}")

            def decays(i):
                for c in range(NC):
                    R = ROWS[c]
                    b = take(f"csb{i}{c}")
                    for j in range(4):
                        ins = cum_rows(b[0:R, P * j:P * j + R], c, 4 * i + j, R)
                    end(ins, f"csb{i}{c}")

            def old_states(t):
                pe.wait_ge(s[f"ld_st{t % 4}"], 16 * (t // 4 + 1))
                for hf, k in (("a", 0), ("b", 4)):
                    b = take(f"h0{t}{hf}")
                    for j in range(4):
                        ins = tr(b[:, P * j:P * (j + 1)], hbuf[t % 4][:, k + j])
                    end(ins, f"h0{t}{hf}")

            decays(0)
            old_states(0)
            for i in range(4):
                g = i // 2
                if i < 3:
                    decays(i + 1)
                for t in (2 * i, 2 * i + 1):
                    b = take(f"yi{t}")
                    pe.wait_ge(s["mt"], 3 * i + 3)
                    for c in range(NC):
                        R, mt = ROWS[c], dm[i % 2][c]
                        for q_ in range(2):
                            hd = 2 * t + q_
                            ins = nc.tensor.matmul(b[64 * q_:64 * q_ + 64, P * c:P * c + R], xdt[0:R, c, HD * hd:HD * (hd + 1)],
                                                   mt[0:R, hd % 4, 0:R], start=True, stop=True)
                    end(ins, f"yi{t}")
                    if t < KT - 1:
                        old_states(t + 1)
                    b = take(f"yx{t}")
                    done(pe, "s01")
                    nc.tensor.matmul(b[:, 0:P], s0T[:, P * t:P * (t + 1)], xcT[:, 10 + g, P:2 * P], start=True, stop=True)
                    done(pe, f"h0{t}b")
                    for k in range(NB):
                        ins = nc.tensor.matmul(b[:, P + LS * k:P + LS * (k + 1)], h0T[:, k],
                                               xcT[:, 10 + g, NP + LS * k:NP + LS * (k + 1)], start=True, stop=True)
                    end(ins, f"yx{t}")
                    pe.wait_ge(s["bblk"], 1)
                    for hf, k in (("a", 0), ("b", 4)):
                        b = take(f"ns{t}{hf}")
                        end(nc.tensor.matmul(b[:, :], wx[0:NS, 2, P * t:P * (t + 1)], bblk[0:NS, g, k:k + 4],
                                             start=True, stop=True), f"ns{t}{hf}")
            for g in range(2):
                b = take(f"s1{g}")
                end(nc.tensor.matmul(b[:, :], btok[:, 1, g], wx[:, 1, 512 * g:512 * g + 512], start=True, stop=True), f"s1{g}")
            done(pe, "s11")
            for i in range(2):
                b = take(f"hl{i}")
                for j in range(4):
                    ins = tr(b[:, P * j:P * (j + 1)], hl[:, P * (4 * i + j):P * (4 * i + j + 1)])
                end(ins, f"hl{i}")
            def proj_split(kind, m, hi_, lo_, ready=None):
                job, u = f"{kind}{m}", unit_of(f"{kind}{m // 4}", m % 4 // 2)
                b = take(job)
                pe.wait_ge(s["wlo"], u + 1)
                for k in range(KT):
                    if ready:
                        pe.wait_ge(s[ready], k + 1)
                    wh, wl = (v[u % 2][:, k, P * (m % 2):P * (m % 2 + 1)] for v in (uhi, ulo))
                    nc.tensor.matmul(b[:, 0:T], wh, hi_[:, k], start=(k == 0), stop=False)
                    nc.tensor.matmul(b[:, 0:T], wh, lo_[:, k], start=False, stop=False)
                    ins = nc.tensor.matmul(b[:, 0:T], wl, hi_[:, k], start=False, stop=(k == KT - 1))
                end(ins, job)

            def tok_split(kind, i, c, hi_, lo_):
                R, job, u = ROWS[c], f"{kind}{i}{c}", unit_of(f"{kind}0") + i
                b = take(job)
                pe.wait_ge(s["wlo"], u + 1)
                for k in range(KT):
                    th_, tl_ = (v[:, k, P * c:P * c + R] for v in (hi_, lo_))
                    nc.tensor.matmul(b[0:R, 0:256], th_, uhi[u % 2][:, k], start=(k == 0), stop=False)
                    nc.tensor.matmul(b[0:R, 0:256], th_, ulo[u % 2][:, k], start=False, stop=False)
                    ins = nc.tensor.matmul(b[0:R, 0:256], tl_, uhi[u % 2][:, k], start=False, stop=(k == KT - 1))
                end(ins, job)

            for m in range(4, KT):
                proj_split("z", m, hn_hi, hn_lo, "hn_lo" if m == 4 else None)
            for m in range(KT):
                if m == 4:
                    b = take("ssy")
                    pe.wait_ge(s["ysq"], KT)
                    for k in range(KT):
                        ins = nc.tensor.matmul(b[:, 0:T], ones[:, :], ysq[:, k], start=(k == 0), stop=(k == KT - 1))
                    end(ins, "ssy")
                proj_split("ga", m, hn_hi, hn_lo)
            pe.wait_ge(s["yb_lo"], KT)
            for m in range(KT):
                proj_split("sb", m, yb_hi, yb_lo)
            for m in range(KT):
                proj_split("gb", m, hn_hi, hn_lo)
            pe.wait_ge(s["u5_lo"], 1)
            for i in range(2):
                for kind in ("gv", "gg"):
                    for m in range(4 * i, 4 * i + 4):
                        proj_split(kind, m, u5_hi, u5_lo)

            pe.wait_ge(s["mrg_lo"], KT)
            for i in range(4):
                for c in range(NC):
                    tok_split("mx", i, c, mrg_hi, mrg_lo)

            def norm_tr(kind, use):
                for c in range(NC):
                    R = ROWS[c]
                    pe.wait_ge(s["hn2"], 3 * use + c + 1)
                    for hf in range(2):
                        b = take(f"{kind}{c}{hf}")
                        src = hn2[c % 2] if kind == "hq" else tn[:, c]
                        for j in range(4):
                            ins = tr(b[:, P * j:P * j + R], src[0:R, P * (4 * hf + j):P * (4 * hf + j + 1)], R)
                        end(ins, f"{kind}{c}{hf}")
                done(pe, f"{kind}20")
                done(pe, f"{kind}21")

            norm_tr("hq", 0)
            pe.wait_ge(s["q_lo"], 2 * NC)
            for m in range(KT):
                proj_split("q", m, q_hi, q_lo)
            done(pe, "q7")

            def scores(k):
                c, hd = divmod(k, MH)
                b = take(f"sc{c}{hd}")
                for i in range(2):
                    ins = nc.tensor.matmul(b[:, 0:MEM], qT[:, 2 * hd + i, P * c:P * (c + 1)], kT[:, 2 * hd + i],
                                           start=(i == 0), stop=(i == 1))
                end(ins, f"sc{c}{hd}")

            scores(0)
            scores(1)
            for k in range(2 * MH):
                c, hd = divmod(k, MH)
                b = take(f"pt{c}{hd}")
                done(pe, f"sc{c}{hd}")
                for i in range(2):
                    ins = tr(b[:, P * i:P * (i + 1)], pr[k % 2][:, P * i:P * (i + 1)])
                end(ins, f"pt{c}{hd}")
                if k + 2 < 2 * MH:
                    scores(k + 2)
                b = take(f"ao{c}{hd}")
                done(pe, f"pt{c}{hd}")
                for dt_i in range(2):
                    for i in range(2):
                        ins = nc.tensor.matmul(b[:, P * dt_i:P * (dt_i + 1)],
                                               vm[:, i, MD * hd + P * dt_i:MD * hd + P * (dt_i + 1)], pT[k % 2][:, i],
                                               start=(i == 0), stop=(i == 1))
                end(ins, f"ao{c}{hd}")
            pe.wait_ge(s["zeroed"], 1)

            def keys(bb):
                K = kv[bb % 2][:, 0]
                pe.wait_ge(s[f"ld_k{bb % 2}"], 16 * (bb // 2 + 1))
                for i in range(4):
                    b = take(f"kt{bb}{i}")
                    for k in range(2):
                        for m in range(2):
                            ft = 2 * i + k
                            ins = tr(b[:, 256 * k + P * m:256 * k + P * (m + 1)], K[:, m, P * ft:P * (ft + 1)])
                    end(ins, f"kt{bb}{i}")

            def sample_scores(bb):
                for i in range(4):
                    done(pe, f"kt{bb}{i}")
                if bb:
                    pe.wait_ge(s["pexp"], 8 + bb)
                cols = slice(NP + LS * bb, NP + LS * (bb + 1))
                for hd in range(MH):
                    for k in range(2):
                        ins = nc.tensor.matmul(psum[6][32 * hd:32 * hd + LS, 0:MEM], qT[:, 2 * hd + k, cols],
                                               kbT[bb % 2][:, 2 * hd + k], start=(k == 0), stop=(k == 1))
                ins.then_inc(s["sb_full"], 1)

            def sample_out(bb):
                b = take(f"ot{bb}")
                pe.wait_ge(s["osb"], bb + 1)
                for k in range(2):
                    ins = tr(b[:, P * k:P * (k + 1)], oS[:, P * k:P * (k + 1)])
                end(ins, f"ot{bb}")

            keys(0)
            sample_scores(0)
            for bb in range(NB):
                V = kv[bb % 2][:, 1]
                if bb < NB - 1:
                    keys(bb + 1)
                if bb:
                    sample_out(bb - 1)
                b = take(f"sp{bb}")
                pe.wait_ge(s["pexp"], 8 + bb + 1)
                for k in range(2):
                    ins = tr(b[:, P * k:P * (k + 1)], pr[bb % 2][:, P * k:P * (k + 1)])
                end(ins, f"sp{bb}")
                if bb < NB - 1:
                    sample_scores(bb + 1)
                done(pe, f"sp{bb}")
                pe.wait_ge(s[f"ld_v{bb % 2}"], 16 * (bb // 2 + 1))
                if bb:
                    pe.wait_ge(s["osb"], bb)
                for hd in range(MH):
                    for k in range(2):
                        ins = nc.tensor.matmul(psum[7][32 * hd:32 * hd + LS, 0:MD], pT[bb % 2][:, k, 32 * hd:32 * hd + LS],
                                               V[:, k, MD * hd:MD * (hd + 1)], start=(k == 0), stop=(k == 1))
                ins.then_inc(s["ob_full"], 1)
            sample_out(NB - 1)
            done(pe, "ot7")
            done(pe, "ao13")
            pe.wait_ge(s["ao_lo"], 2)
            for i in range(4):
                for c in range(NC):
                    tok_split("o", i, c, ao_hi, ao_lo)
            norm_tr("ft", 1)
            b = take("lg")
            for c in range(NC):
                R = ROWS[c]
                for k in range(KT):
                    ins = nc.tensor.matmul(b[0:R, 36 * c:36 * (c + 1)], tT[:, k, P * c:P * c + R], wr[:, k],
                                           start=(k == 0), stop=(k == KT - 1))
            end(ins, "lg")
            b = take("rk")
            pe.wait_ge(s["rt_oh"], 1)
            oh = rt[:, 4, :, 0:NG]
            for c in range(NC):
                R = ROWS[c]
                for c2 in range(c):
                    nc.tensor.matmul(b[0:R, NG * c:NG * (c + 1)], ones[:, 0:R], oh[:, c2], start=(c2 == 0), stop=False)
                nc.tensor.matmul(b[0:R, NG * c:NG * (c + 1)], before[0:R, 0:R], oh[0:R, c], start=(c == 0), stop=True)
            for c in range(NC):
                ins = nc.tensor.matmul(b[:, 16:16 + NG], ones[0:ROWS[c], :], oh[0:ROWS[c], c], start=(c == 0), stop=(c == NC - 1))
            end(ins, "rk")
            assert at[0] == len(PLAN)

            for i in range(RB):
                last = max(j for j in range(len(PLAN)) if j % RB == i)
                pe.wait_ge(free[i], last // RB + 1)
            npass = load_passes(pe)
            with pe.Fori(0, npass) as rr:
                def gather(grp, half):
                    pe.wait_ge(s["pg"], grp + 1)
                    pe.wait_ge(s["gx_free"], grp * 3 + half + 1)
                    for j in range(4):
                        k = 4 * half + j
                        for c in range(NC):
                            R = ROWS[c]
                            ins = nc.tensor.matmul(psum[5][:, P * j:P * (j + 1)], tn[0:R, c, P * k:P * (k + 1)], pg[0:R, c],
                                                   start=(c == 0), stop=(c == NC - 1))
                    ins.then_inc(s["gx_full"], 1)

                def slots_in(grp, g, skip):
                    pe.wait_ge(s["gx_free"], grp * 3 + 3)
                    for c in range(NC):
                        R = ROWS[c]
                        tr(psum[5][:, P * c:P * c + R], pg[0:R, c], R)
                    for c in range(NC):
                        R = ROWS[c]
                        ins = nc.tensor.matmul(psum[5][:, T:T + NE], pg[0:R, c], comb[0:R, c], start=(c == 0), stop=(c == NC - 1))
                    ins.then_inc(s["gx_full"], 1)

                def group(g, last):
                    grp = rr * NG + g
                    base = grp * GCH
                    pe.wait_ge(s["gx_free"], grp * 3 + 3)
                    for two in range(NE // 2):
                        b2, e2 = base + two * NCH, grp * NE + 2 * two

                        def split_product(bank_, hi_, lo_, wh, wl, start, stop):
                            nc.tensor.matmul(bank_, hi_, wh, start=start, stop=False)
                            nc.tensor.matmul(bank_, hi_, wl, start=False, stop=False)
                            return nc.tensor.matmul(bank_, lo_, wh, start=False, stop=stop)

                        def turn(x):
                            pe.wait_ge(s["hh"], e2 + x + 3)
                            pe.wait_ge(s["hthi"], e2 + x + 1)
                            pe.wait_ge(s["htlo"], e2 + x + 1)
                            for j in range(4):
                                ins = tr(psum[4][:, P * j:P * (j + 1)], hh[x][:, P * j:P * (j + 1)])
                            ins.then_inc(s["t_full"], 1)

                        for pos, (x, part, half) in enumerate(CHUNKS):
                            pe.wait_ge(s["lo"], b2 + pos + 1 + LO0)
                            k_ = 4 if part < 2 else 2
                            wh, wl = (v[pos % PAIR].rearrange("p (k n) -> p k n", k=k_) for v in (whi, wlo))
                            if part < 2:
                                if part == 0 and half == 0:
                                    pe.wait_ge(s["hh"], e2 + x + 1)
                                for k in range(4):
                                    kk = 4 * half + k
                                    ins = split_product(psum[2 * part + x][:, :], xhi[:, kk], xlo[:, kk], wh[:, k], wl[:, k],
                                                        kk == 0, kk == KT - 1)
                            else:
                                if half == 0:
                                    pe.wait_ge(s["htlo"], e2 + x + 2)
                                    if two == 0 and x == 0:
                                        pe.wait_ge(s["sc_free"], grp * 6 + 1)
                                for n_ in range(2):
                                    for j in range(2):
                                        jj = 2 * half + j
                                        ins = split_product(psum[6 + n_][:, :], hthi[x][:, jj], htlo[x][:, jj],
                                                            wh[:, j, BLK * n_:BLK * (n_ + 1)], wl[:, j, BLK * n_:BLK * (n_ + 1)],
                                                            two == 0 and x == 0 and jj == 0,
                                                            two == NE // 2 - 1 and x == 1 and jj == 3)
                                    if n_ == 0 and two == NE // 2 - 1 and pos == NCH - 1:
                                        ins.then_inc(s["y_half"], 1)
                            ins.then_inc(s["chunk_done"], 1)
                            if pos == 5:
                                turn(0)
                            if pos == 8:
                                turn(1)
                            if two == NE // 2 - 1 and pos in (7, 9) and not last:
                                gather(grp + 1, (pos - 7) // 2)
                    for i in range(2):
                        pe.wait_ge(s["y_free"], grp * 2 + i + 1)
                        for c in range(NC):
                            R, k = ROWS[c], 3 * i + c
                            if k == 2:
                                pe.wait_ge(s["y_free"], grp * 2 + 2)
                            if k >= 3:
                                pe.wait_ge(s["sc_free"], grp * 6 + k - 1)
                            elif k == 0 and not last:
                                pe.wait_ge(s["gx_free"], grp * 3 + 6)
                            ins = nc.tensor.matmul(psum[5 + k % 3][0:R, :], pgT[:, P * c:P * c + R],
                                                   ysum[:, BLK * i:BLK * (i + 1)], start=True, stop=True)
                            ins.then_inc(s["sc_full"], 1)
                    if not last:
                        pe.wait_ge(s["sc_free"], grp * 6 + 5)
                        slots_in(grp + 1, g, 1)

                for half in range(2):
                    gather(rr * NG, half)
                slots_in(rr * NG, 0, 0)
                with pe.Fori(0, NG - 1) as g:
                    group(g, False)
                group(NG - 1, True)
                pe.wait_ge(s["sc_free"], rr * (NG * 6) + (NG * 6 + 1))

        @block.vector
        def _(dve):
            n = [0]

            def q(ins):
                n[0] += 1
                ins.then_inc(s["dve"], 1)
                dve.wait_ge(s["dve"], n[0])

            TT, TS, STT = dve.tensor_tensor, dve.tensor_scalar, dve.scalar_tensor_tensor

            def root(use, cols=slice(0, NC)):
                TS(var[:, cols], ss[:, cols], 1.0 / D, EPS, ALU.mult, ALU.add).then_inc(s["var"], 1)
                dve.wait_ge(s["var"], use + 1)
                dve.wait_ge(s["rs0"], use + 1)
                q(dve.reciprocal(rs0[:, cols], rs0[:, cols]))
                q(TT(rs1[:, cols], rs0[:, cols], rs0[:, cols], ALU.mult))
                q(TT(rs1[:, cols], rs1[:, cols], var[:, cols], ALU.mult))
                q(TS(rs1[:, cols], rs1[:, cols], -0.5, 1.5, ALU.mult, ALU.add))
                q(TT(rs[:, cols], rs0[:, cols], rs1[:, cols], ALU.mult))

            dve.wait_ge(s["consts"], 1)
            dve.wait_ge(s["ld_par"], 16 * 13)
            q(dve.tensor_reduce(grp2[:, :], sel16[:, :, :].rearrange("p i a -> p a i"), AX.X, ALU.add))
            dve.memset(cvin[0][:, 0:3], 0.0)
            dve.memset(cvin[1][:, 0:3], 0.0)
            dve.tensor_copy(lamrow[0:NST, 2].rearrange("p (h n) -> p h n", h=2), lsrow[0:NST].unsqueeze(2).to_broadcast([NST, 2, 64]))
            dve.tensor_copy(ddrow[0:KT].rearrange("p (h n) -> p h n", h=2),
                            dd8[0:KT].unsqueeze(2).to_broadcast([KT, 2, 64])).then_inc(s["rows"], 1)
            got(dve, "par")
            dve.tensor_copy(vec[:, :], bank("par")[:, 0:124])
            emptied(dve.tensor_copy(lam[:, :], bank("par")[:, 128:232]), "par")
            done(dve, "par")
            TS(hglu[:, :], vec[:, V_GLU + KT:V_GLU + 2 * KT], 0.5, None, ALU.mult).then_inc(s["s5w"], 1)
            dve.wait_ge(s["ss"], NC)
            root(0)
            def norm_in(i, kind, c):
                R = ROWS[c] if kind == "x" else P
                src = xt[0:R, c] if kind == "x" else memraw[:, c]
                if i >= 2:
                    j = i - 2
                    got(dve, f"x{j}1")
                TS(xn[i % 2][0:R], src, rs[0:R, i:i + 1], None, ALU.mult).then_inc(s["xn"], 1)
                dst, v0 = (hnT, V_MIX) if kind == "x" else (mnT, V_KV)
                for hf in range(2):
                    job = f"{kind}{c}{hf}"
                    got(dve, job)
                    emptied(TT(dst[:, 4 * hf:4 * hf + 4, P * c:P * c + R],
                               bank(job)[:, :].rearrange("p (k l) -> p k l", k=4)[:, :, 0:R],
                               vec[:, v0 + 4 * hf:v0 + 4 * hf + 4].unsqueeze(2).to_broadcast([P, 4, R]), ALU.mult), job)

            for c in range(NC):
                norm_in(c, "x", c)

            (step, xr, xi, mag, k_, t0, red, redc, lbr, lbi, cr, ci, den, t1, t2, t3) = (s5p[:, i] for i in range(16))
            lr, li = lam[:, 0:NST], lam[:, NST:2 * NST]
            dve.wait_ge(s["s5c"], 1)
            q(TT(xi, li, step, ALU.mult))
            TT(xr, lr, step, ALU.mult).then_inc(s["s5w"], 1)
            magic = 12582912.0
            q(TS(k_, xi, 1.0 / TWO_PI, magic, ALU.mult, ALU.add))
            q(TS(k_, k_, magic, None, ALU.subtract))
            q(STT(out=red, in0=k_, scalar=-6.28125, in1=xi, op0=ALU.mult, op1=ALU.add))
            q(STT(out=red, in0=k_, scalar=-(TWO_PI - 6.28125), in1=red, op0=ALU.mult, op1=ALU.add))
            q(TS(red, red, PI, -PI, ALU.min, ALU.max))
            q(TS(redc, red, TWO_PI / 4, None, ALU.add))
            q(TS(t0, redc, PI, -TWO_PI, ALU.is_gt, ALU.mult))
            q(TT(redc, redc, t0, ALU.add))
            TS(redc, redc, PI, -PI, ALU.min, ALU.max).then_inc(s["s5w"], 1)
            dve.wait_ge(s["s5c"], 3)
            er, ei = e[:, 0, 0], e[:, 0, 1]
            q(TT(lbr, mag, er, ALU.mult))
            q(TT(lbi, mag, ei, ALU.mult))
            for k in range(1, 8):
                q(TT(t1, e[:, k - 1, 0], e[:, k - 1, 0], ALU.mult))
                q(TT(t2, e[:, k - 1, 1], e[:, k - 1, 1], ALU.mult))
                q(TT(e[:, k, 0], t1, t2, ALU.subtract))
                if k < 7:
                    q(STT(out=e[:, k, 1], in0=e[:, k - 1, 0], scalar=2.0, in1=e[:, k - 1, 1], op0=ALU.mult, op1=ALU.mult))
                else:
                    STT(out=e[:, k, 1], in0=e[:, k - 1, 0], scalar=2.0, in1=e[:, k - 1, 1], op0=ALU.mult, op1=ALU.mult)\
                        .then_inc(s["s5par"], 1)
            dve.wait_ge(s["s5par"], 1)
            q(TT(t1, lr, lr, ALU.mult))
            q(TT(t2, li, li, ALU.mult))
            q(TT(den, t1, t2, ALU.add))
            q(dve.reciprocal(den, den))
            q(TS(t0, lbr, 1.0, None, ALU.subtract))
            q(TT(t1, t0, lr, ALU.mult))
            q(TT(t2, lbi, li, ALU.mult))
            q(TT(t1, t1, t2, ALU.add))
            q(TT(cr, t1, den, ALU.mult))
            q(TT(t1, lbi, lr, ALU.mult))
            q(TT(t2, t0, li, ALU.mult))
            q(TT(t1, t1, t2, ALU.subtract))
            q(TT(ci, t1, den, ALU.mult))
            dve.wait_ge(s["ld_s5"], 16 * 7)
            dve.wait_ge(s["ss"], 5)
            crb, cib = (v.unsqueeze(2).to_broadcast([P, NST, S5K]) for v in (cr, ci))
            tm = view(tmp512, (NST, S5K))
            tm2 = view(junk[:, 0:512], (NST, S5K))
            for ri in range(2):
                q(TT(tm, bnat[:, ri], crb, ALU.mult))
                q(TT(tm2, bnat[:, 1 - ri], cib, ALU.mult))
                q(TT(tm, tm, tm2, ALU.subtract if ri == 0 else ALU.add))
                for h_ in range(2):
                    ins = TS(bx[:, ri, :, h_], tm, half2[:, h_:h_ + 1], None, ALU.mult)
                    if ri == 1 and h_ == 1:
                        ins.then_inc(s["bx"], 1)
                    else:
                        q(ins)
            for ri in range(2):
                for h_ in range(2):
                    ins = TS(cx[:, ri, :, h_], cnat[:, ri], grp2[:, h_:h_ + 1], 1.0 if ri == 0 else -1.0, ALU.mult, ALU.mult)
            ins.then_inc(s["cx"], 1)
            done(dve, "s5h")
            lb = [v.unsqueeze(1).to_broadcast([P, NB, NST]) for v in (lbr, lbi)]
            tj = view(tmp512[:, 0:256], (NB, NST))
            for ri in range(2):
                q(TT(inj[:, ri], h0s[:, ri], lb[0], ALU.mult))
                q(TT(tj, h0s[:, 1 - ri], lb[1], ALU.mult))
                ins = TT(inj[:, ri], inj[:, ri], tj, ALU.subtract if ri == 0 else ALU.add)
                if ri == 0:
                    q(ins)
            ins.then_inc(s["inj"], 1)
            dve.wait_ge(s["inj"], 1)
            root(1, slice(NC, NC + 2))
            for c in range(2):
                norm_in(NC + c, "m", c)

            def conv(m):
                job = f"xbc{m}"
                done(dve, job)
                vi, vo = cvin[m % 2], cvout[m % 2]
                if m >= 2:
                    dve.wait_ge(s["xc"], m - 1)
                q(dve.tensor_copy(vi[:, 259:347].rearrange("p (b l) -> p b l", b=NB)[:, :, 0:3],
                                  cst[:, m].rearrange("p (b t) -> p b t", b=NB)))
                q(TS(vo, vi[:, 0:344], vec[:, V_CW + m:V_CW + m + 1], vec[:, V_CB + m:V_CB + m + 1], ALU.mult, ALU.add))
                for k in range(1, 4):
                    q(STT(out=vo, in0=vi[:, k:k + 344], scalar=vec[:, V_CW + CT * k + m:V_CW + CT * k + m + 1], in1=vo,
                          op0=ALU.mult, op1=ALU.add))
                dve.tensor_copy(last3[:, m, 0:3], vi[:, 256:259])
                dve.tensor_copy(last3[:, m, 3:27].rearrange("p (b t) -> p b t", b=NB),
                                vi[:, 259:347].rearrange("p (b l) -> p b l", b=NB)[:, :, 8:11]).then_inc(s["convout"], 1)

            def y5_read(ft):
                dve.wait_ge(s["y5_full"], 4 * ft + 4)
                STT(out=u5T[:, ft], in0=u5T[:, ft], scalar=vec[:, V_D5 + ft:V_D5 + ft + 1], in1=psum[6 + ft % 2][:, 0:T],
                    op0=ALU.mult, op1=ALU.add).then_inc(s["y5_free"], 1)

            def finish_tables(oc):
                dve.wait_ge(s["tab_half"], oc + 1)
                tb, js = tab[oc % 2], slice(4 * oc, 4 * oc + 4)
                for ri in range(2):
                    dve.tensor_copy(tb[:, ri, :, NP:T].rearrange("p j (b l) -> p j b l", b=NB),
                                    tb[:, ri, :, 0:LS].unsqueeze(2).to_broadcast([P, 4, NB, LS]))
                for k in (5, 6, 7):
                    m = 2 ** k
                    new, old = tb[:, :, :, m:2 * m], tb[:, :, :, 0:m]
                    er = e[:, k, 0, js].unsqueeze(1).unsqueeze(3).to_broadcast([P, 2, 4, m])
                    ei = e[:, k, 1, js].unsqueeze(1).unsqueeze(3).to_broadcast([P, 2, 4, m])
                    TT(new, old, er, ALU.mult)
                    q(TT(tabtmp2[:, :, :, 0:m], old, ei, ALU.mult))
                    TT(new[:, 0], new[:, 0], tabtmp2[:, 1, :, 0:m], ALU.subtract)
                    ins = TT(new[:, 1], new[:, 1], tabtmp2[:, 0, :, 0:m], ALU.add)
                    if k < 7:
                        q(ins)
                ins.then_inc(s["tab_ready"], 1)
                dve.wait_ge(s["tab_ready"], oc + 1)

            for i in range(4):
                got(dve, f"bt{i}")
            finish_tables(0)
            for st in range(NST):
                tb, j = tab[st // 4 % 2], st % 4
                cs_ = tb[:, 0:1, j].to_broadcast([P, 2, T])
                sn_ = tb[:, 1:2, j].to_broadcast([P, 2, T])
                done(dve, f"bu{st}i")
                done(dve, f"bu{st}r")
                if st:
                    dve.wait_ge(s["scan"], 2 * st)
                TT(m1, ub[st % 2], cs_, ALU.mult)
                q(TT(m2, ub[st % 2], sn_, ALU.mult))
                TT(m1[:, 0], m1[:, 0], m2[:, 1], ALU.add).then_inc(s["tab_used"], 1)
                q(TT(m1[:, 1], m1[:, 1], m2[:, 0], ALU.subtract))
                first = m1[:, :, NP:T].rearrange("p r (b l) -> p r b l", b=NB)[:, :, :, 0]
                q(TT(first, first, inj[:, :, :, st], ALU.add))
                if st >= 2:
                    dve.wait_ge(s["s5rot"], st - 1)
                for ri in range(2):
                    ins = dve.tensor_tensor_scan(wb[st % 2][:, ri], rm[st % 2], m1[:, ri], 0.0, ALU.mult, ALU.add)
                    ins.then_inc(s["scan"], 1)
                if 1 <= st <= CT:
                    conv(st - 1)
                if st % 4 == 3 and st < NST - 1:
                    dve.wait_ge(s["scan"], 2 * st + 2)
                    finish_tables(st // 4 + 1)
                if st % 4 == 2 and st > 4:
                    y5_read(st // 4 - 1)
                if st == 27:
                    got(dve, "dt3")
                    dve.wait_ge(s["ld_small"], 16 * 7)
                    TT(dtx[:, 0:2], bank("dt3")[:, 0:32].rearrange("p (c n) -> p c n", c=2),
                       dtb[:, :].unsqueeze(1).to_broadcast([P, 2, HEADS]), ALU.add)
                    emptied(TT(dtx[0:NS, 2], bank("dt3")[0:NS, 32:48], dtb[0:NS, :], ALU.add), "dt3")
                    done(dve, "dt3")
                    q(TS(dtm, dtx, -1.0, None, ALU.mult))
                    TT(dte, dtx, dtm, ALU.min).then_inc(s["dtx"], 1)
                if st == 28:
                    dve.wait_ge(s["dtx"], 1)
                    q(TS(dtm, dtx, 0.0, None, ALU.max))
                    dve.wait_ge(s["sp_e"], 2)
                    q(TT(dt_, dtm, dtl, ALU.add))
                    STT(out=dtA, in0=dt_, scalar=-1.0, in1=anegb.unsqueeze(1).to_broadcast([P, NC, HEADS]),
                        op0=ALU.mult, op1=ALU.mult).then_inc(s["dt_ready"], 1)
                if st == 29:
                    got(dve, "cs")
                    for dst, c0 in ((csk, 0), (tot, 48)):
                        dve.tensor_copy(dst[:, 0:2], bank("cs")[:, c0:c0 + 32].rearrange("p (c n) -> p c n", c=2))
                        ins = dve.tensor_copy(dst[0:NS, 2], bank("cs")[0:NS, c0 + 32:c0 + 48])
                    emptied(ins, "cs")
                    done(dve, "cs")
                    TT(dtl, tot, csk, ALU.subtract).then_inc(s["cs_in"], 1)
            y5_read(KT - 1)

            dve.wait_ge(s["wdec"], 1)
            q(TT(wend, wend, dt_, ALU.mult))
            dve.wait_ge(s["s5rot"], NST)
            dve.wait_ge(s["sl"], NST)
            for c in range(NC):
                R = ROWS[c]
                for i in range(2):
                    job = f"tr{c}{i}"
                    got(dve, job)
                    src = bank(job)[0:R, :].rearrange("p (n d) -> p n d", n=8)
                    cols, hs = slice(512 * i, 512 * i + 512), slice(8 * i, 8 * i + 8)
                    TT(xdt[0:R, c, cols].rearrange("p (n d) -> p n d", n=8), src,
                       dt_[0:R, c, hs].unsqueeze(2).to_broadcast([R, 8, HD]), ALU.mult)
                    emptied(TT(wx[0:R, c, cols].rearrange("p (n d) -> p n d", n=8), src,
                               wend[0:R, c, hs].unsqueeze(2).to_broadcast([R, 8, HD]), ALU.mult), job)
            done(dve, "tb2")
            for g in range(2):
                ins = TT(bblk[0:NS, g], btok[0:NS, 2, g].unsqueeze(1).to_broadcast([NS, NB, P]),
                         same_s[:, :, 0:1].to_broadcast([NS, NB, P]), ALU.mult)
            ins.then_inc(s["bblk"], 1)
            done(dve, "cb2")
            done(dve, "ecp1")
            done(dve, "s01")
            dve.wait_ge(s["out_k"], 16)
            dve.wait_ge(s["out_s5"], 96)
            dve.wait_ge(s["etot"], 1)

            def gaps(i):
                for c in range(NC):
                    R, job, d_ = ROWS[c], f"csb{i}{c}", dm[i % 2][c][0:ROWS[c]]
                    got(dve, job)
                    if i >= 2:
                        got(dve, f"yi{2 * i - 3}")
                    emptied(TT(d_, bank(job)[0:R, :].rearrange("p (n l) -> p n l", n=4)[:, :, 0:R],
                               csk[0:R, c, 4 * i:4 * i + 4].unsqueeze(2).to_broadcast([R, 4, R]), ALU.subtract), job)
                    done(dve, job)
                    mask = neg[:, :] if c < 2 else neg_s[:, :, :].rearrange("p b l -> p (b l)")
                    TT(d_, d_, mask.unsqueeze(1).to_broadcast([R, 4, R]), ALU.add).then_inc(s["csd"], 1)

            gaps(0)
            for i in range(4):
                g = i // 2
                for c in range(NC):
                    R, d_ = ROWS[c], dm[i % 2][c][0:ROWS[c]]
                    dve.wait_ge(s["csm"], 3 * i + c + 1)
                    TT(d_, d_, cbT[0:R, c, g, 0:R].unsqueeze(1).to_broadcast([R, 4, R]), ALU.mult).then_inc(s["mt"], 1)
                if i < 3:
                    gaps(i + 1)
                for t in (2 * i, 2 * i + 1):
                    hb = hbuf[t % 4]
                    got(dve, f"h0{t}b")
                    q(TT(hb, hb, ecs[:, t, P:192].rearrange("p (b l) -> p b l", b=NB)[:, :, LS - 1:LS].to_broadcast([P, NB, P]),
                         ALU.mult))
                    got(dve, f"yi{t}")
                    emptied(STT(out=y[:, t], in0=xcT[:, t], scalar=lam[:, 96 + t:97 + t], in1=bank(f"yi{t}")[:, 0:T],
                                op0=ALU.mult, op1=ALU.add), f"yi{t}")
                    got(dve, f"yx{t}")
                    emptied(TT(ytmp, ecs[:, t], bank(f"yx{t}")[:, 0:192], ALU.mult), f"yx{t}")
                    done(dve, f"yx{t}")
                    q(TT(y[:, t, P:T], y[:, t, P:T], ytmp, ALU.add))
                    for hf, k in (("a", 0), ("b", 4)):
                        job = f"ns{t}{hf}"
                        got(dve, job)
                        emptied(TT(hb[:, k:k + 4], hb[:, k:k + 4], bank(job)[:, :].rearrange("p (b n) -> p b n", b=4),
                                   ALU.add), job)
            dve.wait_ge(s["out_st0"], 32)
            for g in range(2):
                cols = slice(512 * g, 512 * g + 512)
                q(TT(hl[:, cols].rearrange("p (n d) -> p n d", n=8), s0T[:, cols].rearrange("p (n d) -> p n d", n=8),
                     etot[:, 1, 8 * g:8 * g + 8].unsqueeze(2).to_broadcast([P, 8, HD]), ALU.mult))
                got(dve, f"s1{g}")
                emptied(TT(hl[:, cols], hl[:, cols], bank(f"s1{g}")[:, :], ALU.add), f"s1{g}")
            def split_unit(u):
                if u < UNITS:
                    dve.wait_ge(s["whi"], u + 1)
                    TT(ulo[u % 2], unit_raw(u), uhi[u % 2].bitcast(F32), ALU.subtract).then_inc(s["wlo"], 1)

            def low(part, high, whole, v, count):
                dve.wait_ge(s[part + "_hi"], count)
                TT(v(high[1]), v(whole), v(high[0]).bitcast(F32), ALU.subtract).then_inc(s[part + "_lo"], 1)

            split_unit(0)
            for k in range(KT):
                low("hn", (hn_hi, hn_lo), hnT, lambda x: x[:, k], k + 1)
            dve.wait_ge(s["zs"], 1)
            for m in range(KT):
                if m == 4:
                    split_unit(1)
                if m == 6:
                    split_unit(2)
                if m >= 4:
                    done(dve, f"z{m}")
                TT(y[:, m], y[:, m], zT[:, m], ALU.mult).then_inc(s["y_done"], 1)
            split_unit(3)
            split_unit(4)
            got(dve, "ssy")
            emptied(TS(yv, bank("ssy")[:, 0:T], 1.0 / D, EPS, ALU.mult, ALU.add), "ssy")
            dve.wait_ge(s["yr"], 1)
            q(dve.reciprocal(yr0, yr0))
            q(TT(yr1, yr0, yr0, ALU.mult))
            q(TT(yr1, yr1, yv, ALU.mult))
            q(TS(yr1, yr1, -0.5, 1.5, ALU.mult, ALU.add))
            q(TT(rb, yr0, yr1, ALU.mult))
            for m in range(KT):
                STT(out=y[:, m], in0=y[:, m], scalar=vec[:, V_SSD + m:V_SSD + m + 1], in1=rb, op0=ALU.mult, op1=ALU.mult)\
                    .then_inc(s["yn"], 1)
            split_unit(5)
            for m in range(KT):
                low("yb", (yb_hi, yb_lo), y, lambda x: x[:, m], m + 1)
            split_unit(6)
            for m in range(KT):
                if m % 2 == 0:
                    split_unit(unit_of("sb0") + m // 2 + 1)
                got(dve, f"sb{m}")
                done(dve, f"ga{m}")
                emptied(STT(out=mrg[:, m], in0=mrg[:, m], scalar=1.0, in1=bank(f"sb{m}")[:, 0:T], op0=ALU.add, op1=ALU.mult),
                        f"sb{m}")
            done(dve, "sb7")
            split_unit(unit_of("gb0", 1))
            split_unit(unit_of("gb1", 0))
            low("u5", (u5_hi, u5_lo), u5T, lambda x: x, 1)
            split_unit(unit_of("gb1", 1))
            split_unit(unit_of("gv0", 0))
            for m in range(KT):
                if m % 4 == 0:
                    for i in range(2):
                        split_unit(unit_of(f"gv{m // 4}") + i + 1)
                if m % 2 == 0:
                    split_unit(unit_of(f"gg{m // 4}") + m % 4 // 2 + 1)
                v = val[:, m % 4]
                done(dve, f"gg{m}")
                q(STT(out=v, in0=th[m % 2], scalar=1.0, in1=v, op0=ALU.add, op1=ALU.mult))
                q(STT(out=v, in0=thB[:, m], scalar=1.0, in1=v, op0=ALU.add, op1=ALU.mult))
                STT(out=mrg[:, m], in0=v, scalar=0.5, in1=mrg[:, m], op0=ALU.mult, op1=ALU.add).then_inc(s["glu_used"], 1)
                if m:
                    low("mrg", (mrg_hi, mrg_lo), mrg, lambda x: x[:, m - 1], m)
            low("mrg", (mrg_hi, mrg_lo), mrg, lambda x: x[:, KT - 1], KT)
            dve.wait_ge(s["ld_h"], 32)
            for i in range(4):
                split_unit(unit_of("mx0") + i + 1)
                for c in range(NC):
                    R, job = ROWS[c], f"mx{i}{c}"
                    got(dve, job)
                    v = h[0:R, c, 256 * i:256 * (i + 1)]
                    emptied(STT(out=v, in0=bank(job)[0:R, 0:256], scalar=0.5, in1=v, op0=ALU.mult, op1=ALU.add), job)

            def norm(kind, use, gain, dst):
                dve.wait_ge(s["ss"], 5 + 3 * use)
                root(use + 1)

                def scale(c):
                    R = ROWS[c]
                    if kind == "hq" and c == 2:
                        got(dve, "hq01")
                    TS((hn2[c % 2] if kind == "hq" else tn[:, c])[0:R], h[0:R, c], rs[0:R, c:c + 1], None, ALU.mult).then_inc(
                        s["hn2"], 1)

                scale(0)
                scale(1)
                for c in range(NC):
                    R = ROWS[c]
                    for hf in range(2):
                        job = f"{kind}{c}{hf}"
                        got(dve, job)
                        emptied(TT(dst[:, 4 * hf:4 * hf + 4, P * c:P * c + R],
                                   bank(job)[:, :].rearrange("p (k l) -> p k l", k=4)[:, :, 0:R],
                                   vec[:, gain + 4 * hf:gain + 4 * hf + 4].unsqueeze(2).to_broadcast([P, 4, R]), ALU.mult), job)
                    if c == 0:
                        scale(2)

            norm("hq", 1, V_Q, hn2T)
            for c in range(NC):
                for hf in range(2):
                    low("q", (q_hi, q_lo), hn2T, lambda x: x[:, 4 * hf:4 * hf + 4, P * c:P * c + ROWS[c]], 2 * c + hf + 1)
            for i in range(4):
                split_unit(unit_of("q0") + i + 1)
            split_unit(unit_of("o0", 1))

            def minus_max(k, src):
                q(dve.reduce_max(att[:, k % 2, 3:4], src[:, 0:MEM], AX.X))
                TS(att[:, k % 2, 0:1], att[:, k % 2, 3:4], -1.0, None, ALU.mult).then_inc(s["nmax"], 1)

            def inverse(k):
                dve.wait_ge(s["pexp"], k + 1)
                q(dve.reciprocal(att[:, k % 2, 2:3], att[:, k % 2, 1:2]))
                return att[:, k % 2, 2:3]

            def head_out(k):
                c, hd = divmod(k, MH)
                got(dve, f"ao{c}{hd}")
                emptied(dve.tensor_copy(aoT[:, 2 * hd:2 * hd + 2, P * c:P * (c + 1)],
                                        bank(f"ao{c}{hd}")[:, 0:256].rearrange("p (k l) -> p k l", k=2)), f"ao{c}{hd}")

            dve.memset(psum[6][:, :], 0.0)
            dve.memset(psum[7][:, :], 0.0).then_inc(s["zeroed"], 1)
            got(dve, "sc00")
            minus_max(0, bank("sc00"))
            for k in range(2 * MH):
                c, hd = divmod(k, MH)
                if k < 7:
                    job = "sc%d%d" % divmod(k + 1, MH)
                    got(dve, job)
                    minus_max(k + 1, bank(job))
                inv = inverse(k)
                emptied(TS(pr[k % 2], pr[k % 2], inv, None, ALU.mult), f"sc{c}{hd}")
                if k:
                    head_out(k - 1)
            head_out(7)

            def keys(b):
                for i in range(2):
                    job = f"kt{b}{2 * i + 1}"
                    got(dve, job)
                    if b >= 2 and i == 0:
                        dve.wait_ge(s["sb_full"], b - 1)
                    emptied(dve.tensor_copy(kbT[b % 2][:, 4 * i + 2:4 * i + 4].rearrange("p k m -> p (k m)"),
                                            bank(job)[:, :]), job)

            def sample_out(b):
                got(dve, f"ot{b}")
                emptied(dve.tensor_copy(
                    aoT[:, :, NP + LS * b:NP + LS * (b + 1)].rearrange("p (h k) l -> p k h l", k=2),
                    bank(f"ot{b}")[:, 0:256].rearrange("p (k h l) -> p k h l", k=2, h=MH)[:, :, :, 0:LS]), f"ot{b}")

            keys(0)
            dve.wait_ge(s["sb_full"], 1)
            minus_max(8, psum[6])
            for b in range(NB):
                if b < NB - 1:
                    keys(b + 1)
                if b:
                    sample_out(b - 1)
                inv = inverse(8 + b)
                if b < NB - 1:
                    dve.wait_ge(s["sb_full"], b + 2)
                    minus_max(8 + b + 1, psum[6])
                dve.wait_ge(s["ob_full"], b + 1)
                TS(oS, psum[7][:, 0:MD], inv, None, ALU.mult).then_inc(s["osb"], 1)
                if b == 2:
                    low("ao", (ao_hi, ao_lo), aoT, lambda x: x[:, :, 0:NP], 1)
            sample_out(NB - 1)
            low("ao", (ao_hi, ao_lo), aoT, lambda x: x[:, :, NP:T], 2)
            for i in range(4):
                if i:
                    split_unit(unit_of("o0") + i + 1)
                for c in range(NC):
                    R, job = ROWS[c], f"o{i}{c}"
                    got(dve, job)
                    v = h[0:R, c, 256 * i:256 * (i + 1)]
                    emptied(TT(v, v, bank(job)[0:R, 0:256], ALU.add), job)
            norm("ft", 2, V_FFN, tT)

            q(dve.memset(rtl, 0.0))

            def chunk_lo(pos, n):
                dve.wait_ge(s["hi"], n)
                TT(wlo[pos % PAIR], raw[pos % RAW], whi[pos % PAIR].bitcast(F32), ALU.subtract).then_inc(s["lo"], 1)

            chunk_lo(0, 1)
            chunk_lo(1, 2)
            got(dve, "lg")
            TT(rtl[:, 0:2], bank("lg")[:, 0:72].rearrange("p (c n) -> p c n", c=2),
               rbias[:, :].unsqueeze(1).to_broadcast([P, 2, 36]), ALU.add)
            emptied(TT(rtl[0:NS, 2], bank("lg")[0:NS, 72:108], rbias[0:NS, :], ALU.add), "lg")
            done(dve, "lg")

            def top(i):
                return rt[:, i, :, 0:1]

            def wide(v, k):
                return v.to_broadcast([P, NC, k])

            def first_max(src, k, mx, out):
                q(dve.tensor_reduce(top(mx), src, AX.X, ALU.max))
                q(TT(rt[:, 3, :, 0:k], src, wide(top(mx), k), ALU.is_equal))
                q(STT(out=rt[:, 5, :, 0:k], in0=rt[:, 3, :, 0:k], scalar=-99.0,
                      in1=iota[:, 0:k].unsqueeze(1).to_broadcast([P, NC, k]), op0=ALU.mult, op1=ALU.add))
                q(dve.tensor_reduce(top(6), rt[:, 5, :, 0:k], AX.X, ALU.min))
                return TT(rt[:, out, :, 0:k], rt[:, 5, :, 0:k], wide(top(6), k), ALU.is_equal)

            lgG, lgE = rtl[:, :, 0:NG], rtl[:, :, NG:]
            first_max(lgG, NG, 0, 4).then_inc(s["rt_oh"], 1)
            dve.wait_ge(s["rt_oh"], 1)
            oh = rt[:, 4, :, 0:NG]
            TT(rt[:, 1, :, 0:NG], lgG, wide(top(0), NG), ALU.subtract).then_inc(s["rt_a"], 1)
            q(TT(rte.rearrange("p c (g e) -> p c g e", g=NG), lgE.rearrange("p c (g e) -> p c g e", g=NG),
                 oh.unsqueeze(3).to_broadcast([P, NC, NG, NE]), ALU.mult))
            q(dve.tensor_reduce(rt[:, 8], rte.rearrange("p c (g e) -> p c e g", g=NG), AX.X, ALU.add))
            q(first_max(rt[:, 8], NE, 9, 10))
            q(STT(out=rt[:, 13], in0=rt[:, 10], scalar=-1e30, in1=rt[:, 8], op0=ALU.mult, op1=ALU.add))
            q(first_max(rt[:, 13], NE, 14, 15))
            TT(top(11), top(14), top(9), ALU.subtract).then_inc(s["rt_a"], 1)
            dve.wait_ge(s["rt_e"], 1)
            q(dve.tensor_reduce(top(7), rt[:, 2, :, 0:NG], AX.X, ALU.add))
            q(dve.reciprocal(top(7), top(7)))
            dve.wait_ge(s["rt_e"], 2)
            q(TS(top(16), top(12), 1.0, None, ALU.add))
            q(dve.reciprocal(top(16), top(16)))
            q(TT(top(16), top(16), top(7), ALU.mult))
            q(TT(top(17), top(16), top(12), ALU.mult))
            q(TT(comb[:, :, :], rt[:, 10], wide(top(16), NE), ALU.mult))
            q(TT(rt[:, 18], rt[:, 15], wide(top(17), NE), ALU.mult))
            q(TT(comb[:, :, :], comb[:, :, :], rt[:, 18], ALU.add))
            chunk_lo(2, 3)
            got(dve, "rk")
            STT(out=rg[:, 0:2, :], in0=bank("rk")[:, 0:8].rearrange("p (c g) -> p c g", c=2), scalar=1.0, in1=oh[:, 0:2],
                op0=ALU.add, op1=ALU.mult)
            STT(out=rg[0:NS, 2, :], in0=bank("rk")[0:NS, 8:12], scalar=1.0, in1=oh[0:NS, 2], op0=ALU.add, op1=ALU.mult)
            emptied(dve.reduce_max(rt[:, 19, 0, 0:1], bank("rk")[:, 16:16 + NG], AX.X), "rk")
            done(dve, "rk")
            q(TS(rg[:, :, :], rg[:, :, :], 1.0, None, ALU.subtract))
            q(TS(rt[:, 20, 0, 0:1], rt[:, 19, 0, 0:1], float(P), 1.0, ALU.is_gt, ALU.add))
            q(TS(rt[:, 21, 0, 0:1], rt[:, 19, 0, 0:1], float(2 * P), None, ALU.is_gt))
            TT(np_i[:, :], rt[:, 20, 0, 0:1], rt[:, 21, 0, 0:1], ALU.add).then_inc(s["npass"], 1)

            chunk_lo(3, 4)
            npass = load_passes(dve)
            with dve.Fori(0, npass) as rr:
                def choose(grp, g, skip):
                    for c in range(NC):
                        ins = TS(pg[:, c], iota[:, :], rg[:, c, skip:][:, bass.ds(g, 1)], None, ALU.is_equal)
                    ins.then_inc(s["pg"], 1)

                def tokens_lo(grp, half):
                    dve.wait_ge(s["xhi"], grp * 2 + half + 1)
                    for j in range(4):
                        k = 4 * half + j
                        ins = STT(out=xlo[:, k], in0=psum[5][:, P * j:P * (j + 1)], scalar=vec[:, V_FFN + k:V_FFN + k + 1],
                                  in1=xhi[:, k].bitcast(F32), op0=ALU.mult, op1=ALU.subtract)
                    ins.then_inc(s["gx_free"], 1)

                def group(g, last):
                    grp = rr * NG + g
                    base = grp * GCH
                    for two in range(NE // 2):
                        b2, e2 = base + two * NCH, grp * NE + 2 * two

                        def hidden(x):
                            dve.wait_ge(s["chunk_done"], b2 + (4, 8)[x] + CD0)
                            dve.wait_ge(s["sil"], e2 + x + 1)
                            if two == 0 and x == 0:
                                dve.wait_ge(s["gx_free"], grp * 3 + 4)
                            STT(out=hh[x], in0=sil[x], scalar=cg[:, bass.ds(g * NE + 2 * two + x, 1)], in1=psum[2 + x][:, :],
                                op0=ALU.mult, op1=ALU.mult).then_inc(s["hh"], 1)

                        def ht(x):
                            dve.wait_ge(s["hthi"], e2 + x + 2)
                            TT(htlo[x].rearrange("p j n -> p (j n)"), psum[4][:, :],
                               hthi[x].rearrange("p j n -> p (j n)").bitcast(F32), ALU.subtract).then_inc(s["htlo"], 1)

                        for pos in range(NCH):
                            if pos == 3:
                                hidden(0)
                            if pos == 7:
                                hidden(1)
                            if two < NE // 2 - 1 or pos < NCH - 1:
                                chunk_lo(pos + AHEAD, b2 + pos + AHEAD + 1)
                            if pos == 5:
                                ht(0)
                            if two == NE // 2 - 1 and not last:
                                if pos == 3:
                                    choose(grp + 1, g, 1)
                                if pos in (7, 9):
                                    tokens_lo(grp + 1, (pos - 7) // 2)
                            if pos == 7:
                                ht(1)
                    dve.wait_ge(s["y_half"], grp + 1)
                    dve.tensor_copy(ysum[:, 0:BLK], psum[6][:, :]).then_inc(s["y_free"], 1)
                    dve.wait_ge(s["chunk_done"], base + GCH + CD0)
                    dve.tensor_copy(ysum[:, BLK:D], psum[7][:, :]).then_inc(s["y_free"], 1)
                    for i in range(2):
                        for c in range(NC):
                            R, k = ROWS[c], 3 * i + c
                            dve.wait_ge(s["sc_full"], grp * 6 + k + 1)
                            v = h[0:R, c, BLK * i:BLK * (i + 1)]
                            TT(v, v, psum[5 + k % 3][0:R, :], ALU.add).then_inc(s["sc_free"], 1)
                    chunk_lo(NCH - 1 + AHEAD, base + GCH + AHEAD)

                choose(rr * NG, 0, 0)
                for half in range(2):
                    tokens_lo(rr * NG, half)
                with dve.Fori(0, NG - 1) as g:
                    group(g, False)
                group(NG - 1, True)
                TS(rg[:, :, :], rg[:, :, :], float(P), None, ALU.subtract).then_inc(s["rgdec"], 1)
                dve.wait_ge(s["rgdec"], rr + 1)
            q(TS(rs1[:, 0:1], rs[:, 0:1], 1.0, None, ALU.mult))
            TS(rs1[:, 0:1], rs[:, 0:1], 1.0, None, ALU.mult).then_inc(s["fin"], 1)

            dve.wait_ge(s["ss"], 14)
            root(4)
            dve.wait_ge(s["ld_fin"], 16)
            for c in range(NC):
                R = ROWS[c]
                if c >= 2:
                    dve.wait_ge(s["out_y0"], 16)
                q(TS(fy[c % 2][0:R], h[0:R, c], rs[0:R, c:c + 1], None, ALU.mult))
                TT(fy[c % 2][0:R], fy[c % 2][0:R], gfin[0:R], ALU.mult).then_inc(s["fy"], 1)


_INS = [
    'x_prompt', 'x_sample', 'state_conv', 'state_ssd', 'state_s5_re', 'state_s5_im', 'cache_mem_k', 'cache_mem_v',
    'mem_prompt', 'norm_mix_g', 'w_in', 'conv_w', 'conv_b', 'ssd_dt_bias', 'ssd_a_log', 'ssd_d', 'ssd_norm_g',
    'w_ssd_branch', 's5_lambda_re', 's5_lambda_im', 's5_log_step', 's5_b_re', 's5_b_im', 's5_c_re', 's5_c_im', 's5_d',
    'w_glu', 'b_glu', 'w_mix_out', 'norm_mem_q_g', 'norm_mem_kv_g', 'w_mem_q', 'w_mem_k', 'w_mem_v', 'w_mem_o',
    'norm_ffn_g', 'w_router_group', 'b_router_group', 'w_router_expert', 'b_router_expert', 'w_exp_gate', 'w_exp_up',
    'w_exp_down', 'norm_final_g',
]
_OUTS = [
    ("yp", (1, NP, D)), ("ys", (NB, LS, D)), ("cvp", (1, 1, 3, CD)), ("ssdp", (1, 1, HEADS, HD, STATE)),
    ("rep", (1, 1, S5G, S5N)), ("imp", (1, 1, S5G, S5N)), ("mk", (1, 1, MEM, MH, MD)), ("mv", (1, 1, MEM, MH, MD)),
    ("cvs", (1, NB, 3, CD)), ("ssds", (1, NB, HEADS, HD, STATE)), ("res", (1, NB, S5G, S5N)), ("ims", (1, NB, S5G, S5N)),
]


def kernel(**inputs):
    import numpy as _np
    import concourse.bacc as _bacc
    from concourse import mybir as _mybir
    from concourse.bass_utils import run_bass_kernel_spmd as _run

    nc = _bacc.Bacc("TRN2", target_bir_lowering=False, num_devices=1)
    arrays, a, o = {}, {}, {}
    for name in _INS:
        x = _np.ascontiguousarray(inputs[name])
        arrays[f"in_{name}_dram"] = x
        a[name] = nc.dram_tensor(f"in_{name}_dram", x.shape, _mybir.dt.from_np(x.dtype), kind="ExternalInput").ap()
    for name, shape in _OUTS:
        o[name] = nc.dram_tensor(f"out_{name}_dram", shape, _mybir.dt.float32, kind="ExternalOutput").ap()
    layer(nc, a, o)
    r = _run(nc, [arrays], core_ids=[0])
    return tuple(r.results[0][f"out_{name}_dram"] for name, _ in _OUTS)
```
